# Optimizing a Trainium2 kernel written in Bass

```python
import math
import jax, jax.numpy as jnp
from jax import lax
import numpy as np
import jax
import jax.numpy as jnp

D_MODEL = 1024
BATCH = 1
SEQ = 512
DEPTH = 2

N_META = 16
EPS = 1e-6
A_HEADS = 4
A_WIDTH = D_MODEL
A_HEAD_DIM = A_WIDTH // A_HEADS
A_CHUNK = 64
B_WIDTH = D_MODEL
B_BLOCKS = 8
B_BLOCK_DIM = B_WIDTH // B_BLOCKS
B_CONV = 4
LRU_C = 8.0
C_HEADS = D_MODEL // 128
C_QK_DIM = D_MODEL // (2 * C_HEADS)
C_V_DIM = 2 * C_QK_DIM
ROT_DIM = C_QK_DIM // 4
ROPE_THETA = 500000.0
Q_BLOCK = 128
D_FF = 4 * D_MODEL
N_AB = (DEPTH + 1) // 2
N_C = DEPTH // 2
AB_SPLITS = [A_WIDTH, A_WIDTH, A_WIDTH, A_WIDTH, A_HEADS, A_HEADS, B_WIDTH, B_WIDTH]
AB_IN = sum(AB_SPLITS)
C_SPLITS = [C_HEADS * 2 * C_QK_DIM, C_HEADS * 2 * C_QK_DIM, C_HEADS * C_V_DIM]
C_IN = sum(C_SPLITS)


def _rmsnorm(x, g):
    xf = x.astype(jnp.float32)
    y = xf * lax.rsqrt(jnp.mean(xf * xf, axis=-1, keepdims=True) + EPS)
    return (y * g.astype(jnp.float32)).astype(x.dtype)

def _split(a, sizes):
    return jnp.split(a, np.cumsum(sizes)[:-1].tolist(), axis=-1)

def _mlstm_chunk(state, inp):
    c_mem, n_mem, m_prev = state
    q, k, v, log_i, log_f = inp
    L = q.shape[2]
    b = jnp.cumsum(log_f, axis=-1)
    causal = jnp.tril(jnp.ones((L, L), dtype=bool))
    log_d = b[..., :, None] - b[..., None, :] + log_i[..., None, :]
    log_d = jnp.where(causal, log_d, -jnp.inf)
    log_prev = b + m_prev[..., None]
    m_t = jnp.maximum(log_prev, jnp.max(log_d, axis=-1))
    d = jnp.exp(log_d - m_t[..., None])
    w_prev = jnp.exp(log_prev - m_t)
    s = jnp.einsum('bhtd,bhsd->bhts', q, k) * d
    num = (w_prev[..., None] * jnp.einsum('bhvk,bhtk->bhtv', c_mem, q)
           + jnp.einsum('bhts,bhsv->bhtv', s, v))
    den = w_prev * jnp.einsum('bhk,bhtk->bht', n_mem, q) + jnp.sum(s, axis=-1)
    h = num / jnp.maximum(jnp.abs(den), jnp.exp(-m_t))[..., None]
    log_end = b[..., -1:] - b + log_i
    m_new = jnp.maximum(b[..., -1] + m_prev, jnp.max(log_end, axis=-1))
    w_s = jnp.exp(log_end - m_new[..., None])
    decay = jnp.exp(b[..., -1] + m_prev - m_new)
    c_new = decay[..., None, None] * c_mem + jnp.einsum('bhs,bhsv,bhsk->bhvk', w_s, v, k)
    n_new = decay[..., None] * n_mem + jnp.einsum('bhs,bhsk->bhk', w_s, k)
    return (c_new, n_new, m_new), h

def _mlstm(q, k, v, i_pre, f_pre):
    bsz, t_all, nh, dh = q.shape
    seq = t_all - N_META
    nc = seq // A_CHUNK
    q = q.transpose(0, 2, 1, 3)
    k = k.transpose(0, 2, 1, 3) * (dh ** -0.5)
    v = v.transpose(0, 2, 1, 3)
    log_i = i_pre.transpose(0, 2, 1)
    log_f = jax.nn.log_sigmoid(f_pre).transpose(0, 2, 1)
    state = (jnp.zeros((bsz, nh, dh, dh), jnp.float32),
             jnp.zeros((bsz, nh, dh), jnp.float32),
             jnp.zeros((bsz, nh), jnp.float32))
    state, h_meta = _mlstm_chunk(
        state, (q[:, :, :N_META], k[:, :, :N_META], v[:, :, :N_META],
                log_i[:, :, :N_META], log_f[:, :, :N_META]))

    def chunks(a):
        a = a[:, :, N_META:]
        return jnp.moveaxis(a.reshape(bsz, nh, nc, A_CHUNK, *a.shape[3:]), 2, 0)

    _, h_rest = lax.scan(_mlstm_chunk, state,
                         (chunks(q), chunks(k), chunks(v), chunks(log_i), chunks(log_f)))
    h_rest = jnp.moveaxis(h_rest, 0, 2).reshape(bsz, nh, seq, dh)
    h = jnp.concatenate([h_meta, h_rest], axis=2)
    return h.transpose(0, 2, 1, 3)

def _rg_lru_branch(xb, gate, conv_w, conv_b, w_r, b_r, w_i, b_i, lam):
    bsz, t_all, w = xb.shape
    xc = lax.conv_general_dilated(
        xb.astype(jnp.float32), conv_w.astype(jnp.float32)[:, None, :],
        window_strides=(1,), padding=[(B_CONV - 1, 0)],
        dimension_numbers=('NWC', 'WIO', 'NWC'), feature_group_count=w)
    xc = xc + conv_b.astype(jnp.float32)
    xg = xc.reshape(bsz, t_all, B_BLOCKS, B_BLOCK_DIM)
    r = jax.nn.sigmoid(jnp.einsum('btnd,nde->btne', xg, w_r.astype(jnp.float32)).reshape(bsz, t_all, w)
                       + b_r.astype(jnp.float32))
    i = jax.nn.sigmoid(jnp.einsum('btnd,nde->btne', xg, w_i.astype(jnp.float32)).reshape(bsz, t_all, w)
                       + b_i.astype(jnp.float32))
    log_a = -LRU_C * r * jax.nn.softplus(-lam.astype(jnp.float32))
    a = jnp.exp(log_a)
    u = jnp.sqrt(-jnp.expm1(2.0 * log_a)) * (i * xc)

    def combine(left, right):
        a1, b1 = left
        a2, b2 = right
        return a1 * a2, a2 * b1 + b2

    _, h = lax.associative_scan(combine, (a, u), axis=1)
    return h * jax.nn.gelu(gate.astype(jnp.float32))

def _ab_mixer(hn, w_in, if_bias, mlstm_norm, conv_w, conv_b, w_r, b_r, w_i, b_i, lam, w_out):
    bsz, t_all, _ = hn.shape
    proj = hn @ w_in
    q, k, v, o, gi, gf, xb, gate = _split(proj, AB_SPLITS)
    f32 = jnp.float32
    hs = (bsz, t_all, A_HEADS, A_HEAD_DIM)
    ifb = if_bias.astype(f32)
    h_a = _mlstm(q.astype(f32).reshape(hs), k.astype(f32).reshape(hs), v.astype(f32).reshape(hs),
                 gi.astype(f32) + ifb[:A_HEADS], gf.astype(f32) + ifb[A_HEADS:])
    h_a = jax.nn.sigmoid(o.astype(f32)).reshape(hs) * h_a
    h_a = h_a * lax.rsqrt(jnp.mean(h_a * h_a, axis=-1, keepdims=True) + EPS)
    h_a = (h_a * mlstm_norm.astype(f32).reshape(A_HEADS, A_HEAD_DIM)).reshape(bsz, t_all, A_WIDTH)
    h_b = _rg_lru_branch(xb, gate, conv_w, conv_b, w_r, b_r, w_i, b_i, lam)
    y = jnp.concatenate([h_a, h_b], axis=-1).astype(hn.dtype)
    return y @ w_out

def _partial_rope(x, cos, sin):
    half = ROT_DIM // 2
    x1, x2, rest = x[..., :half], x[..., half:ROT_DIM], x[..., ROT_DIM:]
    c = cos[:, None, None, :]
    s = sin[:, None, None, :]
    return jnp.concatenate([x1 * c - x2 * s, x2 * c + x1 * s, rest], axis=-1)

def _diff_attend(qb, q_pos, kh, vh, k_pos, lam):
    s = jnp.einsum('bhcqd,bhckd->bhcqk', qb, kh)
    mask = k_pos[None, :] <= q_pos[:, None]
    p = jax.nn.softmax(jnp.where(mask, s, -jnp.inf), axis=-1)
    pd = p[:, :, 0] - lam * p[:, :, 1]
    return jnp.einsum('bhqk,bhkv->bhqv', pd, vh)

def _diff_attn(hn, w_in, lam_vecs, subln, w_out, lambda_init):
    bsz, t_all, _ = hn.shape
    seq = t_all - N_META
    f32 = jnp.float32
    q, k, v = _split(hn @ w_in, C_SPLITS)
    q = q.astype(f32).reshape(bsz, t_all, C_HEADS, 2, C_QK_DIM)
    k = k.astype(f32).reshape(bsz, t_all, C_HEADS, 2, C_QK_DIM)
    v = v.astype(f32).reshape(bsz, t_all, C_HEADS, C_V_DIM)
    pos = jnp.arange(t_all, dtype=jnp.int32)
    inv_freq = jnp.power(jnp.float32(ROPE_THETA), -jnp.arange(0, ROT_DIM, 2, dtype=f32) / ROT_DIM)
    ang = pos.astype(f32)[:, None] * inv_freq[None, :]
    cos, sin = jnp.cos(ang), jnp.sin(ang)
    q = _partial_rope(q, cos, sin) * (C_QK_DIM ** -0.5)
    k = _partial_rope(k, cos, sin)
    lv = lam_vecs.astype(f32)
    lam = jnp.exp(jnp.sum(lv[0] * lv[1])) - jnp.exp(jnp.sum(lv[2] * lv[3])) + lambda_init
    qh = q.transpose(0, 2, 3, 1, 4)
    kh = k.transpose(0, 2, 3, 1, 4)
    vh = v.transpose(0, 2, 1, 3)
    o_meta = _diff_attend(qh[:, :, :, :N_META], pos[:N_META], kh[:, :, :, :N_META],
                          vh[:, :, :N_META], pos[:N_META], lam)
    nb = seq // Q_BLOCK
    q_blocks = jnp.moveaxis(qh[:, :, :, N_META:].reshape(bsz, C_HEADS, 2, nb, Q_BLOCK, C_QK_DIM), 3, 0)
    pos_blocks = pos[N_META:].reshape(nb, Q_BLOCK)
    o_rest = lax.map(lambda a: _diff_attend(a[0], a[1], kh, vh, pos, lam), (q_blocks, pos_blocks))
    o_rest = jnp.moveaxis(o_rest, 0, 2).reshape(bsz, C_HEADS, seq, C_V_DIM)
    o = jnp.concatenate([o_meta, o_rest], axis=2)
    o = o * lax.rsqrt(jnp.mean(o * o, axis=-1, keepdims=True) + EPS) * subln.astype(f32)
    o = o * (1.0 - lambda_init)
    o = o.transpose(0, 2, 1, 3).reshape(bsz, t_all, C_HEADS * C_V_DIM).astype(hn.dtype)
    return o @ w_out

def _sq_relu_mlp(hn, w1, w2):
    a = jax.nn.relu(hn @ w1)
    return (a * a) @ w2

def first_inputs(seed: int = 0) -> dict:
    key = jax.random.key(seed)
    ks = jax.random.split(key, 24)
    f32 = jnp.float32

    def nrm(k, shape, scale):
        return jax.random.normal(k, shape, f32) * scale

    x = nrm(ks[0], (BATCH, SEQ, D_MODEL), 1.0)
    meta_tokens = nrm(ks[1], (N_META, D_MODEL), 1.0)
    norm_mix = 1.0 + nrm(ks[2], (DEPTH, D_MODEL), 0.05)
    norm_mlp = 1.0 + nrm(ks[3], (DEPTH, D_MODEL), 0.05)
    norm_final = 1.0 + nrm(ks[4], (D_MODEL,), 0.05)
    ab_w_in = nrm(ks[5], (N_AB, D_MODEL, AB_IN), D_MODEL ** -0.5)
    i_b = -1.0 + nrm(ks[6], (N_AB, A_HEADS), 0.1)
    f_b = jnp.linspace(3.0, 6.0, A_HEADS, dtype=f32)[None, :] + nrm(ks[7], (N_AB, A_HEADS), 0.1)
    ab_if_bias = jnp.concatenate([i_b, f_b], axis=-1)
    mlstm_norm = 1.0 + nrm(ks[8], (N_AB, A_WIDTH), 0.05)
    lru_conv_w = nrm(ks[9], (N_AB, B_CONV, B_WIDTH), B_CONV ** -0.5)
    lru_conv_b = nrm(ks[10], (N_AB, B_WIDTH), 0.01)
    lru_w_r = nrm(ks[11], (N_AB, B_BLOCKS, B_BLOCK_DIM, B_BLOCK_DIM), B_BLOCK_DIM ** -0.5)
    lru_b_r = nrm(ks[12], (N_AB, B_WIDTH), 0.01)
    lru_w_i = nrm(ks[13], (N_AB, B_BLOCKS, B_BLOCK_DIM, B_BLOCK_DIM), B_BLOCK_DIM ** -0.5)
    lru_b_i = nrm(ks[14], (N_AB, B_WIDTH), 0.01)
    u = jax.random.uniform(ks[15], (N_AB, B_WIDTH), f32, 0.9, 0.999)
    p = u ** (1.0 / LRU_C)
    lru_lambda = jnp.log(p) - jnp.log1p(-p)
    ab_w_out = nrm(ks[16], (N_AB, A_WIDTH + B_WIDTH, D_MODEL), (A_WIDTH + B_WIDTH) ** -0.5)
    c_w_in = nrm(ks[17], (N_C, D_MODEL, C_IN), D_MODEL ** -0.5)
    c_lambda = nrm(ks[18], (N_C, 4, C_QK_DIM), 0.1)
    c_subln = 1.0 + nrm(ks[19], (N_C, C_V_DIM), 0.05)
    c_w_out = nrm(ks[20], (N_C, C_HEADS * C_V_DIM, D_MODEL), (C_HEADS * C_V_DIM) ** -0.5)
    mlp_w1 = nrm(ks[21], (DEPTH, D_MODEL, D_FF), D_MODEL ** -0.5)
    mlp_w2 = nrm(ks[22], (DEPTH, D_FF, D_MODEL), D_FF ** -0.5)
    return {"x": x, "meta_tokens": meta_tokens, "norm_mix": norm_mix, "norm_mlp": norm_mlp,
            "norm_final": norm_final, "ab_w_in": ab_w_in, "ab_if_bias": ab_if_bias,
            "mlstm_norm": mlstm_norm, "lru_conv_w": lru_conv_w, "lru_conv_b": lru_conv_b,
            "lru_w_r": lru_w_r, "lru_b_r": lru_b_r, "lru_w_i": lru_w_i, "lru_b_i": lru_b_i,
            "lru_lambda": lru_lambda, "ab_w_out": ab_w_out, "c_w_in": c_w_in,
            "c_lambda": c_lambda, "c_subln": c_subln, "c_w_out": c_w_out,
            "mlp_w1": mlp_w1, "mlp_w2": mlp_w2}

def first_block(x, meta_tokens, norm_mix, norm_mlp, norm_final, ab_w_in, ab_if_bias,
              mlstm_norm, lru_conv_w, lru_conv_b, lru_w_r, lru_b_r, lru_w_i, lru_b_i,
              lru_lambda, ab_w_out, c_w_in, c_lambda, c_subln, c_w_out, mlp_w1, mlp_w2):
    bsz = x.shape[0]
    meta = jnp.broadcast_to(meta_tokens[None].astype(x.dtype), (bsz, N_META, x.shape[-1]))
    h = jnp.concatenate([meta, x], axis=1)
    for layer in range(DEPTH):
        j = layer // 2
        hn = _rmsnorm(h, norm_mix[layer])
        if layer % 2 == 0:
            h = h + _ab_mixer(hn, ab_w_in[j], ab_if_bias[j], mlstm_norm[j], lru_conv_w[j],
                              lru_conv_b[j], lru_w_r[j], lru_b_r[j], lru_w_i[j], lru_b_i[j],
                              lru_lambda[j], ab_w_out[j])
        else:
            lambda_init = 0.8 - 0.6 * math.exp(-0.3 * layer)
            h = h + _diff_attn(hn, c_w_in[j], c_lambda[j], c_subln[j], c_w_out[j], lambda_init)
        h = h + _sq_relu_mlp(_rmsnorm(h, norm_mlp[layer]), mlp_w1[layer], mlp_w2[layer])
    h = _rmsnorm(h, norm_final)
    return h[:, N_META:, :]


HEAD_DIM = 64
N_EVEN = (DEPTH + 1) // 2
N_ODD = DEPTH // 2
NORM_EPS = 1e-6
D_FF_2 = ((8 * D_MODEL // 3 + 255) // 256) * 256

POOL_WINDOWS = (2, 4, 8, 16)
POOL_GROUPS = len(POOL_WINDOWS)
POOL_WIDTH = D_MODEL // 4
POOL_GC = POOL_WIDTH // POOL_GROUPS

ATTN_Q_HEADS = (3 * D_MODEL // 4) // HEAD_DIM
ATTN_KV_HEADS = ATTN_Q_HEADS // 3
GQA_GROUP = ATTN_Q_HEADS // ATTN_KV_HEADS
WINDOW = 128
ATTN_BLOCK = 128
ROPE_THETA_2 = 10000.0
EVEN_IN = POOL_WIDTH + (ATTN_Q_HEADS + 2 * ATTN_KV_HEADS) * HEAD_DIM
EVEN_MIX = POOL_WIDTH + ATTN_Q_HEADS * HEAD_DIM

CONV_CH = D_MODEL // 2
CONV_K = 31

SSM_INNER = D_MODEL
SSM_HEAD_DIM = 64
SSM_HEADS = SSM_INNER // SSM_HEAD_DIM
SSM_GROUPS = 4
SSM_STATE = 128
SSM_CONV = 4
SSM_CHUNK = 128
SSM_XBC = SSM_INNER + 2 * SSM_GROUPS * SSM_STATE
ODD_IN = 2 * CONV_CH + SSM_INNER + SSM_XBC + 2 * SSM_HEADS
ODD_MIX = CONV_CH + SSM_INNER


def rms_norm(x, w):
    xf = x.astype(jnp.float32)
    y = xf * lax.rsqrt(jnp.mean(xf * xf, axis=-1, keepdims=True) + NORM_EPS)
    return (y * w.astype(jnp.float32)).astype(x.dtype)

def layer_norm(x, g, b):
    xf = x.astype(jnp.float32)
    mu = jnp.mean(xf, axis=-1, keepdims=True)
    xc = xf - mu
    y = xc * lax.rsqrt(jnp.mean(xc * xc, axis=-1, keepdims=True) + NORM_EPS)
    return (y * g.astype(jnp.float32) + b.astype(jnp.float32)).astype(x.dtype)

def swiglu(h, w_gate, w_up, w_down):
    return (jax.nn.silu(h @ w_gate) * (h @ w_up)) @ w_down

def depthwise_conv(x, w, b, pad_left, pad_right):
    y = lax.conv_general_dilated(
        x, w[:, None, :].astype(x.dtype), window_strides=(1,),
        padding=[(pad_left, pad_right)],
        dimension_numbers=('NWC', 'WIO', 'NWC'),
        feature_group_count=x.shape[-1])
    return y + b.astype(x.dtype)

def rope_tables(seq_len):
    inv = 1.0 / (ROPE_THETA_2 ** (jnp.arange(0, HEAD_DIM, 2, dtype=jnp.float32) / HEAD_DIM))
    ang = jnp.arange(seq_len, dtype=jnp.float32)[:, None] * inv[None, :]
    return jnp.cos(ang), jnp.sin(ang)

def apply_rope(t, cos, sin):
    tf = t.astype(jnp.float32)
    t1, t2 = tf[..., :HEAD_DIM // 2], tf[..., HEAD_DIM // 2:]
    c, s = cos[None, :, None, :], sin[None, :, None, :]
    return jnp.concatenate([t1 * c - t2 * s, t2 * c + t1 * s], axis=-1).astype(t.dtype)

def multiscale_pool(u, w_grp, scale):
    b, S, C = u.shape
    uf = u.astype(jnp.float32)
    cs = jnp.concatenate([jnp.zeros((b, 1, C), jnp.float32), jnp.cumsum(uf, axis=1)], axis=1)
    t = jnp.arange(S)
    outs = []
    for g, w in enumerate(POOL_WINDOWS):
        lo = jnp.clip(t - w // 2, 0, S)
        hi = jnp.clip(t + w - w // 2, 0, S)
        csg = cs[..., g * POOL_GC:(g + 1) * POOL_GC]
        cnt = (hi - lo).astype(jnp.float32)[None, :, None]
        mean = (jnp.take(csg, hi, axis=1) - jnp.take(csg, lo, axis=1)) / cnt
        outs.append(mean - uf[..., g * POOL_GC:(g + 1) * POOL_GC])
    p = jnp.stack(outs, axis=2).astype(u.dtype)
    y = jnp.einsum('bsgc,gcd->bsgd', p, w_grp).reshape(b, S, C)
    return y * scale

def windowed_gqa(q, k, v, sink):
    b, S = q.shape[0], q.shape[1]
    nb = S // ATTN_BLOCK
    qb = q.reshape(b, nb, ATTN_BLOCK, ATTN_KV_HEADS, GQA_GROUP, HEAD_DIM)

    def band(t):
        tp = jnp.pad(t, ((0, 0), (ATTN_BLOCK, ATTN_BLOCK), (0, 0), (0, 0)))
        tp = tp.reshape(b, nb + 2, ATTN_BLOCK, ATTN_KV_HEADS, HEAD_DIM)
        return jnp.concatenate([tp[:, :-2], tp[:, 1:-1], tp[:, 2:]], axis=2)

    kw, vw = band(k), band(v)
    s = jnp.einsum('bnqhgd,bnkhd->bnhgqk', qb, kw).astype(jnp.float32) * (HEAD_DIM ** -0.5)
    blk = jnp.arange(nb)[:, None, None] * ATTN_BLOCK
    qpos = blk + jnp.arange(ATTN_BLOCK)[None, :, None]
    kpos = blk - ATTN_BLOCK + jnp.arange(3 * ATTN_BLOCK)[None, None, :]
    valid = (jnp.abs(qpos - kpos) <= WINDOW) & (kpos >= 0) & (kpos < S)
    s = jnp.where(valid[None, :, None, None], s, -jnp.inf)
    sk = sink.astype(jnp.float32).reshape(ATTN_KV_HEADS, GQA_GROUP)[None, None, :, :, None, None]
    m = jnp.maximum(jnp.max(s, axis=-1, keepdims=True), sk)
    p = jnp.exp(s - m)
    denom = jnp.sum(p, axis=-1, keepdims=True) + jnp.exp(sk - m)
    o = jnp.einsum('bnhgqk,bnkhd->bnqhgd', (p / denom).astype(v.dtype), vw)
    return o.reshape(b, S, ATTN_Q_HEADS * HEAD_DIM)

def ssd_scan(x, dt, A, Bm, Cm):
    b, L, H, P = x.shape
    G, N = Bm.shape[2], Bm.shape[3]
    Hg = H // G
    c = L // SSM_CHUNK
    X = (x * dt[..., None]).reshape(b, c, SSM_CHUNK, G, Hg, P)
    a = jnp.moveaxis((dt * A).reshape(b, c, SSM_CHUNK, G, Hg), 2, -1)
    a_cs = jnp.cumsum(a, axis=-1)
    Bc = Bm.reshape(b, c, SSM_CHUNK, G, N)
    Cc = Cm.reshape(b, c, SSM_CHUNK, G, N)
    lower = jnp.tril(jnp.ones((SSM_CHUNK, SSM_CHUNK), bool))
    seg = a_cs[..., :, None] - a_cs[..., None, :]
    Lmat = jnp.exp(jnp.where(lower, seg, -jnp.inf))
    CB = jnp.einsum('bclgn,bcsgn->bcgls', Cc, Bc)
    y_diag = jnp.einsum('bcghls,bcsghp->bclghp', CB[:, :, :, None] * Lmat, X)
    decay_s = jnp.exp(a_cs[..., -1:] - a_cs)
    states = jnp.einsum('bclgn,bcghl,bclghp->bcghpn', Bc, decay_s, X)
    chunk_decay = jnp.exp(a_cs[..., -1])

    def step(h, inp):
        st, d = inp
        return h * d[..., None, None] + st, h

    h0 = jnp.zeros((b, G, Hg, P, N), jnp.float32)
    _, prev = lax.scan(step, h0, (jnp.moveaxis(states, 1, 0), jnp.moveaxis(chunk_decay, 1, 0)))
    prev = jnp.moveaxis(prev, 0, 1)
    y_off = jnp.einsum('bclgn,bcghpn,bcghl->bclghp', Cc, prev, jnp.exp(a_cs))
    return (y_diag + y_off).reshape(b, L, H, P)

def even_mixer(h, w_in, pool_w, pool_scale, sink, w_out, cos, sin):
    b, S, _ = h.shape
    proj = h @ w_in
    qw, kw = ATTN_Q_HEADS * HEAD_DIM, ATTN_KV_HEADS * HEAD_DIM
    o = POOL_WIDTH
    u = proj[..., :o]
    q = proj[..., o:o + qw].reshape(b, S, ATTN_Q_HEADS, HEAD_DIM)
    k = proj[..., o + qw:o + qw + kw].reshape(b, S, ATTN_KV_HEADS, HEAD_DIM)
    v = proj[..., o + qw + kw:o + qw + 2 * kw].reshape(b, S, ATTN_KV_HEADS, HEAD_DIM)
    q = apply_rope(q, cos, sin)
    k = apply_rope(k, cos, sin)
    pool_out = multiscale_pool(u, pool_w, pool_scale)
    attn_out = windowed_gqa(q, k, v, sink)
    return jnp.concatenate([pool_out, attn_out], axis=-1) @ w_out

def odd_mixer(h, w_in, dw_w, dw_b, ln_g, ln_b, conv_w, conv_b, A_log, dt_bias, D_skip, norm_w, w_out):
    b, S, _ = h.shape
    proj = h @ w_in
    glu_a = proj[..., :CONV_CH]
    glu_b = proj[..., CONV_CH:2 * CONV_CH]
    o = 2 * CONV_CH
    z = proj[..., o:o + SSM_INNER]
    o += SSM_INNER
    xbc = proj[..., o:o + SSM_XBC]
    o += SSM_XBC
    dt_raw = proj[..., o:o + 2 * SSM_HEADS].reshape(b, S, 2, SSM_HEADS)
    g = glu_a * jax.nn.sigmoid(glu_b)
    g = depthwise_conv(g, dw_w, dw_b, CONV_K // 2, CONV_K // 2)
    g = jax.nn.silu(layer_norm(g, ln_g, ln_b))
    xbc = jax.nn.silu(depthwise_conv(xbc, conv_w, conv_b, SSM_CONV // 2, SSM_CONV - 1 - SSM_CONV // 2))
    gn = SSM_GROUPS * SSM_STATE
    xs = xbc[..., :SSM_INNER].reshape(b, S, SSM_HEADS, SSM_HEAD_DIM).astype(jnp.float32)
    Bm = xbc[..., SSM_INNER:SSM_INNER + gn].reshape(b, S, SSM_GROUPS, SSM_STATE).astype(jnp.float32)
    Cm = xbc[..., SSM_INNER + gn:].reshape(b, S, SSM_GROUPS, SSM_STATE).astype(jnp.float32)
    dt = jax.nn.softplus(dt_raw.astype(jnp.float32) + dt_bias.astype(jnp.float32))
    A = -jnp.exp(A_log.astype(jnp.float32))
    flip = lambda t: jnp.flip(t, axis=1)
    y_f = ssd_scan(xs, dt[:, :, 0], A[0], Bm, Cm)
    y_b = flip(ssd_scan(flip(xs), flip(dt[:, :, 1]), A[1], flip(Bm), flip(Cm)))
    y = (y_f + y_b + xs * D_skip.astype(jnp.float32)[:, None]).reshape(b, S, SSM_INNER)
    y = rms_norm(y * jax.nn.silu(z.astype(jnp.float32)), norm_w).astype(h.dtype)
    return jnp.concatenate([g, y], axis=-1) @ w_out

def second_inputs(seed: int = 0) -> dict:
    key = jax.random.key(seed)
    ks = jax.random.split(key, 24)
    f32 = jnp.float32

    def nrm(k, shape, fan_in):
        return jax.random.normal(k, shape, f32) * (fan_in ** -0.5)

    def near_one(k, shape, s):
        return 1.0 + s * jax.random.normal(k, shape, f32)

    dt0 = jnp.exp(jax.random.uniform(ks[20], (N_ODD, 2, SSM_HEADS), f32,
                                     minval=math.log(1e-3), maxval=math.log(1e-1)))
    return {
        'x': jax.random.normal(ks[0], (BATCH, SEQ, D_MODEL), f32),
        'norm_w': near_one(ks[1], (DEPTH, 6, D_MODEL), 0.05),
        'ffn_w_gate': nrm(ks[2], (DEPTH, 2, D_MODEL, D_FF_2), D_MODEL),
        'ffn_w_up': nrm(ks[3], (DEPTH, 2, D_MODEL, D_FF_2), D_MODEL),
        'ffn_w_down': nrm(ks[4], (DEPTH, 2, D_FF_2, D_MODEL), D_FF_2),
        'ev_w_in': nrm(ks[5], (N_EVEN, D_MODEL, EVEN_IN), D_MODEL),
        'ev_pool_w': nrm(ks[6], (N_EVEN, POOL_GROUPS, POOL_GC, POOL_GC), POOL_GC),
        'ev_pool_scale': near_one(ks[7], (N_EVEN, POOL_WIDTH), 0.1),
        'ev_sink': 0.5 * jax.random.normal(ks[8], (N_EVEN, ATTN_Q_HEADS), f32),
        'ev_w_out': nrm(ks[9], (N_EVEN, EVEN_MIX, D_MODEL), EVEN_MIX),
        'od_w_in': nrm(ks[10], (N_ODD, D_MODEL, ODD_IN), D_MODEL),
        'cv_dw_w': nrm(ks[11], (N_ODD, CONV_K, CONV_CH), CONV_K),
        'cv_dw_b': 0.02 * jax.random.normal(ks[12], (N_ODD, CONV_CH), f32),
        'cv_ln_g': near_one(ks[13], (N_ODD, CONV_CH), 0.05),
        'cv_ln_b': 0.02 * jax.random.normal(ks[14], (N_ODD, CONV_CH), f32),
        'ssm_conv_w': nrm(ks[15], (N_ODD, SSM_CONV, SSM_XBC), SSM_CONV),
        'ssm_conv_b': 0.02 * jax.random.normal(ks[16], (N_ODD, SSM_XBC), f32),
        'ssm_A_log': jnp.log(jax.random.uniform(ks[17], (N_ODD, 2, SSM_HEADS), f32, minval=1.0, maxval=16.0)),
        'ssm_dt_bias': dt0 + jnp.log(-jnp.expm1(-dt0)),
        'ssm_D': near_one(ks[18], (N_ODD, SSM_HEADS), 0.1),
        'ssm_norm_w': near_one(ks[19], (N_ODD, SSM_INNER), 0.05),
        'od_w_out': nrm(ks[21], (N_ODD, ODD_MIX, D_MODEL), ODD_MIX),
    }

def second_block(x, norm_w, ffn_w_gate, ffn_w_up, ffn_w_down,
              ev_w_in, ev_pool_w, ev_pool_scale, ev_sink, ev_w_out,
              od_w_in, cv_dw_w, cv_dw_b, cv_ln_g, cv_ln_b,
              ssm_conv_w, ssm_conv_b, ssm_A_log, ssm_dt_bias, ssm_D, ssm_norm_w, od_w_out):
    cos, sin = rope_tables(x.shape[1])
    for l in range(DEPTH):
        nw = norm_w[l]
        x = x + 0.5 * rms_norm(swiglu(rms_norm(x, nw[0]), ffn_w_gate[l, 0], ffn_w_up[l, 0], ffn_w_down[l, 0]), nw[1])
        hn = rms_norm(x, nw[2])
        i = l // 2
        if l % 2 == 0:
            m = even_mixer(hn, ev_w_in[i], ev_pool_w[i], ev_pool_scale[i], ev_sink[i], ev_w_out[i], cos, sin)
        else:
            m = odd_mixer(hn, od_w_in[i], cv_dw_w[i], cv_dw_b[i], cv_ln_g[i], cv_ln_b[i],
                          ssm_conv_w[i], ssm_conv_b[i], ssm_A_log[i], ssm_dt_bias[i], ssm_D[i],
                          ssm_norm_w[i], od_w_out[i])
        x = x + rms_norm(m, nw[3])
        x = x + 0.5 * rms_norm(swiglu(rms_norm(x, nw[4]), ffn_w_gate[l, 1], ffn_w_up[l, 1], ffn_w_down[l, 1]), nw[5])
    return x


def setup_inputs(seed=0):
    out = dict(first_inputs(seed))
    for name, value in second_inputs(seed + 1).items():
        if name != "x":
            out[name + "_2"] = value
    return out


def reference(
    x, meta_tokens, norm_mix, norm_mlp, norm_final, ab_w_in, ab_if_bias, mlstm_norm, lru_conv_w,
    lru_conv_b, lru_w_r, lru_b_r, lru_w_i, lru_b_i, lru_lambda, ab_w_out, c_w_in, c_lambda,
    c_subln, c_w_out, mlp_w1, mlp_w2, norm_w_2, ffn_w_gate_2, ffn_w_up_2, ffn_w_down_2,
    ev_w_in_2, ev_pool_w_2, ev_pool_scale_2, ev_sink_2, ev_w_out_2, od_w_in_2, cv_dw_w_2,
    cv_dw_b_2, cv_ln_g_2, cv_ln_b_2, ssm_conv_w_2, ssm_conv_b_2, ssm_A_log_2, ssm_dt_bias_2,
    ssm_D_2, ssm_norm_w_2, od_w_out_2,
):
    x = first_block(
        x, meta_tokens, norm_mix, norm_mlp, norm_final, ab_w_in, ab_if_bias, mlstm_norm,
        lru_conv_w, lru_conv_b, lru_w_r, lru_b_r, lru_w_i, lru_b_i, lru_lambda, ab_w_out,
        c_w_in, c_lambda, c_subln, c_w_out, mlp_w1, mlp_w2,
    )
    return second_block(
        x, norm_w_2, ffn_w_gate_2, ffn_w_up_2, ffn_w_down_2, ev_w_in_2, ev_pool_w_2,
        ev_pool_scale_2, ev_sink_2, ev_w_out_2, od_w_in_2, cv_dw_w_2, cv_dw_b_2, cv_ln_g_2,
        cv_ln_b_2, ssm_conv_w_2, ssm_conv_b_2, ssm_A_log_2, ssm_dt_bias_2, ssm_D_2,
        ssm_norm_w_2, od_w_out_2,
    )


_drawn_inputs = setup_inputs


def setup_inputs(seed=0):
    import zlib

    import numpy as np

    out = dict(_drawn_inputs(seed))
    spreads = {}
    factors = {'lru_b_r': 64.0,
     'lru_b_i': 52.262,
     'ev_sink_2': 8.0,
     'cv_dw_b_2': 6.577,
     'cv_ln_g_2': 4.577,
     'cv_ln_b_2': 26.56,
     'ssm_conv_b_2': 3.775,
     'ssm_D_2': 10.31,
     'ssm_norm_w_2': 5.222}
    for name, (base, spread) in spreads.items():
        noise = np.random.default_rng([zlib.crc32(name.encode()), seed]).standard_normal(out[name].shape)
        drawn = base * np.exp(spread * noise) if base else spread * noise
        out[name] = jnp.asarray(drawn.astype(out[name].dtype))
    for name, factor in factors.items():
        out[name] = (out[name] * factor).astype(out[name].dtype)
    return out
```

```python
import math
from contextlib import ExitStack

import numpy as np

import concourse.bass as bass
from concourse import mybir

P = 128
D = 1024
DT = D // P
META = 16
SEQ = 512
T1 = META + SEQ
T2 = SEQ
A_HEADS, A_DIM = 4, 256
CONV1 = 4
LRU_C = 8.0
C_HEADS, C_QK, C_V = 8, 64, 128
ROT1, THETA1 = C_QK // 4, 500000.0
LAMBDA_INIT = 0.8 - 0.6 * math.exp(-0.3)
FF1_PARTS = [8, 8, 8, 8]
FF2 = 2816
FF2_PARTS = [8, 8, 6]
POOL_W = (2, 4, 8, 16)
HD = 64
Q_HEADS, KV_HEADS = 12, 4
GROUP = Q_HEADS // KV_HEADS
THETA2 = 10000.0
CONV_K = 31
SSM_HEADS, SSM_GROUPS = 16, 4
EPS = 1e-6
BIG = 1e30

CHUNKS = {}


def _plan():
    n = 0

    def take(name, count):
        nonlocal n
        CHUNKS[name] = n
        n += count

    for name, count in (("xb", 8), ("gate", 8), ("q", 8), ("k", 8), ("v", 8), ("gi", 1), ("gf", 1),
                        ("o", 8), ("out_a", 8), ("out_b", 8)):
        take(name, count)
    for p, f in enumerate(FF1_PARTS):
        take(f"mlp0_up{p}", f)
        take(f"mlp0_down{p}", 8)
    for name, count in (("cq", 8), ("ck", 8), ("cv", 8), ("c_out", 8)):
        take(name, count)
    for p, f in enumerate(FF1_PARTS):
        take(f"mlp1_up{p}", f)
        take(f"mlp1_down{p}", 8)

    def ffn(i):
        for p, f in enumerate(FF2_PARTS):
            take(f"ffn{i}_up{p}", 2 * f)
            take(f"ffn{i}_down{p}", 8)

    ffn(0)
    for name, count in (("eu", 2), ("eq", 6), ("ek", 2), ("ev", 2), ("e_out", 8)):
        take(name, count)
    ffn(1)
    ffn(2)
    for name, count in (("dt", 1), ("xbc", 16), ("z", 8), ("ga", 4), ("gb", 4), ("o_out_g", 8), ("o_out_y", 8)):
        take(name, count)
    ffn(3)
    CHUNKS["end"] = n


_plan()
N_CHUNKS = CHUNKS["end"]

VEC = {}


def _vecs():
    n = 0
    for name, cols in (("norm_mix", 16), ("norm_mlp", 16), ("norm_final", 8), ("mlstm_norm", 8), ("conv_w", 32),
                       ("conv_b", 8), ("b_r", 8), ("b_i", 8), ("lam", 8), ("subln", 1), ("norm_w_2", 96),
                       ("pool_scale", 2), ("dw_w", 4 * CONV_K), ("dw_b", 4), ("ln_g", 4), ("ln_b", 4),
                       ("sconv_w", 64), ("sconv_b", 16), ("ssm_d", 8), ("ssm_norm", 8), ("i_bias", 1),
                       ("f_bias", 1), ("a_log", 1), ("dt_bias", 1), ("sink", 12), ("c_lambda", 256)):
        VEC[name] = n
        n += cols
    VEC["end"] = n


_vecs()

NORMS = {}


def _norms():
    q = base = 0
    order = [("mix0", 8)] + [(f"mh{h}", 2) for h in range(A_HEADS)] + [("mlp0", 8), ("mix1", 8)]
    order += [(f"ch{h}", 1) for h in range(C_HEADS)] + [("mlp1", 8), ("final", 8)]
    order += [("f0", 8), ("f0p", 8), ("even", 8), ("evenp", 8), ("f1", 8), ("f1p", 8)]
    order += [("f2", 8), ("f2p", 8), ("odd", 8), ("ssm", 8), ("ln", 4), ("oddp", 8), ("f3", 8), ("f3p", 8)]
    for name, size in order:
        NORMS[name] = (q, base, size)
        q += 1
        base += size


_norms()


def build(nc, xT, weights, vecs, mats, lru_w, pool_w, rope1, rope2, pool_inv, out, upto=99):
    f32, f32r = mybir.dt.float32, mybir.dt.float32r
    ALU, ACT, AX = mybir.AluOpType, mybir.ActivationFunctionType, mybir.AxisListType
    tt, stt, ts = nc.vector.tensor_tensor, nc.vector.scalar_tensor_tensor, nc.vector.tensor_scalar
    mm = nc.tensor.matmul

    ctx = ExitStack()
    with ctx:
        def sb(name, shape, dt=f32):
            return ctx.enter_context(nc.sbuf_tensor(name, shape, dt))

        def sem(name):
            return ctx.enter_context(nc.semaphore(name))

        H = sb("resid", [P, DT, T1])
        XH, XL = sb("x_hi", [P, DT, T1], f32r), sb("x_lo", [P, DT, T1], f32r)
        YH, YL = sb("y_hi", [P, DT, T1], f32r), sb("y_lo", [P, DT, T1], f32r)
        RAW = sb("w_raw", [P, 4, DT * P])
        WH, WL = sb("w_hi", [P, 2, DT * P], f32r), sb("w_lo", [P, 2, DT * P], f32r)
        ident = sb("ident", [P, P])
        MATS = sb("mats", [P, 8, P])
        mask_ge, mask_le, rot1, rot2 = (MATS[:, i, :] for i in range(4))
        dup = [MATS[:, 4 + i, :] for i in range(2)]
        rot_dup = [MATS[:, 6 + i, :] for i in range(2)]
        ones = sb("ones", [P, P])
        V = sb("vecs_sb", [P, VEC["end"]])
        PW = sb("pool_w_sb", [P, 2, P])
        ROPE = sb("rope_sb", [P, 2, T1])
        SM = sb("small", [P, 64])
        AR = sb("arena", [P, 35 * T1])

        def area(at, tiles, width=T1):
            return AR[:, at * T1:at * T1 + tiles * width].rearrange("p (f t) -> p f t", t=width)

        G = ctx.enter_context(nc.psum_tensor("psum", [P, 8, 512], f32))
        GF = G[:, :, :].rearrange("p b n -> p (b n)")
        SCR = area(29, 6)

        def vec(name, i=0, rows=P):
            return V[0:rows, VEC[name] + i:VEC[name] + i + 1]

        const_loaded = sem("const_loaded")
        rope_loaded = sem("rope_loaded")
        raw_loaded = [sem(f"raw_loaded{i}") for i in range(4)]
        high_ready, low_ready = sem("high_ready"), sem("low_ready")
        tile_done, psum_free = sem("tile_done"), sem("psum_free")
        squared, summed, var_ready, std_ready = sem("squared"), sem("summed"), sem("var_ready"), sem("std_ready")
        norm_ready = sem("norm_ready")
        h_ready, h_high, h_low = sem("h_ready"), sem("h_high"), sem("h_low")
        silu_done = sem("silu_done")
        ones_ready = sem("ones_ready")
        out_done = sem("out_done")
        st = {k: sem(k) for k in (
            "lru_w", "lru_sp", "lru_xc", "lru_ps", "lru_sg", "lru_ex", "lru_v", "lru_sq", "lru_h", "lru_ge",
            "ml_gate", "ml_abs", "ml_m", "ml_em", "ml_tr", "ml_col", "ml_vt", "ml_vc", "ml_bc", "ml_bcc",
            "ml_s", "ml_dg", "ml_d", "ml_p", "ml_pv", "ml_h", "ml_sig", "ml_og",
            "c_lam", "c_lex", "c_rot", "c_rope", "c_vt", "c_vc", "c_s", "c_mx", "c_e", "c_pd", "c_pt", "c_ptc",
            "c_pv", "c_o",
            "e_pool", "e_pm", "e_rot", "e_rope", "e_vt", "e_vc", "e_s", "e_mx", "e_e", "e_p", "e_pt", "e_ptc",
            "e_pv", "e_o", "inv_loaded",
            "o_dt", "o_ab", "o_a", "o_tr", "o_col", "o_cv", "o_si", "o_xt", "o_xc", "o_cb", "o_bc",
            "o_fe", "o_dg", "o_w", "o_m", "o_y", "o_yd", "o_z", "o_g", "o_gc", "o_mu", "o_xm", "o_sl", "lam_ready")}

        block = ctx.enter_context(nc.Block())

        def is1(n):
            return n < CHUNKS["ffn0_up0"]

        def slots(n):
            return 2 if is1(n) else 4

        def acc(n, c):
            s = (n + c) % slots(n)
            return G[:, 2 * s:2 * s + 2, 0:T1 // 2] if is1(n) else G[:, s:s + 1, 0:T2]

        def toks(ap, n):
            return ap.rearrange("p (a t) -> p a t", a=2 if is1(n) else 1)

        def width(n):
            return T1 if is1(n) else T2

        def fours(eng, count, step, peel=False):
            full = count // 4
            looped = full - 1 if peel else full
            if looped > 1:
                with eng.Fori(0, looped) as i:
                    for c in range(4):
                        step(i, c)
            else:
                looped = 0
            for i in range(looped, full):
                for c in range(4):
                    step(i, c)
            for c in range(count - 4 * full):
                step(full, c)

        def pieces(c0, c1):
            return [(a, b) for a, b in ((c0, min(c1, 512)), (max(c0, 512), c1)) if a < b]

        def load_chunk(sp, n, slot):
            sp.dma_start(RAW[:, slot, :], weights[n]).then_inc(raw_loaded[slot], 16)

        def stream(sp):
            total = N_CHUNKS if upto > 90 else LAST
            for n in range(4):
                load_chunk(sp, n, n)
            full = total // 4
            with sp.Fori(1, full) as i:
                for c in range(4):
                    sp.wait_ge(low_ready, 4 * i + c - 3)
                    load_chunk(sp, 4 * i + c, c)
            for n in range(4 * full, total):
                sp.wait_ge(low_ready, n - 3)
                load_chunk(sp, n, n % 4)

        STAGE_CHUNK_END = {1: "q", 2: "mlp0_up0", 3: "cq", 4: "mlp1_up0", 5: "ffn0_up0", 6: "eu", 7: "ffn1_up0",
                           8: "ffn2_up0", 9: "dt", 10: "ffn3_up0"}
        LAST = CHUNKS[STAGE_CHUNK_END[upto]] + 2 if upto in STAGE_CHUNK_END else N_CHUNKS

        def split_high(act, n, i, c):
            act.wait_ge(raw_loaded[(n + c) % 4], 16 * (i + (n + c) // 4 + 1))
            if n + c >= 2:
                act.wait_ge(tile_done, 4 * i + n + c - 1)
            nc.scalar.activation(WH[:, (n + c) % 2, :], RAW[:, (n + c) % 4, :], ACT.Copy).then_inc(high_ready, 1)

        def pool_stream(pool):
            total = LAST

            def step(i, c):
                pool.wait_ge(high_ready, 4 * i + c + 1)
                nc.gpsimd.tensor_tensor(WL[:, c % 2, :], RAW[:, c, :], WH[:, c % 2, :],
                                        ALU.subtract).then_inc(low_ready, 1)
            fours(pool, total, step)

        def product(pe, n, count, hi, lo, kt=8):
            w = width(n)
            pe.wait_ge(psum_free, n + 4)

            def step(i, c):
                pe.wait_ge(low_ready, 4 * i + n + c + 1)
                pe.wait_ge(psum_free, 4 * i + n + c - slots(n) + 1 + 4)
                o = acc(n, c)
                parts = o.shape[1]
                ws = (n + c) % 2
                last = None
                for k in range(kt):
                    for p, (wt, x) in enumerate(((WH, hi), (WH, lo), (WL, hi))):
                        for a in range(parts):
                            last = mm(o[:, a, :], wt[:, ws, k * P:k * P + P],
                                      x[:, k, a * (w // parts):(a + 1) * (w // parts)],
                                      start=(k == 0 and p == 0), stop=(k == kt - 1 and p == 2))
                last.then_inc(tile_done, 1)
            fours(pe, count, step)

        def act_idle(act, n, count):
            def step(i, c):
                if n + c + 2 + 4 * (i if isinstance(i, int) else 0) < LAST:
                    split_high(act, n + 2, i, c)
            fours(act, count, step, peel=(n + count + 2 > LAST))

        def take(dve, n, count, op):
            dve.drain()

            def step(i, c):
                dve.wait_ge(tile_done, 4 * i + n + c + 1)
                op(acc(n, c), i, c).then_inc(psum_free, 1)
            fours(dve, count, step)

        def take_copy(dve, n, count, dst, offset=0):
            w = width(n)
            take(dve, n, count, lambda ps, i, c: nc.vector.tensor_copy(
                toks(dst[:, 4 * i + c, offset:offset + w], n), ps))

        def take_add(dve, n, count, dst):
            take(dve, n, count, lambda ps, i, c: tt(toks(dst[:, 4 * i + c, :], n), ps,
                                                    toks(dst[:, 4 * i + c, :], n), ALU.add))

        def norm_act(act, name, srcs, w, split=None, hi=None):
            q, base, size = NORMS[name]
            for f, src in enumerate(srcs):
                if base + f >= 2:
                    act.wait_ge(summed, base + f - 1)
                nc.scalar.activation(SCR[:, (base + f) % 2, 0:w], src, ACT.Square).then_inc(squared, 1)
            act.wait_ge(var_ready, q + 1)
            nc.scalar.activation(SCR[:, 5, 0:w], SCR[:, 4, 0:w], ACT.Sqrt).then_inc(std_ready, 1)

        def norm_pe(pe, name, w):
            q, base, size = NORMS[name]
            if q:
                pe.wait_ge(var_ready, q)
            for f in range(size):
                pe.wait_ge(squared, base + f + 1)
                last = None
                for a, b in pieces(0, w):
                    last = mm(GF[:, 2048 + a:2048 + b], ones[:, :], SCR[:, (base + f) % 2, a:b],
                              start=(f == 0), stop=(f == size - 1))
                last.then_inc(summed, 1)

        def norm_dve_stats(dve, name, w, dims):
            q, base, size = NORMS[name]
            dve.wait_ge(summed, base + size)
            dve.drain()
            ts(SCR[:, 4, 0:w], GF[:, 2048:2048 + w], 1.0 / dims, EPS, ALU.mult, ALU.add).then_inc(var_ready, 1)
            dve.wait_ge(std_ready, q + 1)
            nc.vector.reciprocal(SCR[:, 4, 0:w], SCR[:, 5, 0:w])
            dve.drain()

        def split_act(act, name, his, w):
            for f, hi in enumerate(his):
                tmp = SCR[:, 2 + f % 2, 0:w]
                act.wait_ge(h_ready, READY_AT[name] + f + 1)
                nc.scalar.activation(hi, tmp, ACT.Copy).then_inc(h_high, 1)

        def norm_split_dve(dve, srcs, gains, his, los, w, base):
            n = len(srcs)

            def make(f):
                stt(SCR[:, 2 + f % 2, 0:w], srcs[f], gains[f], SCR[:, 4, 0:w], ALU.mult,
                    ALU.mult).then_inc(h_ready, 1)
            make(0)
            if n > 1:
                make(1)
            for f in range(n):
                dve.wait_ge(h_high, base + f + 1)
                if f < 2:
                    dve.drain()
                tt(los[f], SCR[:, 2 + f % 2, 0:w], his[f], ALU.subtract).then_inc(h_low, 1)
                if f + 2 < n:
                    dve.drain()
                    make(f + 2)
            dve.drain()

        SPLIT_AT, READY_AT = {}, {}
        order = [("mix0", 8), ("lru", 8), ("mh0", 2), ("mh1", 2), ("mh2", 2), ("mh3", 2), ("mlp0", 8)]
        order += [(f"mlp0_{p}", f) for p, f in enumerate(FF1_PARTS)] + [("mix1", 8)]
        order += [(f"ch{h}", 1) for h in range(C_HEADS)] + [("mlp1", 8)]
        order += [(f"mlp1_{p}", f) for p, f in enumerate(FF1_PARTS)]

        def ffn_order(i):
            return [(f"f{i}", 8)] + [(f"ffn{i}_{p}", f) for p, f in enumerate(FF2_PARTS)]
        order += ffn_order(0) + [("even", 8), ("e_pool", 2), ("e_attn", 6)] + ffn_order(1) + ffn_order(2)
        order += [("odd", 8), ("ssm", 8), ("o_g", 4)] + ffn_order(3)
        at = ready = 0
        for name, size in order:
            SPLIT_AT[name] = (at, size)
            READY_AT[name] = ready
            at += size
            if not (name.startswith(("mlp0_", "mlp1_", "ffn")) or name in ("e_attn", "o_g")):
                ready += size

        def split_end(name):
            return sum(SPLIT_AT[name])

        def resid(block2):
            return [H[:, f, META:T1] if block2 else H[:, f, :] for f in range(DT)]

        def gains(name, i):
            return [vec(name, 8 * i + f) for f in range(DT)]

        def in_norm_act(act, name, n):
            w = width(n)
            act.wait_ge(psum_free, n + 4)
            if NORMS[name][0] == 0:
                act.wait_ge(const_loaded, CONST_LOADS)
            if name in ("f0", "even", "f1", "f2", "odd", "f3"):
                act.wait_ge(norm_ready, NORM_WRITES[name])
            norm_act(act, name, resid(not is1(n)), w)
            split_act(act, name, [XH[:, f, 0:w] for f in range(DT)], w)

        def in_norm_dve(dve, name, n, g):
            w = width(n)
            norm_dve_stats(dve, name, w, D)
            norm_split_dve(dve, resid(not is1(n)), g, [XH[:, f, 0:w] for f in range(DT)],
                           [XL[:, f, 0:w] for f in range(DT)], w, SPLIT_AT[name][0])

        NORM_WRITES = {"f0": 1, "even": 2, "f1": 3, "f2": 4, "odd": 5, "f3": 6}

        def post_norm_act(act, name, n, srcs):
            act.wait_ge(psum_free, n + 4)
            norm_act(act, name, srcs, T2)

        def post_norm_dve(dve, name, srcs, g, scale):
            norm_dve_stats(dve, name, T2, D)
            r = resid(True)
            last = None
            for f in range(DT):
                stt(SCR[:, 2 + f % 2, 0:T2], srcs[f], g[f], SCR[:, 4, 0:T2], ALU.mult, ALU.mult)
                dve.drain()
                last = stt(r[f], SCR[:, 2 + f % 2, 0:T2], scale, r[f], ALU.mult, ALU.add)
            last.then_inc(norm_ready, 1)
            dve.drain()

        def mlp_pe(pe, l):
            pe.wait_ge(h_low, split_end(f"mlp{l}"))
            for p, f in enumerate(FF1_PARTS):
                product(pe, CHUNKS[f"mlp{l}_up{p}"], f, XH, XL)
                pe.wait_ge(h_low, split_end(f"mlp{l}_{p}"))
                product(pe, CHUNKS[f"mlp{l}_down{p}"], 8, YH, YL, kt=f)

        def mlp_act(act, l):
            in_norm_act(act, f"mlp{l}", CHUNKS[f"mlp{l}_up0"])
            for p, f in enumerate(FF1_PARTS):
                n, s = CHUNKS[f"mlp{l}_up{p}"], SPLIT_AT[f"mlp{l}_{p}"][0]

                def step(i, c):
                    split_high(act, n + 2, i, c)
                    act.wait_ge(psum_free, 4 * i + n + c + 1 + 4)
                    nc.scalar.activation(YH[:, 4 * i + c, :], SCR[:, 2 + c % 2, :], ACT.Square).then_inc(h_high, 1)
                fours(act, f, step)
                act_idle(act, CHUNKS[f"mlp{l}_down{p}"], 8)

        def mlp_dve(dve, l):
            in_norm_dve(dve, f"mlp{l}", CHUNKS[f"mlp{l}_up0"], gains("norm_mlp", l))
            for p, f in enumerate(FF1_PARTS):
                n, s = CHUNKS[f"mlp{l}_up{p}"], SPLIT_AT[f"mlp{l}_{p}"][0]

                def step(i, c):
                    dve.wait_ge(tile_done, 4 * i + n + c + 1)
                    ps = acc(n, c)
                    ts(toks(SCR[:, 2 + c % 2, :], n), ps, 0.0, None, ALU.max).then_inc(psum_free, 1)
                    dve.drain()
                    tt(SCR[:, c % 2, :], SCR[:, 2 + c % 2, :], SCR[:, 2 + c % 2, :], ALU.mult)
                    dve.drain()
                    dve.wait_ge(h_high, 4 * i + s + c + 1)
                    tt(YL[:, 4 * i + c, :], SCR[:, c % 2, :], YH[:, 4 * i + c, :], ALU.subtract).then_inc(h_low, 1)
                fours(dve, f, step)
                take_add(dve, CHUNKS[f"mlp{l}_down{p}"], 8, H)
            dve.drain()

        YF = area(0, 8)

        def ffn_pe(pe, i):
            norm_pe(pe, f"f{i}", T2)
            pe.wait_ge(h_low, split_end(f"f{i}"))
            for p, f in enumerate(FF2_PARTS):
                product(pe, CHUNKS[f"ffn{i}_up{p}"], 2 * f, XH, XL)
                pe.wait_ge(h_low, split_end(f"ffn{i}_{p}"))
                product(pe, CHUNKS[f"ffn{i}_down{p}"], 8, YH, YL, kt=f)
            norm_pe(pe, f"f{i}p", T2)

        def ffn_act(act, i):
            in_norm_act(act, f"f{i}", CHUNKS[f"ffn{i}_up0"])
            for p, f in enumerate(FF2_PARTS):
                n, (s, _) = CHUNKS[f"ffn{i}_up{p}"], SPLIT_AT[f"ffn{i}_{p}"]

                def step(j, c):
                    split_high(act, n + 2, j, c)
                    if c % 2 == 0:
                        act.wait_ge(tile_done, 4 * j + n + c + 1)
                        nc.scalar.activation(SCR[:, 2 + c // 2, 0:T2], acc(n, c)[:, 0, :],
                                             ACT.Silu).then_inc(silu_done, 1)
                    else:
                        act.wait_ge(psum_free, 4 * j + n + c + 1 + 4)
                        nc.scalar.activation(YH[:, 2 * j + c // 2, 0:T2], SCR[:, c // 2, 0:T2],
                                             ACT.Copy).then_inc(h_high, 1)
                fours(act, 2 * f, step)
                act_idle(act, CHUNKS[f"ffn{i}_down{p}"], 8)
            post_norm_act(act, f"f{i}p", CHUNKS[f"ffn{i}_down2"] + 8, [YF[:, f, 0:T2] for f in range(DT)])

        def ffn_dve(dve, i):
            in_norm_dve(dve, f"f{i}", CHUNKS[f"ffn{i}_up0"], gains("norm_w_2", FFN_NORM[i]))
            for p, f in enumerate(FF2_PARTS):
                n, (s, _) = CHUNKS[f"ffn{i}_up{p}"], SPLIT_AT[f"ffn{i}_{p}"]
                u = i * sum(FF2_PARTS) + sum(FF2_PARTS[:p])

                def step(j, c):
                    if c % 2 == 0:
                        return
                    dve.wait_ge(silu_done, 2 * j + u + c // 2 + 1)
                    dve.wait_ge(tile_done, 4 * j + n + c + 1)
                    tt(SCR[:, c // 2, 0:T2], acc(n, c)[:, 0, :], SCR[:, 2 + c // 2, 0:T2],
                       ALU.mult).then_inc(psum_free, 2)
                    dve.drain()
                    dve.wait_ge(h_high, 2 * j + s + c // 2 + 1)
                    tt(YL[:, 2 * j + c // 2, 0:T2], SCR[:, c // 2, 0:T2], YH[:, 2 * j + c // 2, 0:T2],
                       ALU.subtract).then_inc(h_low, 1)
                fours(dve, 2 * f, step)
                if p == 0:
                    take_copy(dve, CHUNKS[f"ffn{i}_down{p}"], 8, YF)
                else:
                    dve.drain()
                    take_add_2(dve, CHUNKS[f"ffn{i}_down{p}"], 8, YF)
            dve.drain()
            post_norm_dve(dve, f"f{i}p", [YF[:, f, 0:T2] for f in range(DT)], gains("norm_w_2", FFN_NORM[i] + 1), 0.5)

        FFN_NORM = [0, 4, 6, 10]

        def take_add_2(dve, n, count, dst, off=0):
            take(dve, n, count, lambda ps, i, c: tt(toks(dst[:, 4 * i + c, off:off + T2], n), ps,
                                                    toks(dst[:, 4 * i + c, off:off + T2], n), ALU.add))

        def log1p(dve, out, e, z, w):
            ts(z, e, 2.0, None, ALU.add)
            dve.drain()
            nc.vector.reciprocal(w, z)
            dve.drain()
            tt(z, e, w, ALU.mult)
            dve.drain()
            tt(w, z, z, ALU.mult)
            dve.drain()
            ts(out, w, 1.0 / 15, None, ALU.mult)
            dve.drain()
            for k in (13, 11, 9, 7, 5, 3):
                stt(out, out, 1.0 / k, w, ALU.add, ALU.mult)
                dve.drain()
            stt(out, out, 1.0, z, ALU.add, ALU.mult)
            dve.drain()
            ts(out, out, 2.0, None, ALU.mult)
            dve.drain()

        XB = AR[:, 0:DT * (T1 + 3)].rearrange("p (f t) -> p f t", t=T1 + 3)
        XC, GATE = area(9, 2), area(11, 8)
        LRU_W = AR[:, 19 * T1:19 * T1 + 16 * P].rearrange("p (f m) -> p f m", m=P)
        RG, IG, AE, TH, UU, VV = (area(23 + i, 1)[:, 0, :] for i in range(6))
        DECAY = SM[:, 0:8]

        def lru_act(act):
            act_idle(act, CHUNKS["xb"], 8)
            act.wait_ge(psum_free, CHUNKS["gate"] + 4)

            def step(i, c):
                split_high(act, CHUNKS["gate"] + 2, i, c)
                act.wait_ge(tile_done, 4 * i + CHUNKS["gate"] + c + 1)
                nc.scalar.activation(toks(GATE[:, 4 * i + c, :], 0), acc(CHUNKS["gate"], c),
                                     ACT.Gelu_apprx_tanh).then_inc(psum_free, 1)
            fours(act, 8, step)
            nc.scalar.activation(SM[:, 8:16], V[:, VEC["lam"]:VEC["lam"] + 8], ACT.Abs)
            act.drain()
            nc.scalar.activation(SM[:, 16:24], SM[:, 8:16], ACT.Exp, scale=-1.0).then_inc(st["lru_sp"], 1)
            for f in range(DT):
                act.wait_ge(st["lru_ps"], f + 1)
                if f:
                    act.wait_ge(st["lru_h"], f)
                else:
                    act.wait_ge(st["lru_sp"], 2)
                nc.scalar.activation(RG, GF[:, 2048:2048 + T1], ACT.Sigmoid, bias=vec("b_r", f))
                nc.scalar.activation(IG, GF[:, 3072:3072 + T1], ACT.Sigmoid,
                                     bias=vec("b_i", f)).then_inc(st["lru_sg"], 1)
                act.drain()
                nc.scalar.activation(AE, RG, ACT.Exp, scale=DECAY[:, f:f + 1])
                nc.scalar.activation(TH, RG, ACT.Tanh, scale=DECAY[:, f:f + 1]).then_inc(st["lru_ex"], 1)
                act.wait_ge(st["lru_v"], f + 1)
                nc.scalar.activation(VV, UU, ACT.Sqrt, scale=-1.0).then_inc(st["lru_sq"], 1)
                act.wait_ge(h_ready, READY_AT["lru"] + f + 1)
                nc.scalar.activation(YH[:, f, :], SCR[:, 2 + f % 2, :], ACT.Copy).then_inc(h_high, 1)

        def lru_pe(pe):
            pe.wait_ge(h_low, split_end("mix0"))
            product(pe, CHUNKS["xb"], 8, XH, XL)
            product(pe, CHUNKS["gate"], 8, XH, XL)
            for f in range(DT):
                pe.wait_ge(st["lru_xc"], f + 1)
                if f:
                    pe.wait_ge(st["lru_sg"], f)
                last = None
                for g in range(2):
                    for a, b in pieces(0, T1):
                        last = mm(GF[:, 2048 + 1024 * g + a:2048 + 1024 * g + b], LRU_W[:, 8 * g + f, :],
                                  XC[:, f % 2, a:b], start=True, stop=True)
                last.then_inc(st["lru_ps"], 1)

        def lru_dve(dve):
            nc.vector.memset(XB[:, :, 0:3], 0.0)
            take_copy(dve, CHUNKS["xb"], 8, XB, offset=3)
            dve.wait_ge(st["lru_sp"], 1)
            dve.drain()
            log1p(dve, SM[:, 8:16], SM[:, 16:24], SM[:, 24:32], SM[:, 32:40])
            ts(SM[:, 24:32], V[:, VEC["lam"]:VEC["lam"] + 8], -1.0, 0.0, ALU.mult, ALU.max)
            dve.drain()
            tt(SM[:, 8:16], SM[:, 8:16], SM[:, 24:32], ALU.add)
            dve.drain()
            ts(DECAY, SM[:, 8:16], -LRU_C, None, ALU.mult).then_inc(st["lru_sp"], 1)

            def conv(f):
                out = XC[:, f % 2, :]
                ts(out, XB[:, f, 0:T1], vec("conv_w", f), vec("conv_b", f), ALU.mult, ALU.add)
                for j in range(1, CONV1):
                    dve.drain()
                    last = stt(out, XB[:, f, j:j + T1], vec("conv_w", 8 * j + f), out, ALU.mult, ALU.add)
                last.then_inc(st["lru_xc"], 1)

            conv(0)
            for f in range(DT):
                dve.wait_ge(st["lru_ex"], f + 1)
                tt(UU, AE, AE, ALU.mult)
                dve.drain()
                stt(UU, UU, 1.0, TH, ALU.add, ALU.mult).then_inc(st["lru_v"], 1)
                tt(IG, IG, XC[:, f % 2, :], ALU.mult)
                if f + 1 < DT:
                    dve.drain()
                    conv(f + 1)
                dve.drain()
                dve.wait_ge(st["lru_sq"], f + 1)
                tt(VV, VV, IG, ALU.mult)
                dve.drain()
                nc.vector.tensor_tensor_scan(UU, AE, VV, 0.0, ALU.mult, ALU.add)
                dve.drain()
                if f == 0:
                    dve.wait_ge(psum_free, CHUNKS["gate"] + 8 + 4)
                tt(SCR[:, 2 + f % 2, :], UU, GATE[:, f, :], ALU.mult).then_inc(h_ready, 1)
                dve.drain()
                dve.wait_ge(h_high, SPLIT_AT["lru"][0] + f + 1)
                tt(YL[:, f, :], SCR[:, 2 + f % 2, :], YH[:, f, :], ALU.subtract).then_inc(h_low, 1)
                dve.drain()
                dve.sem_inc(st["lru_h"], 1)

        def tail(j):
            return min(P, T1 - P * j)

        N_TT = (T1 + P - 1) // P
        QA, KA, VF = area(0, 8), area(8, 8), area(26, 8)
        VT = AR[:, 16 * T1:16 * T1 + N_TT * D].rearrange("p (j m) -> p j m", m=D)

        def vt_pe(pe, done, copied, n_end):
            pe.wait_ge(psum_free, n_end + 4)
            for f in range(DT):
                if f >= 2:
                    pe.wait_ge(copied, f - 1)
                bank = 2048 + 1024 * (f % 2)
                last = None
                for j in range(N_TT):
                    last = nc.tensor.transpose(GF[0:tail(j), bank + P * j:bank + P * j + P],
                                               VF[:, f, P * j:P * j + tail(j)], ident[:, :])
                last.then_inc(done, 1)

        def vt_act(act, done, copied):
            for f in range(DT):
                bank = 2048 + 1024 * (f % 2)
                act.wait_ge(done, f + 1)
                nc.scalar.activation(VT[:, 0:4, P * f:P * f + P],
                                     GF[:, bank:bank + 512].rearrange("p (j m) -> p j m", m=P), ACT.Copy)
                nc.scalar.activation(VT[0:META, 4, P * f:P * f + P], GF[0:META, bank + 512:bank + 640],
                                     ACT.Copy).then_inc(copied, 1)

        GI, GX, RE, RZ, RW, RL, RB, RM_ = (area(26 + i, 1)[0:A_HEADS, 0, :] for i in range(8))
        NMR, EMR = area(34, 1)[0:A_HEADS, 0, :], area(33, 1)[0:A_HEADS, 0, :]
        NMB, EMB, DM, PM0, RC, PM1, RC2 = (area(26 + i, 1)[:, 0, :] for i in range(7))
        ACOL = SM[:, 0:20]

        def mlstm_pe(pe):
            for s in ("q", "k", "v", "gi", "gf"):
                product(pe, CHUNKS[s], 1 if s in ("gi", "gf") else 8, XH, XL)
                if s == "v":
                    vt_pe(pe, st["ml_vt"], st["ml_vc"], CHUNKS["v"] + 8)
            pe.wait_ge(st["ml_m"], 1)
            pe.wait_ge(st["ml_vc"], DT)
            last = None
            for j in range(N_TT):
                last = nc.tensor.transpose(GF[0:tail(j), 2048 + 4 * j:2048 + 4 * j + 4],
                                           GI[:, P * j:P * j + tail(j)], ident[0:A_HEADS, 0:A_HEADS])
            last.then_inc(st["ml_tr"], 1)
            pe.wait_ge(st["ml_em"], 1)
            pe.wait_ge(st["ml_col"], 1)
            for h in range(A_HEADS):
                if h:
                    pe.wait_ge(st["ml_h"], h)
                last = None
                for row, bank in ((NMR, 0), (EMR, 1024)):
                    for a, b in pieces(0, T1):
                        last = mm(GF[:, bank + a:bank + b], ident[0:A_HEADS, h:h + 1].broadcast_to([A_HEADS, P]),
                                  row[:, a:b], start=True, stop=True)
                last.then_inc(st["ml_bc"], 1)
                for j in range(N_TT):
                    s, r = N_TT * h + j, tail(j)
                    if j == 0:
                        pe.wait_ge(st["ml_bcc"], h + 1)
                    else:
                        pe.wait_ge(st["ml_p"], s)
                    for a, b in pieces(P * j, T1):
                        for e in range(2):
                            last = mm(GF[0:r, a:b], KA[:, 2 * h + e, P * j:P * j + r], QA[:, 2 * h + e, a:b],
                                      start=(e == 0), stop=(e == 1))
                    last.then_inc(st["ml_s"], 1)
                    pe.wait_ge(st["ml_p"], s + 1)
                    p = (PM0, PM1)[s % 2]
                    for a, b in pieces(P * j, T1):
                        end = (3 if b <= 512 else 4)
                        for e in range(2):
                            mm(GF[:, 2048 + 1024 * e + a:2048 + 1024 * e + b],
                               VT[0:r, j, (2 * h + e) * P:(2 * h + e + 1) * P], p[0:r, a:b],
                               start=(j == 0), stop=(j == end))
                        last = mm(GF[:, 1024 + a:1024 + b], ones[0:r, :], p[0:r, a:b],
                                  start=(j == 0), stop=(j == end))
                last.then_inc(st["ml_pv"], 1)
            pe.wait_ge(st["ml_h"], A_HEADS)
            product(pe, CHUNKS["o"], 8, XH, XL)
            for h in range(A_HEADS):
                norm_pe(pe, f"mh{h}", T1)
            pe.wait_ge(h_low, split_end("mh3"))
            product(pe, CHUNKS["out_a"], 8, XH, XL)
            product(pe, CHUNKS["out_b"], 8, YH, YL)

        def mlstm_act(act):
            for s in ("q", "k", "v"):
                act_idle(act, CHUNKS[s], 8)
            vt_act(act, st["ml_vt"], st["ml_vc"])
            act_idle(act, CHUNKS["gi"], 1)
            act_idle(act, CHUNKS["gf"], 1)
            act.wait_ge(psum_free, CHUNKS["gf"] + 1 + 4)
            nc.scalar.activation(RE, GX, ACT.Abs)
            act.drain()
            nc.scalar.activation(RE, RE, ACT.Exp, scale=-1.0).then_inc(st["ml_abs"], 1)
            act.wait_ge(st["ml_m"], 1)
            nc.scalar.activation(EMR, RL, ACT.Exp).then_inc(st["ml_em"], 1)
            for h in range(A_HEADS):
                act.wait_ge(st["ml_bc"], h + 1)
                nc.scalar.activation(NMB, GF[:, 0:T1], ACT.Copy)
                nc.scalar.activation(EMB, GF[:, 1024:1024 + T1], ACT.Copy).then_inc(st["ml_bcc"], 1)
                act.drain()
                for j in range(N_TT):
                    s, r, c0 = N_TT * h + j, tail(j), P * j
                    a = ACOL[0:r, 4 * j + h:4 * j + h + 1]
                    act.wait_ge(st["ml_dg"], s + 1)
                    if c0 + r < T1:
                        nc.scalar.activation(DM[0:r, c0 + r:T1], NMB[0:r, c0 + r:T1], ACT.Exp, bias=a)
                    nc.scalar.activation(DM[0:r, c0:c0 + r], DM[0:r, c0:c0 + r], ACT.Exp).then_inc(st["ml_d"], 1)
                act.wait_ge(st["ml_pv"], h + 1)
                nc.scalar.activation(RC, GF[:, 1024:1024 + T1], ACT.Abs).then_inc(st["ml_sig"], 1)

            def step(i, c):
                split_high(act, CHUNKS["o"] + 2, i, c)
                act.wait_ge(tile_done, 4 * i + CHUNKS["o"] + c + 1)
                nc.scalar.activation(toks(KA[:, 4 * i + c, :], 0), acc(CHUNKS["o"], c),
                                     ACT.Sigmoid).then_inc(psum_free, 1)
            fours(act, 8, step)
            act.wait_ge(st["ml_og"], 1)
            for h in range(A_HEADS):
                norm_act(act, f"mh{h}", [QA[:, 2 * h + e, :] for e in range(2)], T1)
                split_act(act, f"mh{h}", [XH[:, 2 * h + e, :] for e in range(2)], T1)
            act_idle(act, CHUNKS["out_a"], 8)
            act_idle(act, CHUNKS["out_b"], 8)

        def mlstm_dve(dve):
            take_copy(dve, CHUNKS["q"], 8, QA)
            take_copy(dve, CHUNKS["k"], 8, KA)
            take_copy(dve, CHUNKS["v"], 8, VF)
            dve.wait_ge(st["ml_vc"], DT)
            for s, row, bias in (("gi", GI, "i_bias"), ("gf", GX, "f_bias")):
                dve.wait_ge(tile_done, CHUNKS[s] + 1)
                ts(toks(row, 0), acc(CHUNKS[s], 0)[0:A_HEADS, :, :], vec(bias, 0, A_HEADS), None,
                   ALU.add).then_inc(psum_free, 1)
            dve.wait_ge(st["ml_abs"], 1)
            dve.drain()
            log1p(dve, RL, RE, RZ, RW)
            stt(RL, GX, 0.0, RL, ALU.min, ALU.subtract)
            dve.drain()
            nc.vector.tensor_tensor_scan(RB, ones[0:A_HEADS, 0:1].broadcast_to([A_HEADS, T1]), RL, 0.0,
                                         ALU.mult, ALU.add)
            dve.drain()
            tt(GI, GI, RB, ALU.subtract)
            dve.drain()
            nc.vector.tensor_tensor_scan(RE, GI, GI, 0.0, ALU.max, ALU.max)
            dve.drain()
            tt(RL, RB, RE, ALU.add)
            ts(NMR, RE, -1.0, None, ALU.mult)
            dve.drain()
            ts(RL, RL, -1.0, 88.0, ALU.mult, ALU.min).then_inc(st["ml_m"], 1)
            dve.wait_ge(st["ml_tr"], 1)
            nc.vector.tensor_copy(ACOL[:, 0:16], GF[:, 2048:2064])
            nc.vector.tensor_copy(ACOL[0:META, 16:20], GF[0:META, 2064:2068]).then_inc(st["ml_col"], 1)
            for h in range(A_HEADS):
                dve.wait_ge(st["ml_bcc"], h + 1)
                for j in range(N_TT):
                    s, r, c0 = N_TT * h + j, tail(j), P * j
                    dve.drain()
                    stt(DM[0:r, c0:c0 + r], NMB[0:r, c0:c0 + r], ACOL[0:r, 4 * j + h:4 * j + h + 1],
                        mask_ge[0:r, 0:r], ALU.add, ALU.add).then_inc(st["ml_dg"], 1)
                    dve.wait_ge(st["ml_d"], s + 1)
                    dve.wait_ge(st["ml_s"], s + 1)
                    stt((PM0, PM1)[s % 2][0:r, c0:T1], GF[0:r, c0:T1], A_DIM ** -0.5, DM[0:r, c0:T1],
                        ALU.mult, ALU.mult).then_inc(st["ml_p"], 1)
                dve.wait_ge(st["ml_sig"], h + 1)
                tt(RC, RC, EMB, ALU.max)
                dve.drain()
                nc.vector.reciprocal(RC2, RC)
                dve.drain()
                for e in range(2):
                    last = tt(QA[:, 2 * h + e, :], GF[:, 2048 + 1024 * e:2048 + 1024 * e + T1], RC2, ALU.mult)
                last.then_inc(st["ml_h"], 1)
            dve.wait_ge(psum_free, CHUNKS["o"] + 8 + 4)
            dve.drain()
            for f in range(DT):
                last = tt(QA[:, f, :], QA[:, f, :], KA[:, f, :], ALU.mult)
            last.then_inc(st["ml_og"], 1)
            for h in range(A_HEADS):
                norm_dve_stats(dve, f"mh{h}", T1, A_DIM)
                norm_split_dve(dve, [QA[:, 2 * h + e, :] for e in range(2)],
                               [vec("mlstm_norm", 2 * h + e) for e in range(2)],
                               [XH[:, 2 * h + e, :] for e in range(2)], [XL[:, 2 * h + e, :] for e in range(2)],
                               T1, SPLIT_AT[f"mh{h}"][0])
            take_add(dve, CHUNKS["out_a"], 8, H)
            take_add(dve, CHUNKS["out_b"], 8, H)
            dve.drain()

        P0, P1 = (area(26 + i, 1)[:, 0, :] for i in range(2))
        PT = AR[:, 28 * T1:28 * T1 + N_TT * P].rearrange("p (j m) -> p j m", m=P)
        ROT_W = [area(26 + i, 1)[:, 0, :] for i in range(2)]
        LAM, GAIN_C, MX, NEGM, SUM, RSUM = (SM[:, a:b] for a, b in ((40, 41), (41, 42), (42, 44), (44, 46),
                                                                   (46, 48), (48, 50)))

        def diff_steps():
            return [(C_HEADS_I, i) for C_HEADS_I in range(C_HEADS) for i in range(N_TT)]

        def diff_pe(pe):
            norm_pe(pe, "mix1", T1)
            pe.wait_ge(h_low, split_end("mix1"))
            for s in ("cq", "ck", "cv"):
                product(pe, CHUNKS[s], 8, XH, XL)
            vt_pe(pe, st["c_vt"], st["c_vc"], CHUNKS["cv"] + 8)
            for f in range(2 * DT):
                if f >= 2:
                    pe.wait_ge(st["c_rope"], f - 1)
                src = (QA, KA)[f // DT]
                last = None
                for a, b in pieces(0, T1):
                    last = mm(GF[:, 1024 * (f % 2) + a:1024 * (f % 2) + b], rot1, src[:, f % DT, a:b],
                              start=True, stop=True)
                last.then_inc(st["c_rot"], 1)
            pe.wait_ge(st["c_rope"], 2 * DT)
            pe.wait_ge(st["c_vc"], DT)
            steps = diff_steps()

            def scores(n):
                h, i = steps[n]
                r, w, t0 = tail(i), min(T1, P * i + P), P * i
                if n:
                    pe.wait_ge(st["c_e"], n)
                last = None
                for c in range(2):
                    rows = slice(C_QK * c, C_QK * c + C_QK)
                    for a, b in pieces(0, w):
                        diag = a <= t0 < b
                        last = mm(GF[0:r, 1024 * c + a:1024 * c + b], QA[rows, h, t0:t0 + r], KA[rows, h, a:b],
                                  start=True, stop=not diag)
                        if diag:
                            last = mm(GF[0:r, 1024 * c + t0:1024 * c + t0 + r], ident[:, 0:r], mask_le[:, 0:r],
                                      start=False, stop=True)
                last.then_inc(st["c_s"], 1)

            scores(0)
            for n, (h, i) in enumerate(steps):
                r, t0 = tail(i), P * i
                if n + 1 < len(steps):
                    scores(n + 1)
                pe.wait_ge(st["c_pd"], n + 1)
                if n:
                    pe.wait_ge(st["c_ptc"], n)
                last = None
                for b in range(i + 1):
                    kb = tail(b)
                    last = nc.tensor.transpose(GF[0:kb, 2048 + P * b:2048 + P * b + r], P0[0:r, P * b:P * b + kb],
                                               ident[0:r, 0:r])
                last.then_inc(st["c_pt"], 1)
                pe.wait_ge(st["c_ptc"], n + 1)
                if i == 0 and h:
                    pe.wait_ge(st["c_o"], h)
                for b in range(i + 1):
                    kb = tail(b)
                    last = mm(GF[:, 3072 + t0:3072 + t0 + r], VT[0:kb, b, P * h:P * h + P], PT[0:kb, b, 0:r],
                              start=(b == 0), stop=(b == i))
                last.then_inc(st["c_pv"], 1)
            for h in range(C_HEADS):
                norm_pe(pe, f"ch{h}", T1)
            pe.wait_ge(h_low, split_end(f"ch{C_HEADS - 1}"))
            product(pe, CHUNKS["c_out"], 8, XH, XL)

        def diff_act(act):
            in_norm_act(act, "mix1", CHUNKS["cq"])
            for s in ("cq", "ck", "cv"):
                act_idle(act, CHUNKS[s], 8)
            vt_act(act, st["c_vt"], st["c_vc"])
            act.wait_ge(st["c_lam"], 1)
            nc.scalar.activation(SM[:, 52:54], SM[:, 50:52], ACT.Exp).then_inc(st["c_lex"], 1)
            for n, (h, i) in enumerate(diff_steps()):
                r, w = tail(i), min(T1, P * i + P)
                act.wait_ge(st["c_mx"], n + 1)
                if n:
                    act.wait_ge(st["c_pt"], n)
                nc.scalar.activation(P0[0:r, 0:w], GF[0:r, 0:w], ACT.Exp, bias=NEGM[0:r, 0:1], scale=C_QK ** -0.5,
                                     accum_out=SUM[0:r, 0:1])
                nc.scalar.activation(P1[0:r, 0:w], GF[0:r, 1024:1024 + w], ACT.Exp, bias=NEGM[0:r, 1:2],
                                     scale=C_QK ** -0.5, accum_out=SUM[0:r, 1:2]).then_inc(st["c_e"], 1)
                act.wait_ge(st["c_pt"], n + 1)
                if n:
                    act.wait_ge(st["c_pv"], n)
                nb = min(i + 1, 4)
                last = nc.scalar.activation(PT[:, 0:nb, 0:r],
                                            GF[:, 2048:2048 + P * nb].rearrange("p (j m) -> p j m", m=P)[:, :, 0:r],
                                            ACT.Copy)
                if i == 4:
                    last = nc.scalar.activation(PT[0:META, 4, 0:r], GF[0:META, 2560:2560 + r], ACT.Copy)
                last.then_inc(st["c_ptc"], 1)
            act.wait_ge(st["c_o"], C_HEADS)
            for h in range(C_HEADS):
                norm_act(act, f"ch{h}", [QA[:, h, :]], T1)
                split_act(act, f"ch{h}", [XH[:, h, :]], T1)
            act_idle(act, CHUNKS["c_out"], 8)

        def diff_dve(dve):
            in_norm_dve(dve, "mix1", CHUNKS["cq"], gains("norm_mix", 1))
            cl = V[:, VEC["c_lambda"]:VEC["c_lambda"] + 256].rearrange("p (a b m) -> p a b m", a=2, b=2)
            lp = SCR[:, 2, 0:128].rearrange("p (a m) -> p a m", a=2)
            tt(lp, cl[:, :, 0, :], cl[:, :, 1, :], ALU.mult)
            dve.drain()
            nc.vector.reduce_sum(SM[:, 50:52], lp, AX.X).then_inc(st["c_lam"], 1)
            for s, dst in (("cq", QA), ("ck", KA), ("cv", VF)):
                take_copy(dve, CHUNKS[s], 8, dst)
            dve.wait_ge(st["c_lex"], 1)
            tt(LAM, SM[:, 53:54], SM[:, 52:53], ALU.subtract)
            dve.drain()
            ts(LAM, LAM, -LAMBDA_INIT, None, ALU.add)
            ts(GAIN_C, vec("subln"), 1.0 - LAMBDA_INIT, None, ALU.mult)
            dve.wait_ge(st["c_vc"], DT)
            for f in range(2 * DT):
                src = (QA, KA)[f // DT][:, f % DT, :]
                tt(ROT_W[0], src, ROPE[:, 0, :], ALU.mult)
                dve.wait_ge(st["c_rot"], f + 1)
                tt(ROT_W[1], GF[:, 1024 * (f % 2):1024 * (f % 2) + T1], ROPE[:, 1, :], ALU.mult)
                dve.drain()
                tt(src, ROT_W[0], ROT_W[1], ALU.add).then_inc(st["c_rope"], 1)
                dve.drain()
            for n, (h, i) in enumerate(diff_steps()):
                r, w = tail(i), min(T1, P * i + P)
                dve.wait_ge(st["c_s"], n + 1)
                for c in range(2):
                    nc.vector.reduce_max(MX[0:r, c:c + 1], GF[0:r, 1024 * c:1024 * c + w], AX.X)
                dve.drain()
                ts(NEGM[0:r, :], MX[0:r, :], -(C_QK ** -0.5), None, ALU.mult).then_inc(st["c_mx"], 1)
                dve.wait_ge(st["c_e"], n + 1)
                nc.vector.reciprocal(RSUM[0:r, :], SUM[0:r, :])
                dve.drain()
                ts(RSUM[0:r, 1:2], RSUM[0:r, 1:2], LAM[0:r, :], None, ALU.mult)
                dve.drain()
                ts(P1[0:r, 0:w], P1[0:r, 0:w], RSUM[0:r, 1:2], None, ALU.mult)
                dve.drain()
                stt(P0[0:r, 0:w], P0[0:r, 0:w], RSUM[0:r, 0:1], P1[0:r, 0:w], ALU.mult,
                    ALU.add).then_inc(st["c_pd"], 1)
                if i == N_TT - 1:
                    dve.wait_ge(st["c_pv"], n + 1)
                    nc.vector.tensor_copy(QA[:, h, :], GF[:, 3072:3072 + T1]).then_inc(st["c_o"], 1)
                dve.drain()
            for h in range(C_HEADS):
                norm_dve_stats(dve, f"ch{h}", T1, C_V)
                norm_split_dve(dve, [QA[:, h, :]], [GAIN_C], [XH[:, h, :]], [XL[:, h, :]], T1,
                               SPLIT_AT[f"ch{h}"][0])
            take_add(dve, CHUNKS["c_out"], 8, H)
            dve.drain()

        def final_act(act):
            act.wait_ge(psum_free, CHUNKS["ffn0_up0"] + 4)
            norm_act(act, "final", resid(True), T2)

        def final_dve(dve):
            norm_dve_stats(dve, "final", T2, D)
            for f, r in enumerate(resid(True)):
                last = stt(r, r, vec("norm_final", f), SCR[:, 4, 0:T2], ALU.mult, ALU.mult)
            last.then_inc(norm_ready, 1)
            dve.drain()

        EU, EQ, EK, EV, KD = area(0, 2), area(2, 6), area(8, 2), area(10, 2), area(12, 4)
        EVT = AR[:, 16 * T1:16 * T1 + 4 * 256].rearrange("p (j m) -> p j m", m=256)
        EW = [area(18 + i, 1)[:, 0, :] for i in range(2)]
        INV = AR[:, 20 * T1:20 * T1 + 2 * T2].rearrange("p (f t) -> p f t", t=T2)
        PP = area(22, 2)
        EPT = AR[:, 24 * T1:24 * T1 + 10 * P].rearrange("p (j m) -> p j m", m=P)
        EPM = AR[:, 27 * T1:27 * T1 + 4 * 384].rearrange("p (j m) -> p j m", m=384)
        EW2 = [area(24 + i, 1)[:, 0, :] for i in range(2)]
        EMX, ENM, ESUM, ESK, ERS = (SM[:, a:a + 4] for a in (0, 4, 8, 12, 16))
        NB = T2 // P

        def band(n):
            return max(0, n - 1), min(NB - 1, n + 1)

        E_BLOCKS = [(n, b) for n in range(NB) for b in range(band(n)[0], band(n)[1] + 1)]

        def even_pe(pe):
            norm_pe(pe, "even", T2)
            pe.wait_ge(h_low, split_end("even"))
            for s, m in (("eu", 2), ("eq", 6), ("ek", 2), ("ev", 2)):
                product(pe, CHUNKS[s], m, XH, XL)
            pe.wait_ge(psum_free, CHUNKS["e_out"] + 4)
            for f in range(2):
                last = None
                for j in range(NB):
                    last = nc.tensor.transpose(G[:, 4 + f, P * j:P * j + P], EV[:, f, P * j:P * j + P], ident[:, :])
                last.then_inc(st["e_vt"], 1)
            for f in range(10):
                if f >= 2:
                    pe.wait_ge(st["e_rope"], f - 1)
                bank = 2 * (f % 2)
                if f < 6:
                    last = mm(G[:, bank + 1, :], rot2, EQ[:, f, 0:T2], start=True, stop=True)
                else:
                    kv = f - 6
                    mm(G[:, bank, :], dup[kv % 2], EK[:, kv // 2, 0:T2], start=True, stop=True)
                    last = mm(G[:, bank + 1, :], rot_dup[kv % 2], EK[:, kv // 2, 0:T2], start=True, stop=True)
                last.then_inc(st["e_rot"], 1)
            pe.wait_ge(st["e_pool"], 1)
            for f in range(2):
                last = mm(G[:, 6 + f, :], PW[:, f, :], PP[:, f, 0:T2], start=True, stop=True)
            last.then_inc(st["e_pm"], 1)
            pe.wait_ge(st["e_rope"], 10)
            pe.wait_ge(st["e_vc"], 2)
            pe.wait_ge(h_low, split_end("e_pool"))

            def scores(h):
                rows = slice(HD * (h % 2), HD * (h % 2) + HD)
                if h:
                    pe.wait_ge(st["e_e"], h)
                last = None
                for n in range(NB):
                    b0, b1 = band(n)
                    w = P * (b1 - b0 + 1)
                    mm(G[:, n, 0:w], EQ[rows, h // 2, P * n:P * n + P], KD[rows, h // GROUP, P * b0:P * b1 + P],
                       start=True, stop=False)
                    if n > 0:
                        last = mm(G[:, n, 0:P], ident[:, :], mask_ge, start=False, stop=(n == NB - 1))
                    if n < NB - 1:
                        last = mm(G[:, n, w - P:w], ident[:, :], mask_le, start=False, stop=True)
                last.then_inc(st["e_s"], 1)

            scores(0)
            for h in range(Q_HEADS):
                if h + 1 < Q_HEADS:
                    scores(h + 1)
                pe.wait_ge(st["e_p"], h + 1)
                if h:
                    pe.wait_ge(st["e_ptc"], h)
                last = None
                for t, (n, b) in enumerate(E_BLOCKS):
                    last = nc.tensor.transpose(GF[:, 2048 + P * t:2048 + P * t + P],
                                               EPM[:, n, P * (b - band(n)[0]):P * (b - band(n)[0]) + P], ident[:, :])
                last.then_inc(st["e_pt"], 1)
                pe.wait_ge(st["e_ptc"], h + 1)
                if h % 2 == 0 and h:
                    pe.wait_ge(h_low, SPLIT_AT["e_attn"][0] + h // 2)
                rows = slice(HD * (h % 2), HD * (h % 2) + HD)
                for t, (n, b) in enumerate(E_BLOCKS):
                    last = mm(G[rows, 7, P * n:P * n + P], EVT[:, b, HD * (h // GROUP):HD * (h // GROUP) + HD],
                              EPT[:, t, :], start=(b == band(n)[0]), stop=(b == band(n)[1]))
                last.then_inc(st["e_pv"], 1)
            pe.wait_ge(h_low, split_end("e_attn"))
            product(pe, CHUNKS["e_out"], 8, YH, YL)
            norm_pe(pe, "evenp", T2)

        def even_act(act):
            in_norm_act(act, "even", CHUNKS["eu"])
            act.dma_start(INV, pool_inv).then_inc(st["inv_loaded"], 16)
            act.dma_start(ROPE[:, :, 0:T2], rope2).then_inc(st["inv_loaded"], 16)
            for s, m in (("eu", 2), ("eq", 6), ("ek", 2), ("ev", 2)):
                act_idle(act, CHUNKS[s], m)
            for f in range(2):
                act.wait_ge(st["e_vt"], f + 1)
                nc.scalar.activation(EVT[:, :, P * f:P * f + P],
                                     G[:, 4 + f, :].rearrange("p (j m) -> p j m", m=P), ACT.Copy).then_inc(st["e_vc"], 1)
            split_act(act, "e_pool", [YH[:, f, 0:T2] for f in range(2)], T2)
            for h in range(Q_HEADS):
                act.wait_ge(st["e_mx"], h + 1)
                if h:
                    act.wait_ge(st["e_pt"], h)
                for n in range(NB):
                    w = P * (band(n)[1] - band(n)[0] + 1)
                    nc.scalar.activation(EPM[:, n, 0:w], G[:, n, 0:w], ACT.Exp, bias=ENM[:, n:n + 1],
                                         scale=HD ** -0.5, accum_out=ESUM[:, n:n + 1])
                nc.scalar.activation(ESK, ENM, ACT.Exp, bias=vec("sink", h)).then_inc(st["e_e"], 1)
                act.wait_ge(st["e_pt"], h + 1)
                if h:
                    act.wait_ge(st["e_pv"], h)
                nc.scalar.activation(EPT[:, :, :], GF[:, 2048:2048 + 10 * P].rearrange("p (j m) -> p j m", m=P),
                                     ACT.Copy).then_inc(st["e_ptc"], 1)
                if h % 2:
                    act.wait_ge(st["e_pv"], h + 1)
                    nc.scalar.activation(YH[:, 2 + h // 2, 0:T2], G[:, 7, :], ACT.Copy).then_inc(h_high, 1)
            act_idle(act, CHUNKS["e_out"], 8)
            post_norm_act(act, "evenp", CHUNKS["e_out"] + 8, [YF[:, f, 0:T2] for f in range(DT)])

        def even_dve(dve):
            in_norm_dve(dve, "even", CHUNKS["eu"], gains("norm_w_2", 2))
            nc.vector.memset(EU[:, :, 0:8], 0.0)
            nc.vector.memset(EU[:, :, 8 + T2:16 + T2], 0.0)
            take_copy(dve, CHUNKS["eu"], 2, EU, offset=8)
            take_copy(dve, CHUNKS["eq"], 6, EQ)
            take_copy(dve, CHUNKS["ek"], 2, EK)
            take_copy(dve, CHUNKS["ev"], 2, EV)
            dve.wait_ge(st["inv_loaded"], 32)
            dve.drain()
            for f in range(2):
                u, a, b = EU[:, f, :], EW[0], EW[1]
                tt(a[:, 1:T1], u[:, 0:T1 - 1], u[:, 1:T1], ALU.add)
                dve.drain()
                tt(b[:, 2:T1 - 1], a[:, 1:T1 - 2], a[:, 3:T1], ALU.add)
                dve.drain()
                if f:
                    a2, b2 = EW2
                    tt(a2[:, 4:T1 - 3], b[:, 2:T1 - 5], b[:, 6:T1 - 1], ALU.add)
                    dve.drain()
                    tt(b2[:, 8:T1 - 7], a2[:, 4:T1 - 11], a2[:, 12:T1 - 3], ALU.add)
                    dve.drain()
                    a, b = a2, b2
                for rows, s in ((slice(0, 64), a), (slice(64, P), b)):
                    tt(PP[rows, f, 0:T2], s[rows, 8:8 + T2], INV[rows, f, :], ALU.mult)
                dve.drain()
                last = tt(PP[:, f, 0:T2], PP[:, f, 0:T2], u[:, 8:8 + T2], ALU.subtract)
            last.then_inc(st["e_pool"], 1)
            for f in range(10):
                bank = 2 * (f % 2)
                dve.wait_ge(st["e_rot"], f + 1)
                dve.drain()
                dst = EQ[:, f, 0:T2] if f < 6 else KD[:, f - 6, 0:T2]
                tt(EW[0][:, 0:T2], EQ[:, f, 0:T2] if f < 6 else G[:, bank, :], ROPE[:, 0, 0:T2], ALU.mult)
                tt(EW[1][:, 0:T2], G[:, bank + 1, :], ROPE[:, 1, 0:T2], ALU.mult)
                dve.drain()
                tt(dst, EW[0][:, 0:T2], EW[1][:, 0:T2], ALU.add).then_inc(st["e_rope"], 1)
            dve.wait_ge(st["e_pm"], 1)
            for f in range(2):
                ts(SCR[:, 2 + f, 0:T2], G[:, 6 + f, :], vec("pool_scale", f), None, ALU.mult).then_inc(h_ready, 1)
            dve.drain()
            for f in range(2):
                dve.wait_ge(h_high, SPLIT_AT["e_pool"][0] + f + 1)
                tt(YL[:, f, 0:T2], SCR[:, 2 + f, 0:T2], YH[:, f, 0:T2], ALU.subtract).then_inc(h_low, 1)
            for h in range(Q_HEADS):
                dve.wait_ge(st["e_s"], h + 1)
                dve.drain()
                for n in range(NB):
                    w = P * (band(n)[1] - band(n)[0] + 1)
                    nc.vector.reduce_max(EMX[:, n:n + 1], G[:, n, 0:w], AX.X)
                dve.drain()
                ts(EMX, EMX, HD ** -0.5, vec("sink", h), ALU.mult, ALU.max)
                dve.drain()
                ts(ENM, EMX, -1.0, None, ALU.mult).then_inc(st["e_mx"], 1)
                dve.wait_ge(st["e_e"], h + 1)
                tt(ERS, ESUM, ESK, ALU.add)
                dve.drain()
                nc.vector.reciprocal(EMX, ERS)
                dve.drain()
                for n in range(NB):
                    w = P * (band(n)[1] - band(n)[0] + 1)
                    last = ts(EPM[:, n, 0:w], EPM[:, n, 0:w], EMX[:, n:n + 1], None, ALU.mult)
                last.then_inc(st["e_p"], 1)
                if h % 2:
                    dve.wait_ge(h_high, SPLIT_AT["e_attn"][0] + h // 2 + 1)
                    tt(YL[:, 2 + h // 2, 0:T2], G[:, 7, :], YH[:, 2 + h // 2, 0:T2], ALU.subtract).then_inc(h_low, 1)
            take_copy(dve, CHUNKS["e_out"], 8, YF)
            dve.drain()
            post_norm_dve(dve, "evenp", [YF[:, f, 0:T2] for f in range(DT)], gains("norm_w_2", 3), 1.0)

        XBC = area(0, 16)
        XST = AR[:, 16 * T1:16 * T1 + 4 * D].rearrange("p (j m) -> p j m", m=D)
        DTR, SR, ER, OA, OZ, OW = (area(24 + i, 1)[0:32, 0, 0:T2] for i in range(6))
        COLS = AR[:, 30 * T1:30 * T1 + 512]
        STG, CV = area(31, 2), area(33, 2)
        OWT = [area(27 + i, 1)[:, 0, 0:T2] for i in range(2)]
        OM = [area(29, 1)[:, 0, 0:T2], area(31, 1)[:, 0, 0:T2]]
        OWD = AR[:, 32 * T1:32 * T1 + 512].rearrange("p (s m) -> p s m", s=2)
        SZ = area(16, 8)
        GP = AR[:, 8 * T1:8 * T1 + 4 * (T2 + CONV_K - 1)].rearrange("p (f t) -> p f t", t=T2 + CONV_K - 1)
        GA, SB_, CO = area(13, 4), area(17, 4), area(21, 4)
        MU = area(25, 1)[:, 0, 0:T2]
        AEXP = SM[0:32, 0:1]
        FE = [AR[:, 33 * T1:33 * T1 + 2 * T2].rearrange("p (a t) -> p a t", a=2), ROPE[:, :, 0:T2]]

        def odd_pe(pe):
            norm_pe(pe, "odd", T2)
            pe.wait_ge(h_low, split_end("odd"))
            product(pe, CHUNKS["dt"], 1, XH, XL)
            product(pe, CHUNKS["xbc"], 16, XH, XL)
            pe.wait_ge(st["o_dt"], 2)
            last = None
            for i, row in enumerate((SR, ER, DTR)):
                for j in range(NB):
                    last = nc.tensor.transpose(G[:, 4, 128 * i + 32 * j:128 * i + 32 * j + 32],
                                               row[:, P * j:P * j + P], ident[0:32, 0:32])
            last.then_inc(st["o_tr"], 1)
            pe.wait_ge(st["o_si"], 16 + 1)
            for f in range(DT):
                bank = 5 + f % 2
                if f >= 2:
                    pe.wait_ge(st["o_xc"], f - 1)
                for j in range(NB):
                    last = nc.tensor.transpose(G[:, bank, P * j:P * j + P], XBC[:, f, P * j:P * j + P], ident[:, :])
                last.then_inc(st["o_xt"], 1)
            pe.wait_ge(st["o_xc"], DT)
            pe.wait_ge(st["o_col"], 1)

            def broadcast(h):
                if h:
                    pe.wait_ge(st["o_fe"], h)
                mm(G[:, 4, :], ident[0:32, h:h + 1].broadcast_to([32, P]), SR, start=True, stop=True)
                mm(G[:, 5, :], ident[0:32, 16 + h:17 + h].broadcast_to([32, P]), ER, start=True,
                   stop=True).then_inc(st["o_bc"], 1)

            for h in range(SSM_HEADS):
                g = h // (SSM_HEADS // SSM_GROUPS)
                if h % (SSM_HEADS // SSM_GROUPS) == 0:
                    if h:
                        pe.wait_ge(st["o_m"], NB * h)
                    for j in range(NB):
                        last = mm(G[:, j, :], XBC[:, 8 + g, P * j:P * j + P], XBC[:, 12 + g, 0:T2], start=True, stop=True)
                    last.then_inc(st["o_cb"], 1)
                if h == 0:
                    broadcast(0)
                if h + 1 < SSM_HEADS:
                    broadcast(h + 1)
                if h % 2 == 0 and h >= 4:
                    pe.wait_ge(st["o_yd"], h // 2 - 1)
                for j in range(NB):
                    t = NB * h + j
                    pe.wait_ge(st["o_m"], t + 1)
                    mm(G[64 * (h % 2):64 * (h % 2) + 64, 6 + (h // 2) % 2, :], XST[:, j, 64 * h:64 * h + 64], OM[t % 2],
                       start=(j == 0), stop=(j == NB - 1)).then_inc(st["o_y"], 1)
            product(pe, CHUNKS["z"], 8, XH, XL)
            product(pe, CHUNKS["ga"], 4, XH, XL)
            product(pe, CHUNKS["gb"], 4, XH, XL)
            pe.wait_ge(st["o_yd"], SSM_HEADS // 2)
            norm_pe(pe, "ssm", T2)
            pe.wait_ge(st["o_gc"], 1)
            for f in range(4):
                last = mm(G[:, 6, :], ones[:, :], CO[:, f, 0:T2], start=(f == 0), stop=(f == 3))
            last.then_inc(st["o_mu"], 1)
            norm_pe(pe, "ln", T2)
            pe.wait_ge(h_low, split_end("o_g"))
            product(pe, CHUNKS["o_out_g"], 8, XH, XL, kt=4)
            product(pe, CHUNKS["o_out_y"], 8, YH, YL)
            norm_pe(pe, "oddp", T2)

        def odd_act(act):
            in_norm_act(act, "odd", CHUNKS["dt"])
            act_idle(act, CHUNKS["dt"], 1)
            act.wait_ge(psum_free, CHUNKS["dt"] + 1 + 4)
            nc.scalar.activation(OA, DTR, ACT.Abs)
            act.drain()
            nc.scalar.activation(OA, OA, ACT.Exp, scale=-1.0)
            nc.scalar.activation(AEXP, vec("a_log", 0, 32), ACT.Exp).then_inc(st["o_ab"], 1)

            def step(i, c):
                split_high(act, CHUNKS["xbc"] + 2, i, c)
                act.wait_ge(st["o_cv"], 4 * i + c + 1)
                nc.scalar.activation(XBC[:, 4 * i + c, 0:T2], CV[:, c % 2, 0:T2], ACT.Silu).then_inc(st["o_si"], 1)
            fours(act, 16, step)
            for f in range(DT):
                act.wait_ge(st["o_xt"], f + 1)
                nc.scalar.activation(XST[:, :, P * f:P * f + P],
                                     G[:, 5 + f % 2, :].rearrange("p (j m) -> p j m", m=P), ACT.Copy).then_inc(st["o_xc"], 1)

            def sums(h):
                act.wait_ge(st["o_bc"], h + 1)
                if h >= 2:
                    act.wait_ge(st["o_dg"], NB * (h - 1))
                nc.scalar.activation(FE[h % 2], G[:, 4:6, :], ACT.Copy).then_inc(st["o_fe"], 1)

            sums(0)
            for h in range(SSM_HEADS):
                for j in range(NB):
                    t, d0, d1 = NB * h + j, P * j, P * j + P
                    if j == 2 and h + 1 < SSM_HEADS:
                        sums(h + 1)
                    w, wd = OWT[t % 2], OWD[:, t % 2, :]
                    act.wait_ge(st["o_dg"], t + 1)
                    if t >= 2:
                        act.wait_ge(st["o_m"], t - 1)
                    nc.scalar.activation(w[:, d0:d1], wd[:, 0:P], ACT.Exp)
                    nc.scalar.activation(wd[:, P:2 * P], wd[:, P:2 * P], ACT.Exp, scale=-1.0)
                    if d1 < T2:
                        nc.scalar.activation(w[:, d1:T2], FE[h % 2][:, 0, d1:T2], ACT.Exp,
                                             bias=COLS[:, 384 + 32 * j + h:384 + 32 * j + h + 1])
                    if d0:
                        nc.scalar.activation(w[:, 0:d0], FE[h % 2][:, 1, 0:d0], ACT.Exp, scale=-1.0,
                                             bias=COLS[:, 128 + 32 * j + 16 + h:128 + 32 * j + 17 + h])
                    act.drain()
                    act.sem_inc(st["o_w"], 1)

            def evac(n, func, dst):
                act.wait_ge(psum_free, n + 4)

                def step(i, c):
                    split_high(act, n + 2, i, c)
                    act.wait_ge(tile_done, 4 * i + n + c + 1)
                    nc.scalar.activation(dst[:, 4 * i + c, 0:T2], acc(n, c)[:, 0, :], func).then_inc(psum_free, 1)
                return step
            fours(act, 8, evac(CHUNKS["z"], ACT.Silu, SZ))
            act_idle(act, CHUNKS["ga"], 4)
            fours(act, 4, evac(CHUNKS["gb"], ACT.Sigmoid, SB_))
            act.wait_ge(st["o_z"], 1)
            norm_act(act, "ssm", [XBC[:, f, 0:T2] for f in range(DT)], T2)
            split_act(act, "ssm", [YH[:, f, 0:T2] for f in range(DT)], T2)
            act.wait_ge(st["o_xm"], 1)
            norm_act(act, "ln", [CO[:, f, 0:T2] for f in range(4)], T2)
            act.wait_ge(st["o_g"], 1)
            for f in range(4):
                nc.scalar.activation(GA[:, f, 0:T2], CO[:, f, 0:T2], ACT.Silu, bias=vec("ln_b", f))
            act.drain()
            for f in range(4):
                nc.scalar.activation(XH[:, f, 0:T2], GA[:, f, 0:T2], ACT.Copy).then_inc(h_high, 1)
            act_idle(act, CHUNKS["o_out_g"], 8)
            act_idle(act, CHUNKS["o_out_y"], 8)
            post_norm_act(act, "oddp", CHUNKS["o_out_y"] + 8, [YF[:, f, 0:T2] for f in range(DT)])

        def odd_dve(dve):
            in_norm_dve(dve, "odd", CHUNKS["dt"], gains("norm_w_2", 8))
            dve.wait_ge(tile_done, CHUNKS["dt"] + 1)
            ts(DTR, acc(CHUNKS["dt"], 0)[0:32, 0, :], vec("dt_bias", 0, 32), None, ALU.add).then_inc(psum_free, 1)
            dve.wait_ge(st["o_ab"], 1)
            dve.drain()
            log1p(dve, SR, OA, OZ, OW)
            stt(DTR, DTR, 0.0, SR, ALU.max, ALU.add)
            ts(AEXP, AEXP, -1.0, None, ALU.mult)
            dve.drain()
            ts(OA, DTR, AEXP, None, ALU.mult)
            dve.drain()
            nc.vector.tensor_tensor_scan(SR, ones[0:32, 0:1].broadcast_to([32, T2]), OA, 0.0, ALU.mult, ALU.add)
            dve.drain()
            tt(ER, SR, OA, ALU.subtract).then_inc(st["o_dt"], 2)
            nc.vector.memset(STG[:, :, 0:2], 0.0)
            nc.vector.memset(STG[:, :, 2 + T2:3 + T2], 0.0).then_inc(st["o_si"], 1)

            def step(i, c):
                dve.drain()
                dve.wait_ge(tile_done, 4 * i + CHUNKS["xbc"] + c + 1)
                x, o = STG[:, c % 2, :], CV[:, c % 2, 0:T2]
                nc.vector.tensor_copy(x[:, 2:2 + T2], acc(CHUNKS["xbc"], c)[:, 0, :]).then_inc(psum_free, 1)
                dve.drain()
                dve.wait_ge(st["o_si"], 4 * i + c + 1)

                def col(name, j):
                    return V[:, bass.ds(VEC[name] + 16 * j + c + 4 * i, 1)]
                last = ts(o, x[:, 0:T2], col("sconv_w", 0), col("sconv_b", 0), ALU.mult, ALU.add)
                for j in range(1, 4):
                    dve.drain()
                    last = stt(o, x[:, j:j + T2], col("sconv_w", j), o, ALU.mult, ALU.add)
                last.then_inc(st["o_cv"], 1)
            fours(dve, 16, step)
            dve.wait_ge(st["o_tr"], 1)
            nc.vector.tensor_copy(COLS[:, 0:384], G[:, 4, 0:384])
            ts(COLS[:, 384:512], G[:, 4, 0:128], -1.0, None, ALU.mult).then_inc(st["o_col"], 1)
            dve.wait_ge(st["o_si"], 16 + 1)
            dve.drain()

            def diagonal(t):
                h, j = t // NB, t % NB
                d0, d1 = P * j, P * j + P
                wd = OWD[:, t % 2, :]
                if j == 0:
                    dve.wait_ge(st["o_fe"], h + 1)
                stt(wd[:, 0:P], FE[h % 2][:, 0, d0:d1], COLS[:, 384 + 32 * j + h:385 + 32 * j + h], mask_ge,
                    ALU.add, ALU.add)
                stt(wd[:, P:2 * P], FE[h % 2][:, 1, d0:d1], COLS[:, 128 + 32 * j + 16 + h:128 + 32 * j + 17 + h], mask_le,
                    ALU.subtract, ALU.subtract).then_inc(st["o_dg"], 1)

            total = NB * SSM_HEADS
            diagonal(0)
            for t in range(total):
                h, j = t // NB, t % NB
                d0, d1 = P * j, P * j + P
                w, wd, m = OWT[t % 2], OWD[:, t % 2, :], OM[t % 2]
                if t + 1 < total:
                    dve.drain()
                    diagonal(t + 1)
                if j == 0:
                    dve.wait_ge(st["o_cb"], h // (SSM_HEADS // SSM_GROUPS) + 1)
                dve.wait_ge(st["o_w"], t + 1)
                if t >= 2:
                    dve.wait_ge(st["o_y"], t - 1)
                dtf = COLS[:, 256 + 32 * j + h:257 + 32 * j + h]
                dtb = COLS[:, 256 + 32 * j + 16 + h:257 + 32 * j + 16 + h]
                dve.drain()
                stt(wd[:, P:2 * P], wd[:, P:2 * P], dtb, G[:, j, d0:d1], ALU.mult, ALU.mult)
                stt(m[:, d0:T2], w[:, d0:T2], dtf, G[:, j, d0:T2], ALU.mult, ALU.mult)
                if d0:
                    stt(m[:, 0:d0], w[:, 0:d0], dtb, G[:, j, 0:d0], ALU.mult, ALU.mult)
                dve.drain()
                tt(m[:, d0:d1], m[:, d0:d1], wd[:, P:2 * P], ALU.add).then_inc(st["o_m"], 1)
                if j == NB - 1 and h % 2:
                    f = h // 2
                    dve.wait_ge(st["o_y"], t + 1)
                    stt(XBC[:, f, 0:T2], XBC[:, f, 0:T2], vec("ssm_d", f), G[:, 6 + f % 2, :], ALU.mult,
                        ALU.add).then_inc(st["o_yd"], 1)
            dve.wait_ge(psum_free, CHUNKS["z"] + 8 + 4)
            dve.drain()
            for f in range(DT):
                last = tt(XBC[:, f, 0:T2], XBC[:, f, 0:T2], SZ[:, f, 0:T2], ALU.mult)
            last.then_inc(st["o_z"], 1)
            nc.vector.memset(GP[:, :, 0:CONV_K // 2], 0.0)
            nc.vector.memset(GP[:, :, CONV_K // 2 + T2:], 0.0)
            take_copy(dve, CHUNKS["ga"], 4, GA)
            dve.wait_ge(psum_free, CHUNKS["gb"] + 4 + 4)
            dve.drain()
            for f in range(4):
                tt(GP[:, f, CONV_K // 2:CONV_K // 2 + T2], GA[:, f, 0:T2], SB_[:, f, 0:T2], ALU.mult)
            dve.drain()
            for j in range(CONV_K):
                for f in range(4):
                    x, o, wj = GP[:, f, j:j + T2], CO[:, f, 0:T2], vec("dw_w", 4 * j + f)
                    if j == 0:
                        last = ts(o, x, wj, vec("dw_b", f), ALU.mult, ALU.add)
                    else:
                        last = stt(o, x, wj, o, ALU.mult, ALU.add)
                    if j == CONV_K - 1 and f == 3:
                        last.then_inc(st["o_gc"], 1)
                dve.drain()
            norm_dve_stats(dve, "ssm", T2, D)
            norm_split_dve(dve, [XBC[:, f, 0:T2] for f in range(DT)], gains("ssm_norm", 0),
                           [YH[:, f, 0:T2] for f in range(DT)], [YL[:, f, 0:T2] for f in range(DT)], T2,
                           SPLIT_AT["ssm"][0])
            dve.wait_ge(st["o_mu"], 1)
            ts(MU, G[:, 6, :], 1.0 / 512, None, ALU.mult)
            dve.drain()
            for f in range(4):
                last = tt(CO[:, f, 0:T2], CO[:, f, 0:T2], MU, ALU.subtract)
            last.then_inc(st["o_xm"], 1)
            norm_dve_stats(dve, "ln", T2, 512)
            for f in range(4):
                last = stt(CO[:, f, 0:T2], CO[:, f, 0:T2], vec("ln_g", f), SCR[:, 4, 0:T2], ALU.mult, ALU.mult)
            last.then_inc(st["o_g"], 1)
            for f in range(4):
                dve.wait_ge(h_high, SPLIT_AT["o_g"][0] + f + 1)
                tt(XL[:, f, 0:T2], GA[:, f, 0:T2], XH[:, f, 0:T2], ALU.subtract).then_inc(h_low, 1)
            take_copy(dve, CHUNKS["o_out_g"], 8, YF)
            take_add_2(dve, CHUNKS["o_out_y"], 8, YF)
            dve.drain()
            post_norm_dve(dve, "oddp", [YF[:, f, 0:T2] for f in range(DT)], gains("norm_w_2", 9), 1.0)


        CONST_LOADS = 16 * 7

        @block.sync
        def _(sp):
            for dst, src in ((V[:, :], vecs), (MATS[:, :, :], mats[:, 1:9, :]), (ident[:, :], mats[:, 0, :]),
                             (PW[:, :, :], pool_w), (ROPE[:, :, :], rope1),
                             (H[:, :, :], xT.rearrange("(f p) t -> p f t", p=P)), (LRU_W, lru_w)):
                sp.dma_start(dst, src).then_inc(const_loaded, 16)
            stream(sp)

        @block.gpsimd
        def _(pool):
            pool_stream(pool)

        @block.scalar
        def _(act):
            split_high(act, 0, 0, 0)
            split_high(act, 0, 0, 1)
            if upto >= 1:
                in_norm_act(act, "mix0", 0)
                lru_act(act)
            if upto >= 2:
                mlstm_act(act)
            if upto >= 3:
                mlp_act(act, 0)
            if upto >= 4:
                diff_act(act)
            if upto >= 5:
                mlp_act(act, 1)
            if upto >= 6:
                final_act(act)
                ffn_act(act, 0)
            if upto >= 7:
                even_act(act)
            if upto >= 8:
                ffn_act(act, 1)
            if upto >= 9:
                ffn_act(act, 2)
            if upto >= 10:
                odd_act(act)
            if upto >= 11:
                ffn_act(act, 3)
            act.wait_ge(out_done, 1)
            act.dma_start(out.rearrange("(f p) t -> p f t", p=P), H[:, :, META:T1]).then_inc(out_done, 16)
            act.wait_ge(out_done, 17)

        @block.vector
        def _(dve):
            nc.vector.memset(ones[:, :], 1.0).then_inc(ones_ready, 1)
            nc.vector.memset(SM[:, :], 0.0).then_inc(psum_free, 4)
            dve.wait_ge(const_loaded, CONST_LOADS)
            dve.drain()
            if upto >= 1:
                in_norm_dve(dve, "mix0", 0, gains("norm_mix", 0))
                lru_dve(dve)
            if upto >= 2:
                mlstm_dve(dve)
            if upto >= 3:
                mlp_dve(dve, 0)
            if upto >= 4:
                diff_dve(dve)
            if upto >= 5:
                mlp_dve(dve, 1)
            if upto >= 6:
                final_dve(dve)
                ffn_dve(dve, 0)
            if upto >= 7:
                even_dve(dve)
            if upto >= 8:
                ffn_dve(dve, 1)
            if upto >= 9:
                ffn_dve(dve, 2)
            if upto >= 10:
                odd_dve(dve)
            if upto >= 11:
                ffn_dve(dve, 3)
            dve.drain()
            dve.sem_inc(out_done, 1)

        @block.tensor
        def _(pe):
            pe.wait_ge(const_loaded, CONST_LOADS)
            pe.wait_ge(ones_ready, 1)
            if upto >= 1:
                norm_pe(pe, "mix0", T1)
                lru_pe(pe)
            if upto >= 2:
                mlstm_pe(pe)
            if upto >= 3:
                norm_pe(pe, "mlp0", T1)
                mlp_pe(pe, 0)
            if upto >= 4:
                diff_pe(pe)
            if upto >= 5:
                norm_pe(pe, "mlp1", T1)
                mlp_pe(pe, 1)
            if upto >= 6:
                norm_pe(pe, "final", T1)
                ffn_pe(pe, 0)
            if upto >= 7:
                even_pe(pe)
            if upto >= 8:
                ffn_pe(pe, 1)
            if upto >= 9:
                ffn_pe(pe, 2)
            if upto >= 10:
                odd_pe(pe)
            if upto >= 11:
                ffn_pe(pe, 3)


def _chunks(w, k0, kt, columns):
    m = len(columns) * P if isinstance(columns, list) else columns.stop - columns.start
    if isinstance(columns, list):
        cols = np.concatenate([np.arange(c, c + P) for c in columns])
        part = w[k0:k0 + kt * P][:, cols]
    else:
        part = w[k0:k0 + kt * P, columns]
    nt = (m + P - 1) // P
    full = np.zeros((DT * P, nt * P), w.dtype)
    full[0:kt * P, 0:m] = part
    return full.reshape(DT, P, nt, P).transpose(2, 1, 0, 3).reshape(nt, P, DT * P)


def pack_weights(x):
    out = np.zeros((N_CHUNKS, P, DT * P), np.float32)

    def put(name, *args):
        c = _chunks(*args)
        out[CHUNKS[name]:CHUNKS[name] + len(c)] = c

    w = x["ab_w_in"][0]
    for name, a, b in (("q", 0, 1024), ("k", 1024, 2048), ("v", 2048, 3072), ("o", 3072, 4096), ("gi", 4096, 4100),
                       ("gf", 4100, 4104), ("xb", 4104, 5128), ("gate", 5128, 6152)):
        put(name, w, 0, 8, slice(a, b))
    put("out_a", x["ab_w_out"][0], 0, 8, slice(0, D))
    put("out_b", x["ab_w_out"][0], D, 8, slice(0, D))
    for l in range(2):
        at = 0
        for p, f in enumerate(FF1_PARTS):
            put(f"mlp{l}_up{p}", x["mlp_w1"][l], 0, 8, slice(at * P, (at + f) * P))
            put(f"mlp{l}_down{p}", x["mlp_w2"][l], at * P, f, slice(0, D))
            at += f
    w = x["c_w_in"][0]
    for i, name in enumerate(("cq", "ck", "cv")):
        put(name, w, 0, 8, slice(D * i, D * i + D))
    put("c_out", x["c_w_out"][0], 0, 8, slice(0, D))
    for i in range(4):
        g, u, d = (x[f"ffn_w_{s}_2"][i // 2, i % 2] for s in ("gate", "up", "down"))
        at = 0
        for p, f in enumerate(FF2_PARTS):
            n = CHUNKS[f"ffn{i}_up{p}"]
            out[n:n + 2 * f:2] = _chunks(g, 0, 8, slice(at * P, (at + f) * P))
            out[n + 1:n + 2 * f:2] = _chunks(u, 0, 8, slice(at * P, (at + f) * P))
            put(f"ffn{i}_down{p}", d, at * P, f, slice(0, D))
            at += f
    w = x["ev_w_in_2"][0]
    for name, a, b in (("eu", 0, 256), ("eq", 256, 1024), ("ek", 1024, 1280), ("ev", 1280, 1536)):
        put(name, w, 0, 8, slice(a, b))
    put("e_out", x["ev_w_out_2"][0], 0, 8, slice(0, D))
    w = x["od_w_in_2"][0]
    for name, a, b in (("ga", 0, 512), ("gb", 512, 1024), ("z", 1024, 2048), ("xbc", 2048, 4096), ("dt", 4096, 4128)):
        put(name, w, 0, 8, slice(a, b))
    put("o_out_g", x["od_w_out_2"][0], 0, 4, slice(0, D))
    put("o_out_y", x["od_w_out_2"][0], 512, 8, slice(0, D))
    return out


def pack_vectors(x):
    v = np.zeros((P, VEC["end"]), np.float32)

    def put(name, a):
        a = np.asarray(a).reshape(-1, P).T
        v[:, VEC[name]:VEC[name] + a.shape[1]] = a

    for name, key in (("norm_mix", "norm_mix"), ("norm_mlp", "norm_mlp"), ("norm_final", "norm_final"),
                      ("mlstm_norm", "mlstm_norm"), ("conv_w", "lru_conv_w"), ("conv_b", "lru_conv_b"),
                      ("b_r", "lru_b_r"), ("b_i", "lru_b_i"), ("lam", "lru_lambda"), ("subln", "c_subln"),
                      ("norm_w_2", "norm_w_2"), ("pool_scale", "ev_pool_scale_2"), ("dw_w", "cv_dw_w_2"),
                      ("dw_b", "cv_dw_b_2"), ("ln_g", "cv_ln_g_2"), ("ln_b", "cv_ln_b_2"),
                      ("sconv_w", "ssm_conv_w_2"), ("sconv_b", "ssm_conv_b_2"), ("ssm_norm", "ssm_norm_w_2")):
        put(name, x[key])
    put("ssm_d", np.repeat(x["ssm_D_2"][0], HD))
    v[0:A_HEADS, VEC["i_bias"]] = x["ab_if_bias"][0, 0:A_HEADS]
    v[0:A_HEADS, VEC["f_bias"]] = x["ab_if_bias"][0, A_HEADS:]
    v[0:32, VEC["a_log"]] = x["ssm_A_log_2"][0].reshape(-1)
    v[0:32, VEC["dt_bias"]] = x["ssm_dt_bias_2"][0].reshape(-1)
    v[:, VEC["sink"]:VEC["sink"] + Q_HEADS] = x["ev_sink_2"][0]
    v[:, VEC["c_lambda"]:VEC["c_lambda"] + 256] = x["c_lambda"][0].reshape(-1)
    return v


def constants():
    m = np.zeros((9, P, P), np.float32)
    r, c = np.arange(P)[:, None], np.arange(P)[None, :]
    m[0] = np.eye(P)
    m[1] = np.where(c >= r, 0, -BIG)
    m[2] = np.where(c <= r, 0, -BIG)
    for base in (0, 64):
        for i in range(ROT1 // 2):
            m[3, base + ROT1 // 2 + i, base + i] = -1
            m[3, base + i, base + ROT1 // 2 + i] = 1
    for base in (0, 64):
        for i in range(HD // 2):
            m[4, base + 32 + i, base + i] = -1
            m[4, base + i, base + 32 + i] = 1
    for half in range(2):
        for base in (0, 64):
            for i in range(HD):
                m[5 + half, 64 * half + i, base + i] = 1
    for half in range(2):
        m[7 + half] = m[5 + half] @ m[4]

    def tables(t, rot, theta, inv=None):
        half = rot // 2
        f32 = np.float32
        if inv is None:
            inv = np.power(f32(theta), -np.arange(0, rot, 2, dtype=f32) / f32(rot))
        else:
            inv = (f32(1) / (f32(theta) ** (np.arange(0, rot, 2, dtype=f32) / f32(rot)))).astype(f32)
        ang = (inv.astype(f32)[:, None] * np.arange(t, dtype=f32)[None, :]).astype(f32).astype(np.float64)
        out = np.zeros((P, 2, t), np.float32)
        out[:, 0] = 1
        for base in (0, 64):
            for part in range(2):
                rows = slice(base + part * half, base + (part + 1) * half)
                out[rows, 0] = np.cos(ang)
                out[rows, 1] = np.sin(ang)
        return out

    inv = np.zeros((P, 2, T2), np.float32)
    t = np.arange(T2)
    for g, w in enumerate(POOL_W):
        count = np.clip(t + w - w // 2, 0, T2) - np.clip(t - w // 2, 0, T2)
        inv[64 * (g % 2):64 * (g % 2) + 64, g // 2] = 1.0 / count
    return m.transpose(1, 0, 2).copy(), tables(T1, ROT1, THETA1), tables(T2, HD, THETA2, True), inv


def arrays(inputs):
    x = {k: np.asarray(a) for k, a in inputs.items()}
    xT = np.ascontiguousarray(np.concatenate([x["meta_tokens"], x["x"][0]]).T)
    mats, rope1, rope2, inv = constants()
    lru_w = np.concatenate([x["lru_w_r"][0], x["lru_w_i"][0]]).transpose(1, 0, 2).copy()
    pw = np.zeros((P, 2, P), np.float32)
    for g in range(4):
        s = slice(64 * (g % 2), 64 * (g % 2) + 64)
        pw[s, g // 2, s] = x["ev_pool_w_2"][0, g]
    return {"xT": xT, "weights": pack_weights(x), "vecs": pack_vectors(x), "mats": mats, "lru_w": lru_w,
            "pool_w": pw, "rope1": rope1, "rope2": rope2, "pool_inv": inv}


def kernel(**inputs):
    import concourse.bacc as bacc
    from concourse.bass_utils import run_bass_kernel_spmd

    nc = bacc.Bacc("TRN2", target_bir_lowering=False, num_devices=1)
    data = {f"in_{k}": a for k, a in arrays(inputs).items()}
    args = [nc.dram_tensor(k, a.shape, mybir.dt.from_np(a.dtype), kind="ExternalInput").ap() for k, a in data.items()]
    out = nc.dram_tensor("out_dram", (D, T2), mybir.dt.float32, kind="ExternalOutput").ap()
    build(nc, *args, out)
    r = run_bass_kernel_spmd(nc, [data], core_ids=[0])
    return np.ascontiguousarray(r.results[0]["out_dram"].T)[None]
```

```python
import math
from contextlib import ExitStack

import numpy as np

import concourse.bass as bass
from concourse import mybir

P = 128
D = 1024
DT = D // P
META = 16
SEQ = 512
T1 = META + SEQ
T2 = SEQ
A_HEADS, A_DIM = 4, 256
CONV1 = 4
LRU_C = 8.0
C_HEADS, C_QK, C_V = 8, 64, 128
ROT1, THETA1 = C_QK // 4, 500000.0
LAMBDA_INIT = 0.8 - 0.6 * math.exp(-0.3)
FF1_PARTS = [8, 8, 8, 8]
FF2 = 2816
FF2_PARTS = [8, 8, 6]
POOL_W = (2, 4, 8, 16)
HD = 64
Q_HEADS, KV_HEADS = 12, 4
GROUP = Q_HEADS // KV_HEADS
THETA2 = 10000.0
CONV_K = 31
SSM_HEADS, SSM_GROUPS = 16, 4
EPS = 1e-6
BIG = 1e30

CHUNKS = {}


def _plan():
    n = 0

    def take(name, count):
        nonlocal n
        CHUNKS[name] = n
        n += count

    for name, count in (("xb", 8), ("gate", 8), ("qk", 16), ("gi", 1), ("gf", 1), ("v", 8),
                        ("o", 8), ("out_lru", 8), ("out_mlstm", 8)):
        take(name, count)
    for p, f in enumerate(FF1_PARTS):
        take(f"mlp0_up{p}", f)
        take(f"mlp0_down{p}", 8)
    for name, count in (("cq", 8), ("ck", 8), ("cv", 8), ("c_out", 8)):
        take(name, count)
    for p, f in enumerate(FF1_PARTS):
        take(f"mlp1_up{p}", f)
        take(f"mlp1_down{p}", 8)

    def ffn(i):
        for p, f in enumerate(FF2_PARTS):
            take(f"ffn{i}_up{p}", 2 * f)
            take(f"ffn{i}_down{p}", 8)

    ffn(0)
    for name, count in (("eu", 2), ("eq", 6), ("ek", 2), ("ev", 2), ("e_out", 8)):
        take(name, count)
    ffn(1)
    ffn(2)
    for name, count in (("ga", 4), ("gb", 4), ("dt", 1), ("xbc", 16), ("z", 8), ("o_out_g", 8), ("o_out_y", 8)):
        take(name, count)
    ffn(3)
    CHUNKS["end"] = n


_plan()
N_CHUNKS = CHUNKS["end"]

VEC = {}


def _vecs():
    n = 0
    for name, cols in (("norm_mix", 16), ("norm_mlp", 16), ("norm_final", 8), ("mlstm_norm", 8), ("conv_w", 32),
                       ("conv_b", 8), ("b_r", 8), ("b_i", 8), ("lam", 8), ("subln", 1), ("norm_w_2", 96),
                       ("pool_scale", 2), ("dw_w", 4 * CONV_K), ("dw_b", 4), ("ln_g", 4), ("ln_b", 4),
                       ("sconv_w", 64), ("sconv_b", 16), ("ssm_d", 8), ("ssm_norm", 8), ("i_bias", 1),
                       ("f_bias", 1), ("a_log", 1), ("dt_bias", 1), ("sink", 12), ("c_lambda", 256)):
        VEC[name] = n
        n += cols
    VEC["end"] = n


_vecs()

NORMS = {}


def _norms():
    q = base = 0
    order = [("ln", 4), ("ssm", 8)]
    for name, size in order:
        NORMS[name] = (q, base, size)
        q += 1
        base += size


_norms()


def build(nc, xT, weights, vecs, mats, lru_w, pool_w, rope1, rope2, pool_inv, out):
    f32, f32r = mybir.dt.float32, mybir.dt.float32r
    ALU, ACT, AX = mybir.AluOpType, mybir.ActivationFunctionType, mybir.AxisListType
    tt, stt, ts = nc.vector.tensor_tensor, nc.vector.scalar_tensor_tensor, nc.vector.tensor_scalar
    mm = nc.tensor.matmul

    ctx = ExitStack()
    with ctx:
        def sb(name, shape, dt=f32):
            return ctx.enter_context(nc.sbuf_tensor(name, shape, dt))

        def sem(name):
            return ctx.enter_context(nc.semaphore(name))

        H = sb("resid", [P, DT, T1])
        XH, XL = sb("x_hi", [P, DT, T1], f32r), sb("x_lo", [P, DT, T1], f32r)
        YH, YL = sb("y_hi", [P, DT, T1], f32r), sb("y_lo", [P, DT, T1], f32r)
        RAW = sb("w_raw", [P, 4, DT * P])
        WH, WL = sb("w_hi", [P, 2, DT * P], f32r), sb("w_lo", [P, 2, DT * P], f32r)
        ident = sb("ident", [P, P])
        MATS = sb("mats", [P, 8, P])
        mask_ge, mask_le, rot1, rot2 = (MATS[:, i, :] for i in range(4))
        dup = [MATS[:, 4 + i, :] for i in range(2)]
        rot_dup = [MATS[:, 6 + i, :] for i in range(2)]
        ones = sb("ones", [P, P])
        V = sb("vecs_sb", [P, VEC["end"]])
        PW = sb("pool_w_sb", [P, 2, P])
        ROPE = sb("rope_sb", [P, 2, T1])
        SM = sb("small", [P, 64])
        COL = sb("columns", [P, 144])
        RS, ACC = sb("scale", [P, T1]), sb("square_sum", [P, T1])
        AR = sb("arena", [P, 35 * T1])

        def area(at, tiles, width=T1):
            return AR[:, at * T1:at * T1 + tiles * width].rearrange("p (f t) -> p f t", t=width)

        G = ctx.enter_context(nc.psum_tensor("psum", [P, 8, 512], f32))
        GF = G[:, :, :].rearrange("p b n -> p (b n)")
        SCR = area(29, 6)
        SQ = [SCR[:, i, :] for i in range(2)]
        VAR, DEV = SCR[:, 4, 0:T2], SCR[:, 5, 0:T2]
        HSQ = [area(i, 1)[:, 0, :] for i in (26, 27, 28, 33)]
        VCOL, SCOL, RCOL = (COL[:, 8 * i:8 * i + 8] for i in range(3))
        HVAR, HDEV, HCOL = (COL[:, 24 + 40 * i:64 + 40 * i] for i in range(3))

        def vec(name, i=0, rows=P):
            return V[0:rows, VEC[name] + i:VEC[name] + i + 1]

        vecs_loaded, const_loaded = sem("vecs_loaded"), sem("const_loaded")
        x_loaded = [sem(f"x_loaded{f}") for f in range(DT)]
        rope_loaded = sem("rope_loaded")
        raw_loaded = [sem(f"raw_loaded{i}") for i in range(4)]
        high_ready, low_ready = sem("high_ready"), sem("low_ready")
        tile_done, psum_free = sem("tile_done"), sem("psum_free")
        squared, added, summed_up, mean_ready = sem("squared"), sem("added"), sem("summed_up"), sem("mean_ready")
        dev_ready, root_ready, spread, scale_ready = sem("dev_ready"), sem("root_ready"), sem("spread"), sem("scale_ready")
        wide_summed, wide_mean, wide_dev = sem("wide_summed"), sem("wide_mean"), sem("wide_dev")
        x_high, x_low, final_tile, updated = sem("x_high"), sem("x_low"), sem("final_tile"), sem("updated")
        term_ready = sem("term_ready")
        hn_sq, hn_sum, hn_var, hn_dev, hn_rec, hn_bc, hn_used = (sem(k) for k in (
            "hn_sq", "hn_sum", "hn_var", "hn_dev", "hn_rec", "hn_bc", "hn_used"))
        sq_in, sum_in, var_in, std_in = sem("sq_in"), sem("sum_in"), sem("var_in"), sem("std_in")
        h_ready, h_high, h_low = sem("h_ready"), sem("h_high"), sem("h_low")
        silu_done = sem("silu_done")
        ones_ready = sem("ones_ready")
        out_done = sem("out_done")
        st = {k: sem(k) for k in (
            "lru_w", "lru_sp", "lru_xc", "lru_ps", "lru_sg", "lru_ex", "lru_v", "lru_sq", "lru_h", "lru_ge",
            "ml_gate", "ml_abs", "ml_m", "ml_em", "ml_tr", "ml_col", "ml_vt", "ml_vc", "ml_bc", "ml_bcc",
            "ml_s", "ml_dg", "ml_d", "ml_p", "ml_pv", "ml_h", "ml_sig", "ml_rc", "ml_og",
            "c_lam", "c_lex", "c_rot", "c_rope", "c_vt", "c_vc", "c_s", "c_mx", "c_e", "c_pd", "c_pt", "c_ptc",
            "c_pv", "c_o",
            "e_pool", "e_pm", "e_rot", "e_rope", "e_vt", "e_vc", "e_s", "e_mx", "e_e", "e_p", "e_pt", "e_ptc",
            "e_pv", "e_o", "inv_loaded",
            "o_dt", "o_ab", "o_a", "o_tr", "o_col", "o_cv", "o_si", "o_xt", "o_xc", "o_cb", "o_bc",
            "o_fe", "o_gp", "o_gt", "o_gu", "o_dg", "o_w", "o_m", "o_y", "o_yd", "o_z", "o_g", "o_gc", "o_mu", "o_xm", "o_sl")}

        block = ctx.enter_context(nc.Block())

        def is1(n):
            return n < CHUNKS["ffn0_up0"]

        def slots(n):
            return 2 if is1(n) else 4

        def acc(n, c):
            s = (n + c) % slots(n)
            return G[:, 2 * s:2 * s + 2, 0:T1 // 2] if is1(n) else G[:, s:s + 1, 0:T2]

        def toks(ap, n):
            return ap.rearrange("p (a t) -> p a t", a=2 if is1(n) else 1)

        def width(n):
            return T1 if is1(n) else T2

        def fours(eng, count, step, peel=False, start=0):
            full = count // 4
            looped = full - 1 if peel else full
            first = 0
            if start:
                for c in range(start, min(4, count)):
                    step(0, c)
                if count < 4:
                    return
                first = 1
            if looped - first > 1:
                with eng.Fori(first, looped) as i:
                    for c in range(4):
                        step(i, c)
            else:
                looped = first
            for i in range(looped, full):
                for c in range(4):
                    step(i, c)
            for c in range(count - 4 * full):
                step(full, c)

        def pieces(c0, c1):
            return [(a, b) for a, b in ((c0, min(c1, 512)), (max(c0, 512), c1)) if a < b]

        def load_chunk(sp, n, slot):
            sp.dma_start(RAW[:, slot, :], weights[n]).then_inc(raw_loaded[slot], 16)

        def stream(sp):
            total = N_CHUNKS
            full = total // 4
            with sp.Fori(1, full) as i:
                for c in range(4):
                    sp.wait_ge(low_ready, 4 * i + c - 3)
                    load_chunk(sp, 4 * i + c, c)
            for n in range(4 * full, total):
                sp.wait_ge(low_ready, n - 3)
                load_chunk(sp, n, n % 4)

        def split_high(act, n, i, c):
            act.wait_ge(raw_loaded[(n + c) % 4], 16 * (i + (n + c) // 4 + 1))
            if n + c >= 2:
                act.wait_ge(tile_done, 4 * i + n + c - 1)
            nc.scalar.activation(WH[:, (n + c) % 2, :], RAW[:, (n + c) % 4, :], ACT.Copy).then_inc(high_ready, 1)

        def pool_stream(pool, begin, end):
            def one(n, i, c):
                pool.wait_ge(high_ready, 4 * i + n + c + 1)
                nc.gpsimd.tensor_tensor(WL[:, (n + c) % 2, :], RAW[:, (n + c) % 4, :], WH[:, (n + c) % 2, :],
                                        ALU.subtract).then_inc(low_ready, 1)
            fours(pool, end - begin, lambda i, c: one(begin, i, c))

        def product(pe, n, count, hi, lo, kt=8, start=0, follow=False, parts=None):
            w = width(n)
            if start >= count:
                return
            if not start and not follow and parts is None:
                pe.wait_ge(psum_free, n + 4)

            def step(i, c, waits=False):
                pe.wait_ge(low_ready, 4 * i + n + c + 1)
                pe.wait_ge(psum_free, 4 * i + n + c - slots(n) + 1 + 4)
                o = acc(n, c)
                banks = o.shape[1]
                ws = (n + c) % 2
                last = None
                for k in range(kt):
                    if waits:
                        pe.wait_ge(h_low, parts + k + 1)
                    for p, (wt, x) in enumerate(((WH, hi), (WH, lo), (WL, hi))):
                        for a in range(banks):
                            last = mm(o[:, a, :], wt[:, ws, k * P:k * P + P],
                                      x[:, k, a * (w // banks):(a + 1) * (w // banks)],
                                      start=(k == 0 and p == 0), stop=(k == kt - 1 and p == 2))
                last.then_inc(tile_done, 1)
            if parts is not None:
                step(0, 0, True)
                start = 1
            fours(pe, count, step, start=start)

        def act_idle(act, n, count, start=0):
            def step(i, c):
                if n + c + 2 + 4 * (i if isinstance(i, int) else 0) < N_CHUNKS:
                    split_high(act, n + 2, i, c)
            fours(act, count, step, peel=(n + count + 2 > N_CHUNKS), start=start)

        def take(dve, n, count, op):
            dve.drain()

            def step(i, c):
                dve.wait_ge(tile_done, 4 * i + n + c + 1)
                op(acc(n, c), i, c).then_inc(psum_free, 1)
            fours(dve, count, step)

        def take_copy(dve, n, count, dst):
            w = width(n)
            take(dve, n, count, lambda ps, i, c: nc.vector.tensor_copy(toks(dst[:, 4 * i + c, 0:w], n), ps))

        def take_scaled(dve, n, count, dst, offset=0):
            w = width(n)
            take(dve, n, count, lambda ps, i, c: tt(toks(dst[:, 4 * i + c, offset:offset + w], n), ps,
                                                    toks(RS[:, 0:w], n), ALU.mult))

        def take_add(dve, n, count, dst):
            take(dve, n, count, lambda ps, i, c: tt(toks(dst[:, 4 * i + c, :], n), ps,
                                                    toks(dst[:, 4 * i + c, :], n), ALU.add))

        def take_scaled_add(dve, n, count, dst, w):
            def step(i, c):
                t = SCR[:, 4 + c % 2, 0:w]
                dve.drain()
                dve.wait_ge(tile_done, 4 * i + n + c + 1)
                tt(toks(t, n), acc(n, c), toks(RS[:, 0:w], n), ALU.mult).then_inc(psum_free, 1)
                dve.drain()
                tt(dst[:, 4 * i + c, 0:w], dst[:, 4 * i + c, 0:w], t, ALU.add)
            fours(dve, count, step)

        def norm_act(act, name, srcs, w, beside=None):
            q, base, size = NORMS[name]
            for f, src in enumerate(srcs):
                if base + f >= 2:
                    act.wait_ge(sum_in, base + f - 1)
                nc.scalar.activation(SCR[:, (base + f) % 2, 0:w], src, ACT.Square).then_inc(sq_in, 1)
            if beside:
                beside()
            act.wait_ge(var_in, q + 1)
            nc.scalar.activation(SCR[:, 5, 0:w], SCR[:, 4, 0:w], ACT.Sqrt).then_inc(std_in, 1)

        def norm_pe(pe, name, w):
            q, base, size = NORMS[name]
            if q:
                pe.wait_ge(var_in, q)
            for f in range(size):
                pe.wait_ge(sq_in, base + f + 1)
                last = None
                for a, b in pieces(0, w):
                    last = mm(GF[:, 2048 + a:2048 + b], ones[:, :], SCR[:, (base + f) % 2, a:b],
                              start=(f == 0), stop=(f == size - 1))
                last.then_inc(sum_in, 1)

        def norm_dve_stats(dve, name, w, dims):
            q, base, size = NORMS[name]
            dve.wait_ge(sum_in, base + size)
            dve.drain()
            ts(SCR[:, 4, 0:w], GF[:, 2048:2048 + w], 1.0 / dims, EPS, ALU.mult, ALU.add).then_inc(var_in, 1)
            dve.wait_ge(std_in, q + 1)
            nc.vector.reciprocal(SCR[:, 4, 0:w], SCR[:, 5, 0:w])
            dve.drain()

        def split_act(act, name, his, w, start=0):
            for f, hi in enumerate(his, start):
                tmp = SCR[:, 2 + f % 2, 0:w]
                act.wait_ge(h_ready, READY_AT[name] + f + 1)
                nc.scalar.activation(hi, tmp, ACT.Copy).then_inc(h_high, 1)

        def norm_split_dve(dve, srcs, gains, his, los, w, base):
            n = len(srcs)

            def make(f):
                stt(SCR[:, 2 + f % 2, 0:w], srcs[f], gains[f], SCR[:, 4, 0:w], ALU.mult,
                    ALU.mult).then_inc(h_ready, 1)
            make(0)
            if n > 1:
                make(1)
            for f in range(n):
                dve.wait_ge(h_high, base + f + 1)
                if f < 2:
                    dve.drain()
                tt(los[f], SCR[:, 2 + f % 2, 0:w], his[f], ALU.subtract).then_inc(h_low, 1)
                if f + 2 < n:
                    dve.drain()
                    make(f + 2)
            dve.drain()

        SPLIT_AT, READY_AT = {}, {}
        order = [("lru", 8), ("mh", 8)]
        order += [(f"mlp0_{p}", f) for p, f in enumerate(FF1_PARTS)] + [("ch", 8)]
        order += [(f"mlp1_{p}", f) for p, f in enumerate(FF1_PARTS)]

        def ffn_order(i):
            return [(f"ffn{i}_{p}", f) for p, f in enumerate(FF2_PARTS)]
        order += ffn_order(0) + [("e_pool", 2), ("e_attn", 6)] + ffn_order(1) + ffn_order(2)
        order += [("o_g", 4), ("ssm", 8)] + ffn_order(3)
        at = ready = 0
        for name, size in order:
            SPLIT_AT[name] = (at, size)
            READY_AT[name] = ready
            at += size
            if not (name.startswith(("mlp0_", "mlp1_", "ffn")) or name in ("e_attn", "o_g")):
                ready += size

        def split_end(name):
            return sum(SPLIT_AT[name])

        PREPS = ["mix0", "mlp0", "mix1", "mlp1", "f0", "even", "f1", "f2", "odd", "f3"]
        PREP_GAIN = {"mix0": ("norm_mix", 0), "mlp0": ("norm_mlp", 0), "mix1": ("norm_mix", 1), "mlp1": ("norm_mlp", 1),
                     "f0": ("norm_w_2", 0), "even": ("norm_w_2", 2), "f1": ("norm_w_2", 4), "f2": ("norm_w_2", 6),
                     "odd": ("norm_w_2", 8), "f3": ("norm_w_2", 10)}
        SUMS = ["mix0", "mlp0", "mix1", "mlp1", "final", "f0p", "evenp", "f1p", "f2p", "oddp", "f3p"]
        SQUARES = {}
        for name in ("mix0", "mlp0", "mix1", "mlp1", "final", "f0", "f0p", "even", "evenp", "f1", "f1p", "f2", "f2p",
                     "odd", "oddp", "f3", "f3p"):
            SQUARES[name] = 8 * len(SQUARES)

        def resid(block2):
            return [H[:, f, META:T1] if block2 else H[:, f, :] for f in range(DT)]

        def wide(name):
            return PREPS.index(name) < 4 if name in PREPS else False

        def gains(name, i):
            return [vec(name, 8 * i + f) for f in range(DT)]

        def prep_gain(name, f):
            v, i = PREP_GAIN[name]
            return vec(v, 8 * i + f)

        def square(act, name, f, src, w):
            dst = ACC if f == 0 else SQ[f % 2]
            nc.scalar.activation(dst[:, 0:w], src, ACT.Square).then_inc(squared, 1)

        def add_square(dve, name, f, w):
            dve.wait_ge(squared, SQUARES[name] + f + 1)
            dve.drain()
            last = tt(ACC[:, 0:w], ACC[:, 0:w], SQ[f % 2][:, 0:w], ALU.add)
            last.then_inc(added, 1)

        def parts_of(name):
            return (YH, YL) if name == "mix0" else (XH, XL)

        def high_part(act, name, f, w):
            r = resid(not wide(name))[f]
            nc.scalar.activation(parts_of(name)[0][:, f, 0:w], r, ACT.Copy, scale=prep_gain(name, f)).then_inc(x_high, 1)

        def low_part(dve, name, f, w):
            r = resid(not wide(name))[f]
            dve.wait_ge(x_high, 8 * PREPS.index(name) + f + 1)
            hi, lo = parts_of(name)
            stt(lo[:, f, 0:w], r, prep_gain(name, f), hi[:, f, 0:w], ALU.mult, ALU.subtract).then_inc(x_low, 1)

        def token_tiles(w):
            n = (w + P - 1) // P
            return [(min(P * j, w - P), P * j, min(P, w - P * j)) for j in range(n)]

        def sums_pe(pe, name, w):
            k = SUMS.index(name)
            pe.wait_ge(added, 7 * (k + 1))
            for j, (t0, _, _) in enumerate(token_tiles(w)):
                last = mm(G[:, 5, j:j + 1], ACC[:, t0:t0 + P], ones[:, 0:1], start=True, stop=True)
            last.then_inc(summed_up, 1)

        def spread_pe(pe, name, w):
            pe.wait_ge(root_ready, SUMS.index(name) + 1)
            for j, (t0, t1, m) in enumerate(token_tiles(w)):
                last = mm(GF[:, 3072 + t1:3072 + t1 + m], RCOL[:, j:j + 1].broadcast_to([P, P]),
                          ident[:, t1 - t0:t1 - t0 + m], start=True, stop=True)
            last.then_inc(spread, 1)

        def root_act(act, name, w):
            act.wait_ge(mean_ready, SUMS.index(name) + 1)
            n = len(token_tiles(w))
            nc.scalar.activation(SCOL[:, 0:n], VCOL[:, 0:n], ACT.Sqrt).then_inc(dev_ready, 1)

        def root_dve(dve, name, w, scale=1.0):
            k, n = SUMS.index(name), len(token_tiles(w))
            dve.wait_ge(summed_up, k + 1)
            ts(VCOL[:, 0:n], G[:, 5, 0:n], 1.0 / (D * scale ** 2), EPS / scale ** 2, ALU.mult,
               ALU.add).then_inc(mean_ready, 1)
            dve.wait_ge(dev_ready, k + 1)
            nc.vector.reciprocal(RCOL[:, 0:n], SCOL[:, 0:n]).then_inc(root_ready, 1)

        def scale_act(act, name, w, func):
            act.wait_ge(spread, SUMS.index(name) + 1)
            nc.scalar.activation(RS[:, 0:w], GF[:, 3072:3072 + w], func).then_inc(scale_ready, 1)

        SCALES = ["mix0", "mlp0", "mix1", "mlp1"]

        WIDE_SUMS = ["f0", "even", "f1", "f2", "odd", "f3"]

        def first_tiles(pe, name, n, more=None):
            p = PREPS.index(name)
            pe.wait_ge(psum_free, n + 4)
            pe.wait_ge(low_ready, n + 2)
            w = width(n)
            hi, lo = parts_of(name)

            def passes(c, k):
                o = acc(n, c)
                parts = o.shape[1]
                for q, (wt, x) in enumerate(((WH, hi), (WH, lo), (WL, hi))):
                    for a in range(parts):
                        last = mm(o[:, a, :], wt[:, (n + c) % 2, k * P:k * P + P],
                                  x[:, k, a * (w // parts):(a + 1) * (w // parts)],
                                  start=(k == 0 and q == 0), stop=(k == DT - 1 and q == 2))
                if k == DT - 1:
                    last.then_inc(tile_done, 1)

            if is1(n):
                for k in range(DT):
                    pe.wait_ge(x_low, 8 * p + k + 1)
                    passes(0, k)
                if name == "mix0":
                    pe.wait_ge(const_loaded, CONST_LOADS)
                sums_pe(pe, name, w)
                for k in range(DT):
                    passes(1, k)
                    if k == DT // 2:
                        spread_pe(pe, name, w)
            else:
                for k in range(DT):
                    pe.wait_ge(x_low, 8 * p + k + 1)
                    passes(0, k)
                    passes(1, k)
                    pe.wait_ge(squared, SQUARES[name] + k + 1)
                    src = ACC if k == 0 else SQ[k % 2]
                    mm(G[:, 4, :], ones[:, :], src[:, 0:T2], start=(k == 0), stop=(k == DT - 1)).then_inc(wide_summed, 1)

        def first_act(act, name, n, func=ACT.Copy):
            if is1(n):
                root_act(act, name, T1)
                split_high(act, n + 2, 0, 0)
                scale_act(act, name, T1, func)
            else:
                split_high(act, n + 2, 0, 0)
                act.wait_ge(wide_mean, WIDE_SUMS.index(name) + 1)
                nc.scalar.activation(DEV, VAR, ACT.Sqrt).then_inc(wide_dev, 1)

        def first_dve(dve, name, n):
            if is1(n):
                root_dve(dve, name, T1)
                dve.wait_ge(scale_ready, SCALES.index(name) + 1)
            else:
                k = WIDE_SUMS.index(name)
                dve.wait_ge(wide_summed, 8 * (k + 1))
                ts(VAR, G[:, 4, :], 1.0 / D, EPS, ALU.mult, ALU.add).then_inc(wide_mean, 1)
                dve.wait_ge(wide_dev, k + 1)
                nc.vector.reciprocal(RS[:, 0:T2], DEV)
                dve.drain()

        def tail_act(act, n, name, src, w, high):
            for f in range(DT):
                if n + f + 2 < N_CHUNKS:
                    split_high(act, n + 2, f // 4, f % 4)
                act.wait_ge(final_tile, FINALS[name] + f + 1)
                if high:
                    high_part(act, name, f, w)
                if f > 2:
                    act.wait_ge(added, 7 * SUMS.index(name) + f - 2)
                square(act, name, f, src[f], w)

        def tail_dve(dve, n, name, w, finish, low):
            def rest(f):
                if low:
                    low_part(dve, name, f, w)
                if f:
                    add_square(dve, name, f, w)
            for f in range(DT):
                dve.wait_ge(tile_done, n + f + 1)
                finish(acc(n, f), f).then_inc(final_tile, 1)
                dve.drain()
                dve.sem_inc(psum_free, 1)
                if f:
                    rest(f - 1)
            rest(DT - 1)
            dve.drain()

        FINALS = {}
        for name in ("mlp0", "mix1", "mlp1", "final", "f0p", "evenp", "f1p", "f2p", "oddp", "f3p"):
            FINALS[name] = 8 * len(FINALS)

        AFTER = {"final": "f0", "f0p": "even", "evenp": "f1", "f1p": "f2", "f2p": "odd", "oddp": "f3"}
        UPDATES = list(AFTER) + ["f3p"]

        def post_pe(pe, name):
            sums_pe(pe, name, T2)
            spread_pe(pe, name, T2)

        def post_act(act, name):
            root_act(act, name, T2)
            if name in AFTER:
                nxt = AFTER[name]
                for f in range(DT):
                    act.wait_ge(updated, 8 * UPDATES.index(name) + f + 1)
                    high_part(act, nxt, f, T2)
                    if f > 2:
                        act.wait_ge(wide_summed, 8 * WIDE_SUMS.index(nxt) + f - 1)
                    square(act, nxt, f, resid(True)[f], T2)

        def post_dve(dve, name, g, scale, y=None):
            root_dve(dve, name, T2, scale)
            dve.wait_ge(spread, SUMS.index(name) + 1)
            r, ps = resid(True), GF[:, 3072:3072 + T2]
            if name == "final":
                for f in range(DT + 2):
                    if f < DT:
                        stt(r[f], r[f], g[f], ps, ALU.mult, ALU.mult).then_inc(updated, 1)
                    if f >= 2:
                        low_part(dve, AFTER[name], f - 2, T2)
            else:
                y = YF if y is None else y

                def term(f):
                    stt(SCR[:, 2 + f % 2, 0:T2], y[:, f, 0:T2], g[f], ps, ALU.mult, ALU.mult).then_inc(term_ready, 1)
                term(0)
                term(1)
                for f in range(DT):
                    if f + 2 < DT:
                        dve.wait_ge(updated, 8 * UPDATES.index(name) + f + 1)
                        term(f + 2)
                    if name in AFTER:
                        low_part(dve, AFTER[name], f, T2)
            dve.drain()

        def post_pool(pool, name):
            k, r = UPDATES.index(name), resid(True)
            for f in range(DT):
                pool.wait_ge(term_ready, 8 * (k - 1) + f + 1)
                nc.gpsimd.tensor_tensor(r[f], SCR[:, 2 + f % 2, 0:T2], r[f], ALU.add).then_inc(updated, 1)

        def heads_pe(pe, heads, size, base, bc, beside=None):
            tiles = token_tiles(T1)
            if beside:
                beside(0)
            for h in range(heads):
                pe.wait_ge(hn_sq, base + size * (h + 1))
                for j, (t0, _, _) in enumerate(tiles):
                    for e in range(size):
                        last = mm(G[:, 4, 5 * h + j:5 * h + j + 1], HSQ[(size * h + e) % 4][:, t0:t0 + P], ones[:, 0:1],
                                  start=(e == 0), stop=(e == size - 1))
                last.then_inc(hn_sum, 1)
            if beside:
                beside(1)
            pe.wait_ge(hn_rec, 1 if base == 0 else 2)
            for h in range(heads):
                if beside and h == heads // 2:
                    beside(2)
                if h >= 2:
                    pe.wait_ge(hn_used, bc + h - 1)
                for j, (t0, t1, m) in enumerate(tiles):
                    last = mm(GF[:, HB[h % 2] + t1:HB[h % 2] + t1 + m],
                              HCOL[:, 5 * h + j:5 * h + j + 1].broadcast_to([P, P]), ident[:, t1 - t0:t1 - t0 + m],
                              start=True, stop=True)
                last.then_inc(hn_bc, 1)
            if beside:
                beside(3)

        HB = (2048, 3072)

        def heads_act(act, name, src, heads, size, base, bc, hi, beside=None):
            for i in range(heads * size):
                if i >= 4:
                    act.wait_ge(hn_sum, bc + (i - 4) // size + 1)
                nc.scalar.activation(HSQ[i % 4], src[:, i, :], ACT.Square).then_inc(hn_sq, 1)
            if beside:
                beside(1)
            act.wait_ge(hn_var, 1 if base == 0 else 2)
            nc.scalar.activation(HDEV[:, 0:5 * heads], HVAR[:, 0:5 * heads], ACT.Sqrt).then_inc(hn_dev, 1)
            if not beside:
                split_act(act, name, [hi[:, i, :] for i in range(heads * size)], T1)
                return
            n = heads * size
            for k in range(2):
                beside(2 + k)
                split_act(act, name, [hi[:, i, :] for i in range(k * n // 2, (k + 1) * n // 2)], T1, k * n // 2)
            beside(4)

        def heads_dve(dve, name, src, heads, size, dims, g, base, bc, hi, lo, beside=None):
            if beside:
                beside(0)
            dve.wait_ge(hn_sum, bc + heads)
            ts(HVAR[:, 0:5 * heads], G[:, 4, 0:5 * heads], 1.0 / dims, EPS, ALU.mult, ALU.add).then_inc(hn_var, 1)
            dve.wait_ge(hn_dev, 1 if base == 0 else 2)
            nc.vector.reciprocal(HCOL[:, 0:5 * heads], HDEV[:, 0:5 * heads]).then_inc(hn_rec, 1)
            n = heads * size
            if beside:
                beside(1)

            def make(i):
                h = i // size
                if i % size == 0:
                    dve.wait_ge(hn_bc, bc + h + 1)
                last = stt(SCR[:, 2 + i % 2, :], src[:, i, :], g[i], GF[:, HB[h % 2]:HB[h % 2] + T1],
                           ALU.mult, ALU.mult).then_inc(h_ready, 1)
            make(0)
            for i in range(n):
                dve.drain()
                half = beside and i + 1 == n // 2
                if i + 1 < n and not half:
                    make(i + 1)
                dve.wait_ge(h_high, SPLIT_AT[name][0] + i + 1)
                last = tt(lo[:, i, :], SCR[:, 2 + i % 2, :], hi[:, i, :], ALU.subtract).then_inc(h_low, 1)
                if (i + 1) % size == 0:
                    dve.drain()
                    dve.sem_inc(hn_used, 1)
                if half:
                    beside(2)
                    make(i + 1)
            if beside:
                beside(3)
            dve.drain()

        NEXT = {"mlp0": "mix1", "mlp1": "final"}

        def mlp_pe(pe, l):
            first_tiles(pe, f"mlp{l}", CHUNKS[f"mlp{l}_up0"])
            for p, f in enumerate(FF1_PARTS):
                product(pe, CHUNKS[f"mlp{l}_up{p}"], f, XH, XL, start=0 if p else 2, follow=True)
                product(pe, CHUNKS[f"mlp{l}_down{p}"], 8, YH, YL, kt=f, parts=SPLIT_AT[f"mlp{l}_{p}"][0])

        def mlp_act(act, l):
            first_act(act, f"mlp{l}", CHUNKS[f"mlp{l}_up0"], ACT.Square)
            for p, f in enumerate(FF1_PARTS):
                n = CHUNKS[f"mlp{l}_up{p}"]

                def hidden(i, c):
                    act.wait_ge(psum_free, 4 * i + n + c + 1 + 4)
                    nc.scalar.activation(YH[:, 4 * i + c, :], SCR[:, 2 + c % 2, :], ACT.Square).then_inc(h_high, 1)

                def step(i, c):
                    split_high(act, n + 2, i, c)
                    hidden(i, c)
                if p == 0:
                    hidden(0, 0)
                fours(act, f, step, start=0 if p else 1)
                if p < len(FF1_PARTS) - 1:
                    act_idle(act, CHUNKS[f"mlp{l}_down{p}"], 8)
            nxt = NEXT[f"mlp{l}"]
            tail_act(act, CHUNKS[f"mlp{l}_down3"], nxt, *(([H[:, f, :] for f in range(DT)], T1, True) if l == 0 else
                                                          (resid(True), T2, False)))

        def mlp_dve(dve, l):
            first_dve(dve, f"mlp{l}", CHUNKS[f"mlp{l}_up0"])
            for p, f in enumerate(FF1_PARTS):
                n, s = CHUNKS[f"mlp{l}_up{p}"], SPLIT_AT[f"mlp{l}_{p}"][0]

                def step(i, c):
                    dve.wait_ge(tile_done, 4 * i + n + c + 1)
                    ps = acc(n, c)
                    ts(toks(SCR[:, 2 + c % 2, :], n), ps, 0.0, None, ALU.max).then_inc(psum_free, 1)
                    dve.drain()
                    tt(SCR[:, c % 2, :], SCR[:, 2 + c % 2, :], SCR[:, 2 + c % 2, :], ALU.mult)
                    dve.drain()
                    dve.wait_ge(h_high, 4 * i + s + c + 1)
                    tt(YL[:, 4 * i + c, :], SCR[:, c % 2, :], YH[:, 4 * i + c, :], ALU.subtract).then_inc(h_low, 1)
                fours(dve, f, step)
                if p < len(FF1_PARTS) - 1:
                    take_scaled_add(dve, CHUNKS[f"mlp{l}_down{p}"], 8, H, T1)
            n = CHUNKS[f"mlp{l}_down3"]

            def finish(ps, f):
                t = SCR[:, 4 + f % 2, :]
                tt(toks(t, n), ps, toks(RS[:, :], n), ALU.mult)
                dve.drain()
                return tt(H[:, f, :], H[:, f, :], t, ALU.add)
            tail_dve(dve, n, NEXT[f"mlp{l}"], T1 if l == 0 else T2, finish, l == 0)

        YF = area(0, 8)

        def ffn_pe(pe, i):
            first_tiles(pe, f"f{i}", CHUNKS[f"ffn{i}_up0"])
            for p, f in enumerate(FF2_PARTS):
                product(pe, CHUNKS[f"ffn{i}_up{p}"], 2 * f, XH, XL, start=0 if p else 2, follow=True)
                product(pe, CHUNKS[f"ffn{i}_down{p}"], 8, YH, YL, kt=f, parts=SPLIT_AT[f"ffn{i}_{p}"][0])
            post_pe(pe, f"f{i}p")

        def ffn_act(act, i):
            first_act(act, f"f{i}", CHUNKS[f"ffn{i}_up0"])
            for p, f in enumerate(FF2_PARTS):
                n = CHUNKS[f"ffn{i}_up{p}"]

                def work(j, c):
                    act.wait_ge(psum_free, 4 * j + n + c + 1 + 4)
                    if c % 2 == 0:
                        nc.scalar.activation(SCR[:, 2 + c // 2, 0:T2], SCR[:, 2 + c // 2, 0:T2],
                                             ACT.Silu).then_inc(silu_done, 1)
                    else:
                        nc.scalar.activation(YH[:, 2 * j + c // 2, 0:T2], SCR[:, c // 2, 0:T2],
                                             ACT.Copy).then_inc(h_high, 1)

                def step(j, c):
                    split_high(act, n + 2, j, c)
                    work(j, c)
                if p == 0:
                    work(0, 0)
                fours(act, 2 * f, step, start=0 if p else 1)
                if p < len(FF2_PARTS) - 1:
                    act_idle(act, CHUNKS[f"ffn{i}_down{p}"], 8)
            tail_act(act, CHUNKS[f"ffn{i}_down2"], f"f{i}p", [YF[:, f, 0:T2] for f in range(DT)], T2, False)
            post_act(act, f"f{i}p")

        def ffn_dve(dve, i):
            first_dve(dve, f"f{i}", CHUNKS[f"ffn{i}_up0"])
            for p, f in enumerate(FF2_PARTS):
                n, (s, _) = CHUNKS[f"ffn{i}_up{p}"], SPLIT_AT[f"ffn{i}_{p}"]
                u = i * sum(FF2_PARTS) + sum(FF2_PARTS[:p])

                def step(j, c):
                    if c % 2:
                        dve.wait_ge(silu_done, 2 * j + u + c // 2 + 1)
                    dve.wait_ge(tile_done, 4 * j + n + c + 1)
                    if c % 2 == 0:
                        tt(SCR[:, 2 + c // 2, 0:T2], acc(n, c)[:, 0, :], RS[:, 0:T2], ALU.mult).then_inc(psum_free, 1)
                        return
                    tt(SCR[:, c // 2, 0:T2], acc(n, c)[:, 0, :], SCR[:, 2 + c // 2, 0:T2],
                       ALU.mult).then_inc(psum_free, 1)
                    dve.drain()
                    dve.wait_ge(h_high, 2 * j + s + c // 2 + 1)
                    tt(YL[:, 2 * j + c // 2, 0:T2], SCR[:, c // 2, 0:T2], YH[:, 2 * j + c // 2, 0:T2],
                       ALU.subtract).then_inc(h_low, 1)
                fours(dve, 2 * f, step)
                if p == 0:
                    take_scaled(dve, CHUNKS[f"ffn{i}_down{p}"], 8, YF)
                elif p < len(FF2_PARTS) - 1:
                    take_scaled_add(dve, CHUNKS[f"ffn{i}_down{p}"], 8, YF, T2)

            def finish(ps, f):
                t = SCR[:, 4 + f % 2, 0:T2]
                tt(t, ps[:, 0, :], RS[:, 0:T2], ALU.mult)
                dve.drain()
                return tt(YF[:, f, 0:T2], YF[:, f, 0:T2], t, ALU.add)
            dve.drain()
            tail_dve(dve, CHUNKS[f"ffn{i}_down2"], f"f{i}p", T2, finish, False)
            post_dve(dve, f"f{i}p", gains("norm_w_2", FFN_NORM[i] + 1), 0.5)

        FFN_NORM = [0, 4, 6, 10]

        def log1p(dve, out, e, z, w):
            ts(z, e, 2.0, None, ALU.add)
            dve.drain()
            nc.vector.reciprocal(w, z)
            dve.drain()
            tt(z, e, w, ALU.mult)
            dve.drain()
            tt(w, z, z, ALU.mult)
            dve.drain()
            ts(out, w, 1.0 / 15, None, ALU.mult)
            dve.drain()
            for k in (13, 11, 9, 7, 5, 3):
                stt(out, out, 1.0 / k, w, ALU.add, ALU.mult)
                dve.drain()
            stt(out, out, 1.0, z, ALU.add, ALU.mult)
            dve.drain()
            ts(out, out, 2.0, None, ALU.mult)
            dve.drain()

        XB = AR[:, 0:DT * (T1 + 3)].rearrange("p (f t) -> p f t", t=T1 + 3)
        XC, GATE = area(9, 2), area(11, 8)
        LRU_W = AR[:, 19 * T1:19 * T1 + 16 * P].rearrange("p (f m) -> p f m", m=P)
        RG, IG, AE, TH, UU, VV = (area(23 + i, 1)[:, 0, :] for i in range(6))
        DECAY = SM[:, 0:8]
        MQ, MK = area(11, 8), area(0, 8)

        def lru_act(act):
            nc.scalar.activation(SM[:, 8:16], V[:, VEC["lam"]:VEC["lam"] + 8], ACT.Abs)
            act.drain()
            nc.scalar.activation(SM[:, 16:24], SM[:, 8:16], ACT.Exp, scale=-1.0).then_inc(st["lru_sp"], 1)
            act_idle(act, CHUNKS["xb"], 8, start=1)

            def step(i, c):
                split_high(act, CHUNKS["gate"] + 2, i, c)
                act.wait_ge(psum_free, 4 * i + CHUNKS["gate"] + c + 1 + 4)
                nc.scalar.activation(GATE[:, 4 * i + c, :], GATE[:, 4 * i + c, :],
                                     ACT.Gelu_apprx_tanh).then_inc(st["lru_ge"], 1)
            fours(act, 8, step)
            for f in range(DT):
                act.wait_ge(st["lru_ps"], f + 1)
                if f:
                    act.wait_ge(st["lru_h"], f)
                else:
                    act.wait_ge(st["lru_sp"], 2)
                nc.scalar.activation(RG, GF[:, 2048:2048 + T1], ACT.Sigmoid, bias=vec("b_r", f))
                nc.scalar.activation(IG, GF[:, 3072:3072 + T1], ACT.Sigmoid,
                                     bias=vec("b_i", f)).then_inc(st["lru_sg"], 1)
                act.drain()
                nc.scalar.activation(AE, RG, ACT.Exp, scale=DECAY[:, f:f + 1])
                nc.scalar.activation(TH, RG, ACT.Tanh, scale=DECAY[:, f:f + 1]).then_inc(st["lru_ex"], 1)
                split_high(act, CHUNKS["qk"] + 2, f // 2, 2 * (f % 2))
                act.wait_ge(st["lru_v"], f + 1)
                nc.scalar.activation(VV, UU, ACT.Sqrt, scale=-1.0).then_inc(st["lru_sq"], 1)
                act.wait_ge(h_ready, READY_AT["lru"] + f + 1)
                nc.scalar.activation(XH[:, f, :], SCR[:, 2 + f % 2, :], ACT.Copy).then_inc(h_high, 1)
                split_high(act, CHUNKS["qk"] + 2, f // 2, 2 * (f % 2) + 1)

        def lru_pe(pe):
            first_tiles(pe, "mix0", CHUNKS["xb"])
            product(pe, CHUNKS["xb"], 8, YH, YL, start=2)
            product(pe, CHUNKS["gate"], 8, YH, YL, follow=True)
            for f in range(DT):
                pe.wait_ge(st["lru_xc"], f + 1)
                if f:
                    pe.wait_ge(st["lru_sg"], f)
                last = None
                for g in range(2):
                    for a, b in pieces(0, T1):
                        last = mm(GF[:, 2048 + 1024 * g + a:2048 + 1024 * g + b], LRU_W[:, 8 * g + f, :],
                                  XC[:, f % 2, a:b], start=True, stop=True)
                last.then_inc(st["lru_ps"], 1)
                product(pe, CHUNKS["qk"] + 2 * f, 2, YH, YL, follow=True)

        def lru_dve(dve):
            nc.vector.memset(XB[:, :, 0:3], 0.0)
            take_scaled(dve, CHUNKS["xb"], 8, XB, offset=3)
            dve.wait_ge(st["lru_sp"], 1)
            dve.drain()
            log1p(dve, SM[:, 8:16], SM[:, 16:24], SM[:, 24:32], SM[:, 32:40])
            ts(SM[:, 24:32], V[:, VEC["lam"]:VEC["lam"] + 8], -1.0, 0.0, ALU.mult, ALU.max)
            dve.drain()
            tt(SM[:, 8:16], SM[:, 8:16], SM[:, 24:32], ALU.add)
            dve.drain()
            ts(DECAY, SM[:, 8:16], -LRU_C, None, ALU.mult).then_inc(st["lru_sp"], 1)
            take_scaled(dve, CHUNKS["gate"], 8, GATE)

            def conv(f):
                out = XC[:, f % 2, :]
                ts(out, XB[:, f, 0:T1], vec("conv_w", f), vec("conv_b", f), ALU.mult, ALU.add)
                for j in range(1, CONV1):
                    dve.drain()
                    last = stt(out, XB[:, f, j:j + T1], vec("conv_w", 8 * j + f), out, ALU.mult, ALU.add)
                last.then_inc(st["lru_xc"], 1)

            conv(0)
            for f in range(DT):
                dve.wait_ge(st["lru_ex"], f + 1)
                tt(UU, AE, AE, ALU.mult)
                dve.drain()
                stt(UU, UU, 1.0, TH, ALU.add, ALU.mult).then_inc(st["lru_v"], 1)
                tt(IG, IG, XC[:, f % 2, :], ALU.mult)
                if f + 1 < DT:
                    dve.drain()
                    conv(f + 1)
                dve.drain()
                dve.wait_ge(st["lru_sq"], f + 1)
                tt(VV, VV, IG, ALU.mult)
                dve.drain()
                nc.vector.tensor_tensor_scan(UU, AE, VV, 0.0, ALU.mult, ALU.add)
                dve.drain()
                if f == 0:
                    dve.wait_ge(st["lru_ge"], DT)
                tt(SCR[:, 2 + f % 2, :], UU, GATE[:, f, :], ALU.mult).then_inc(h_ready, 1)
                dve.drain()
                dve.wait_ge(h_high, SPLIT_AT["lru"][0] + f + 1)
                tt(XL[:, f, :], SCR[:, 2 + f % 2, :], XH[:, f, :], ALU.subtract).then_inc(h_low, 1)
                dve.drain()
                dve.sem_inc(st["lru_h"], 1)
                for c, dst in enumerate((MQ, MK)):
                    n = CHUNKS["qk"] + 2 * f + c
                    dve.wait_ge(tile_done, n + 1)
                    tt(toks(dst[:, f, :], n), acc(n, 0), toks(RS[:, :], n), ALU.mult).then_inc(psum_free, 1)

        def tail(j):
            return min(P, T1 - P * j)

        N_TT = (T1 + P - 1) // P
        QA, KA, VF = area(0, 8), area(8, 8), area(26, 8)
        VT = AR[:, 16 * T1:16 * T1 + N_TT * D].rearrange("p (j m) -> p j m", m=D)

        def vt_pe(pe, done, copied, n_end, v):
            pe.wait_ge(psum_free, n_end + 4)
            for f in range(DT):
                if f >= 2:
                    pe.wait_ge(copied, f - 1)
                bank = 2048 + 1024 * (f % 2)
                last = None
                for j in range(N_TT):
                    last = nc.tensor.transpose(GF[0:tail(j), bank + P * j:bank + P * j + P],
                                               v[:, f, P * j:P * j + tail(j)], ident[:, :])
                last.then_inc(done, 1)

        def vt_act(act, done, copied, vt, rest):
            for f in range(DT):
                bank = 2048 + 1024 * (f % 2)
                act.wait_ge(done, f + 1)
                nc.scalar.activation(vt[:, 0:4, P * f:P * f + P],
                                     GF[:, bank:bank + 512].rearrange("p (j m) -> p j m", m=P), ACT.Copy)
                nc.scalar.activation(rest[0:META, P * f:P * f + P], GF[0:META, bank + 512:bank + 640],
                                     ACT.Copy).then_inc(copied, 1)

        MV = area(27, 8)
        MVT = AR[:, 19 * T1:19 * T1 + 4 * D].rearrange("p (j m) -> p j m", m=D)
        MVT_REST = AR[:, 8 * T1:8 * T1 + D]
        GI, GX, RE, RZ, RW, RL, RB = (area(i, 1)[0:A_HEADS, 0, :] for i in (19, 20, 21, 22, 23, 10, 24))
        NMR, EMR = ACC[0:A_HEADS, :], area(33, 1)[0:A_HEADS, 0, :]
        NMB, EMB, DM, PM0, RC, PM1, RC2 = (area(i, 1)[:, 0, :] for i in (10, 27, 28, 29, 30, 31, 32))
        ACOL = SM[:, 0:20]

        def mlstm_pe(pe):
            for s, count in (("gi", 1), ("gf", 1), ("v", 8)):
                product(pe, CHUNKS[s], count, YH, YL, follow=True)
            pe.wait_ge(st["ml_m"], 1)
            pe.wait_ge(st["lru_sg"], DT)
            last = None
            for j in range(N_TT):
                last = nc.tensor.transpose(GF[0:tail(j), 2048 + 4 * j:2048 + 4 * j + 4],
                                           GI[:, P * j:P * j + tail(j)], ident[0:A_HEADS, 0:A_HEADS])
            last.then_inc(st["ml_tr"], 1)
            pe.wait_ge(st["ml_col"], 1)
            vt_pe(pe, st["ml_vt"], st["ml_vc"], CHUNKS["v"] + 8, MV)
            pe.wait_ge(st["ml_em"], 1)
            pe.wait_ge(st["ml_vc"], DT)
            for h in range(A_HEADS):
                if h:
                    pe.wait_ge(st["ml_sig"], h)
                last = None
                for row, bank in ((NMR, 0), (EMR, 1024)):
                    for a, b in pieces(0, T1):
                        last = mm(GF[:, bank + a:bank + b], ident[0:A_HEADS, h:h + 1].broadcast_to([A_HEADS, P]),
                                  row[:, a:b], start=True, stop=True)
                last.then_inc(st["ml_bc"], 1)
                for j in range(N_TT):
                    s, r = N_TT * h + j, tail(j)
                    if j == 0:
                        pe.wait_ge(st["ml_bcc"], h + 1)
                    else:
                        pe.wait_ge(st["ml_p"], s)
                    for a, b in pieces(P * j, T1):
                        for e in range(2):
                            last = mm(GF[0:r, a:b], MK[:, 2 * h + e, P * j:P * j + r], MQ[:, 2 * h + e, a:b],
                                      start=(e == 0), stop=(e == 1))
                    last.then_inc(st["ml_s"], 1)
                    pe.wait_ge(st["ml_p"], s + 1)
                    p = (PM0, PM1)[s % 2]
                    if h and j == 0:
                        pe.wait_ge(st["ml_h"], h)
                    for a, b in pieces(P * j, T1):
                        end = (3 if b <= 512 else 4)
                        for e in range(2):
                            v = MVT[:, j, :] if j < 4 else MVT_REST
                            mm(GF[:, 2048 + 1024 * e + a:2048 + 1024 * e + b],
                               v[0:r, (2 * h + e) * P:(2 * h + e + 1) * P], p[0:r, a:b],
                               start=(j == 0), stop=(j == end))
                        last = mm(GF[:, 1024 + a:1024 + b], ones[0:r, :], p[0:r, a:b],
                                  start=(j == 0), stop=(j == end))
                last.then_inc(st["ml_pv"], 1)
            pe.wait_ge(st["ml_h"], A_HEADS)
            product(pe, CHUNKS["o"], 8, YH, YL)
            heads_pe(pe, A_HEADS, 2, 0, 0,
                     lambda k: product(pe, CHUNKS["out_lru"] + 2 * k, 2, XH, XL, follow=k > 0))
            product(pe, CHUNKS["out_mlstm"], 8, YH, YL, parts=SPLIT_AT["mh"][0])

        def mlstm_act(act):
            act_idle(act, CHUNKS["gi"], 1)
            act_idle(act, CHUNKS["gf"], 1)
            act.wait_ge(psum_free, CHUNKS["gf"] + 1 + 4)
            nc.scalar.activation(RE, GX, ACT.Abs)
            act.drain()
            nc.scalar.activation(RE, RE, ACT.Exp, scale=-1.0).then_inc(st["ml_abs"], 1)
            act_idle(act, CHUNKS["v"], 8)
            vt_act(act, st["ml_vt"], st["ml_vc"], MVT, MVT_REST)
            act.wait_ge(st["ml_m"], 1)
            nc.scalar.activation(EMR, RL, ACT.Exp).then_inc(st["ml_em"], 1)
            for h in range(A_HEADS):
                act.wait_ge(st["ml_bc"], h + 1)
                nc.scalar.activation(NMB, GF[:, 0:T1], ACT.Copy)
                if h:
                    act.wait_ge(st["ml_rc"], h)
                nc.scalar.activation(EMB, GF[:, 1024:1024 + T1], ACT.Copy).then_inc(st["ml_bcc"], 1)
                act.drain()
                for j in range(N_TT):
                    s, r, c0 = N_TT * h + j, tail(j), P * j
                    a = ACOL[0:r, 4 * j + h:4 * j + h + 1]
                    act.wait_ge(st["ml_dg"], s + 1)
                    if c0 + r < T1:
                        nc.scalar.activation(DM[0:r, c0 + r:T1], NMB[0:r, c0 + r:T1], ACT.Exp, bias=a)
                    nc.scalar.activation(DM[0:r, c0:c0 + r], DM[0:r, c0:c0 + r], ACT.Exp).then_inc(st["ml_d"], 1)
                act.wait_ge(st["ml_pv"], h + 1)
                nc.scalar.activation(RC, GF[:, 1024:1024 + T1], ACT.Abs).then_inc(st["ml_sig"], 1)

            def step(i, c):
                split_high(act, CHUNKS["o"] + 2, i, c)
                act.wait_ge(psum_free, 4 * i + CHUNKS["o"] + c + 1 + 4)
                nc.scalar.activation(MK[:, 4 * i + c, :], MK[:, 4 * i + c, :], ACT.Sigmoid).then_inc(st["ml_og"], 1)
            fours(act, 8, step)
            act.wait_ge(st["ml_gate"], 1)
            heads_act(act, "mh", MQ, A_HEADS, 2, 0, 0, YH,
                      lambda k: act_idle(act, CHUNKS["out_lru"] + 2 * k - 2, 2))
            tail_act(act, CHUNKS["out_mlstm"], "mlp0", [H[:, f, :] for f in range(DT)], T1, True)

        def mlstm_dve(dve):
            for s, row, bias in (("gi", GI, "i_bias"), ("gf", GX, "f_bias")):
                dve.wait_ge(tile_done, CHUNKS[s] + 1)
                tt(toks(row, 0), acc(CHUNKS[s], 0)[0:A_HEADS, :, :], toks(RS[0:A_HEADS, :], 0), ALU.mult)
                dve.drain()
                ts(row, row, vec(bias, 0, A_HEADS), None, ALU.add).then_inc(psum_free, 1)
            dve.wait_ge(st["ml_abs"], 1)
            dve.drain()
            log1p(dve, RL, RE, RZ, RW)
            take_scaled(dve, CHUNKS["v"], 2, MV)
            stt(RL, GX, 0.0, RL, ALU.min, ALU.subtract)
            dve.drain()
            nc.vector.tensor_tensor_scan(RB, ones[0:A_HEADS, 0:1].broadcast_to([A_HEADS, T1]), RL, 0.0,
                                         ALU.mult, ALU.add)
            dve.drain()
            tt(GI, GI, RB, ALU.subtract)
            dve.drain()
            nc.vector.tensor_tensor_scan(RE, GI, GI, 0.0, ALU.max, ALU.max)
            dve.drain()
            tt(RL, RB, RE, ALU.add)
            ts(NMR, RE, -1.0, None, ALU.mult)
            dve.drain()
            ts(RL, RL, -1.0, 88.0, ALU.mult, ALU.min).then_inc(st["ml_m"], 1)
            take_scaled(dve, CHUNKS["v"] + 2, 6, MV[:, 2:8, :])
            dve.wait_ge(st["ml_tr"], 1)
            nc.vector.tensor_copy(ACOL[:, 0:16], GF[:, 2048:2064])
            nc.vector.tensor_copy(ACOL[0:META, 16:20], GF[0:META, 2064:2068]).then_inc(st["ml_col"], 1)
            for h in range(A_HEADS):
                dve.wait_ge(st["ml_bcc"], h + 1)
                for j in range(N_TT):
                    s, r, c0 = N_TT * h + j, tail(j), P * j
                    dve.drain()
                    stt(DM[0:r, c0:c0 + r], NMB[0:r, c0:c0 + r], ACOL[0:r, 4 * j + h:4 * j + h + 1],
                        mask_ge[0:r, 0:r], ALU.add, ALU.add).then_inc(st["ml_dg"], 1)
                    dve.wait_ge(st["ml_d"], s + 1)
                    dve.wait_ge(st["ml_s"], s + 1)
                    stt((PM0, PM1)[s % 2][0:r, c0:T1], GF[0:r, c0:T1], A_DIM ** -0.5, DM[0:r, c0:T1],
                        ALU.mult, ALU.mult).then_inc(st["ml_p"], 1)
                dve.wait_ge(st["ml_sig"], h + 1)
                tt(RC, RC, EMB, ALU.max).then_inc(st["ml_rc"], 1)
                dve.drain()
                nc.vector.reciprocal(RC2, RC)
                dve.drain()
                for e in range(2):
                    last = tt(MQ[:, 2 * h + e, :], GF[:, 2048 + 1024 * e:2048 + 1024 * e + T1], RC2, ALU.mult)
                last.then_inc(st["ml_h"], 1)
            take_scaled(dve, CHUNKS["o"], 8, MK)
            dve.drain()
            dve.wait_ge(st["ml_og"], DT)
            for f in range(DT):
                last = tt(MQ[:, f, :], MQ[:, f, :], MK[:, f, :], ALU.mult)
            last.then_inc(st["ml_gate"], 1)
            heads_dve(dve, "mh", MQ, A_HEADS, 2, A_DIM, gains("mlstm_norm", 0), 0, 0, YH, YL,
                      lambda k: take_add(dve, CHUNKS["out_lru"] + 2 * k, 2, H[:, 2 * k:2 * k + 2, :]))
            n = CHUNKS["out_mlstm"]
            dve.drain()
            tail_dve(dve, n, "mlp0", T1, lambda ps, f: tt(toks(H[:, f, :], n), ps, toks(H[:, f, :], n), ALU.add), True)

        P0, P1 = (area(26 + i, 1)[:, 0, :] for i in range(2))
        PT = AR[:, 28 * T1:28 * T1 + N_TT * P].rearrange("p (j m) -> p j m", m=P)
        ROT_W = [area(26 + i, 1)[:, 0, :] for i in range(2)]
        LAM, GAIN_C, MX, NEGM, SUM, RSUM = (SM[:, a:b] for a, b in ((40, 41), (41, 42), (42, 44), (44, 46),
                                                                   (46, 48), (48, 50)))

        def diff_steps():
            return [(h, i) for h in range(C_HEADS) for i in range(N_TT)]

        def diff_pe(pe):
            first_tiles(pe, "mix1", CHUNKS["cq"])
            for s in ("cq", "ck", "cv"):
                product(pe, CHUNKS[s], 8, XH, XL, start=2 if s == "cq" else 0, follow=True)
            vt_pe(pe, st["c_vt"], st["c_vc"], CHUNKS["cv"] + 8, VF)
            for f in range(2 * DT):
                if f >= 2:
                    pe.wait_ge(st["c_rope"], f - 1)
                src = (QA, KA)[f // DT]
                last = None
                for a, b in pieces(0, T1):
                    last = mm(GF[:, 1024 * (f % 2) + a:1024 * (f % 2) + b], rot1, src[:, f % DT, a:b],
                              start=True, stop=True)
                last.then_inc(st["c_rot"], 1)
            pe.wait_ge(st["c_rope"], 2 * DT)
            pe.wait_ge(st["c_vc"], DT)
            steps = diff_steps()

            def scores(n):
                h, i = steps[n]
                r, w, t0 = tail(i), min(T1, P * i + P), P * i
                if n:
                    pe.wait_ge(st["c_e"], n)
                last = None
                for c in range(2):
                    rows = slice(C_QK * c, C_QK * c + C_QK)
                    for a, b in pieces(0, w):
                        diag = a <= t0 < b
                        last = mm(GF[0:r, 1024 * c + a:1024 * c + b], QA[rows, h, t0:t0 + r], KA[rows, h, a:b],
                                  start=True, stop=not diag)
                        if diag:
                            last = mm(GF[0:r, 1024 * c + t0:1024 * c + t0 + r], ident[:, 0:r], mask_le[:, 0:r],
                                      start=False, stop=True)
                last.then_inc(st["c_s"], 1)

            scores(0)
            for n, (h, i) in enumerate(steps):
                r, t0 = tail(i), P * i
                if n + 1 < len(steps):
                    scores(n + 1)
                pe.wait_ge(st["c_pd"], n + 1)
                if n:
                    pe.wait_ge(st["c_ptc"], n)
                last = None
                for b in range(i + 1):
                    kb = tail(b)
                    last = nc.tensor.transpose(GF[0:kb, 2048 + P * b:2048 + P * b + r], P0[0:r, P * b:P * b + kb],
                                               ident[0:r, 0:r])
                last.then_inc(st["c_pt"], 1)
                pe.wait_ge(st["c_ptc"], n + 1)
                if i == 0 and h:
                    pe.wait_ge(st["c_o"], h)
                for b in range(i + 1):
                    kb = tail(b)
                    last = mm(GF[:, 3072 + t0:3072 + t0 + r], VT[0:kb, b, P * h:P * h + P], PT[0:kb, b, 0:r],
                              start=(b == 0), stop=(b == i))
                last.then_inc(st["c_pv"], 1)
            heads_pe(pe, C_HEADS, 1, 8, A_HEADS)
            product(pe, CHUNKS["c_out"], 8, YH, YL, parts=SPLIT_AT["ch"][0])

        def diff_act(act):
            first_act(act, "mix1", CHUNKS["cq"])
            for s in ("cq", "ck", "cv"):
                act_idle(act, CHUNKS[s], 8, start=1 if s == "cq" else 0)
            vt_act(act, st["c_vt"], st["c_vc"], VT, VT[:, 4, :])
            act.wait_ge(st["c_lam"], 1)
            nc.scalar.activation(SM[:, 52:54], SM[:, 50:52], ACT.Exp).then_inc(st["c_lex"], 1)
            for n, (h, i) in enumerate(diff_steps()):
                r, w = tail(i), min(T1, P * i + P)
                act.wait_ge(st["c_mx"], n + 1)
                if n:
                    act.wait_ge(st["c_pt"], n)
                nc.scalar.activation(P0[0:r, 0:w], GF[0:r, 0:w], ACT.Exp, bias=NEGM[0:r, 0:1], scale=C_QK ** -0.5,
                                     accum_out=SUM[0:r, 0:1])
                nc.scalar.activation(P1[0:r, 0:w], GF[0:r, 1024:1024 + w], ACT.Exp, bias=NEGM[0:r, 1:2],
                                     scale=C_QK ** -0.5, accum_out=SUM[0:r, 1:2]).then_inc(st["c_e"], 1)
                act.wait_ge(st["c_pt"], n + 1)
                if n:
                    act.wait_ge(st["c_pv"], n)
                nb = min(i + 1, 4)
                last = nc.scalar.activation(PT[:, 0:nb, 0:r],
                                            GF[:, 2048:2048 + P * nb].rearrange("p (j m) -> p j m", m=P)[:, :, 0:r],
                                            ACT.Copy)
                if i == 4:
                    last = nc.scalar.activation(PT[0:META, 4, 0:r], GF[0:META, 2560:2560 + r], ACT.Copy)
                last.then_inc(st["c_ptc"], 1)
            act.wait_ge(st["c_o"], C_HEADS)
            heads_act(act, "ch", QA, C_HEADS, 1, 8, A_HEADS, YH)
            tail_act(act, CHUNKS["c_out"], "mlp1", [H[:, f, :] for f in range(DT)], T1, True)

        def diff_dve(dve):
            first_dve(dve, "mix1", CHUNKS["cq"])
            cl = V[:, VEC["c_lambda"]:VEC["c_lambda"] + 256].rearrange("p (a b m) -> p a b m", a=2, b=2)
            lp = SCR[:, 2, 0:128].rearrange("p (a m) -> p a m", a=2)
            tt(lp, cl[:, :, 0, :], cl[:, :, 1, :], ALU.mult)
            dve.drain()
            nc.vector.reduce_sum(SM[:, 50:52], lp, AX.X).then_inc(st["c_lam"], 1)
            for s, dst in (("cq", QA), ("ck", KA), ("cv", VF)):
                take_scaled(dve, CHUNKS[s], 8, dst)
            dve.wait_ge(st["c_lex"], 1)
            tt(LAM, SM[:, 53:54], SM[:, 52:53], ALU.subtract)
            dve.drain()
            ts(LAM, LAM, -LAMBDA_INIT, None, ALU.add)
            ts(GAIN_C, vec("subln"), 1.0 - LAMBDA_INIT, None, ALU.mult)
            dve.wait_ge(st["c_vc"], DT)
            for f in range(2 * DT):
                src = (QA, KA)[f // DT][:, f % DT, :]
                tt(ROT_W[0], src, ROPE[:, 0, :], ALU.mult)
                dve.wait_ge(st["c_rot"], f + 1)
                tt(ROT_W[1], GF[:, 1024 * (f % 2):1024 * (f % 2) + T1], ROPE[:, 1, :], ALU.mult)
                dve.drain()
                tt(src, ROT_W[0], ROT_W[1], ALU.add).then_inc(st["c_rope"], 1)
                dve.drain()

            def head_out(h):
                dve.wait_ge(st["c_pv"], N_TT * (h + 1))
                nc.vector.tensor_copy(QA[:, h, :], GF[:, 3072:3072 + T1]).then_inc(st["c_o"], 1)
            for n, (h, i) in enumerate(diff_steps()):
                r, w = tail(i), min(T1, P * i + P)
                dve.wait_ge(st["c_s"], n + 1)
                for c in range(2):
                    nc.vector.reduce_max(MX[0:r, c:c + 1], GF[0:r, 1024 * c:1024 * c + w], AX.X)
                dve.drain()
                ts(NEGM[0:r, :], MX[0:r, :], -(C_QK ** -0.5), None, ALU.mult).then_inc(st["c_mx"], 1)
                dve.wait_ge(st["c_e"], n + 1)
                nc.vector.reciprocal(RSUM[0:r, :], SUM[0:r, :])
                dve.drain()
                ts(RSUM[0:r, 1:2], RSUM[0:r, 1:2], LAM[0:r, :], None, ALU.mult)
                dve.drain()
                ts(P1[0:r, 0:w], P1[0:r, 0:w], RSUM[0:r, 1:2], None, ALU.mult)
                dve.drain()
                stt(P0[0:r, 0:w], P0[0:r, 0:w], RSUM[0:r, 0:1], P1[0:r, 0:w], ALU.mult,
                    ALU.add).then_inc(st["c_pd"], 1)
                if i == 0 and h:
                    head_out(h - 1)
                dve.drain()
            head_out(C_HEADS - 1)
            dve.drain()
            heads_dve(dve, "ch", QA, C_HEADS, 1, C_V, [GAIN_C] * C_HEADS, 8, A_HEADS, YH, YL)
            n = CHUNKS["c_out"]
            dve.drain()
            tail_dve(dve, n, "mlp1", T1, lambda ps, f: tt(toks(H[:, f, :], n), ps, toks(H[:, f, :], n), ALU.add), True)

        def final_act(act):
            post_act(act, "final")

        def final_dve(dve):
            post_dve(dve, "final", gains("norm_final", 0), 1.0)

        EU, EQ, EK, EV, KD = area(0, 2), area(2, 6), area(8, 2), area(10, 2), area(12, 4)
        EVT = AR[:, 16 * T1:16 * T1 + 4 * 256].rearrange("p (j m) -> p j m", m=256)
        EW = [area(18 + i, 1)[:, 0, :] for i in range(2)]
        INV = AR[:, 20 * T1:20 * T1 + 2 * T2].rearrange("p (f t) -> p f t", t=T2)
        PP = area(22, 2)
        EPT = AR[:, 24 * T1:24 * T1 + 10 * P].rearrange("p (j m) -> p j m", m=P)
        EPM = AR[:, 27 * T1:27 * T1 + 4 * 384].rearrange("p (j m) -> p j m", m=384)
        EW2 = [area(24 + i, 1)[:, 0, :] for i in range(2)]
        EMX, ENM, ESUM, ESK, ERS = (SM[:, a:a + 4] for a in (0, 4, 8, 12, 16))
        NB = T2 // P

        def band(n):
            return max(0, n - 1), min(NB - 1, n + 1)

        E_BLOCKS = [(n, b) for n in range(NB) for b in range(band(n)[0], band(n)[1] + 1)]

        def even_pe(pe):
            first_tiles(pe, "even", CHUNKS["eu"])
            for s, m in (("eq", 6), ("ek", 2), ("ev", 2)):
                product(pe, CHUNKS[s], m, XH, XL, follow=True)
            pe.wait_ge(psum_free, CHUNKS["e_out"] + 4)
            for f in range(2):
                last = None
                for j in range(NB):
                    last = nc.tensor.transpose(G[:, 4 + f, P * j:P * j + P], EV[:, f, P * j:P * j + P], ident[:, :])
                last.then_inc(st["e_vt"], 1)
            for f in range(10):
                if f >= 2:
                    pe.wait_ge(st["e_rope"], f - 1)
                bank = 2 * (f % 2)
                if f < 6:
                    last = mm(G[:, bank + 1, :], rot2, EQ[:, f, 0:T2], start=True, stop=True)
                else:
                    kv = f - 6
                    mm(G[:, bank, :], dup[kv % 2], EK[:, kv // 2, 0:T2], start=True, stop=True)
                    last = mm(G[:, bank + 1, :], rot_dup[kv % 2], EK[:, kv // 2, 0:T2], start=True, stop=True)
                last.then_inc(st["e_rot"], 1)
            pe.wait_ge(st["e_pool"], 1)
            for f in range(2):
                last = mm(G[:, 6 + f, :], PW[:, f, :], PP[:, f, 0:T2], start=True, stop=True)
            last.then_inc(st["e_pm"], 1)
            pe.wait_ge(st["e_rope"], 10)
            pe.wait_ge(st["e_vc"], 2)
            pe.wait_ge(h_low, split_end("e_pool"))

            def scores(h):
                rows = slice(HD * (h % 2), HD * (h % 2) + HD)
                if h:
                    pe.wait_ge(st["e_e"], h)
                last = None
                for n in range(NB):
                    b0, b1 = band(n)
                    w = P * (b1 - b0 + 1)
                    mm(G[:, n, 0:w], EQ[rows, h // 2, P * n:P * n + P], KD[rows, h // GROUP, P * b0:P * b1 + P],
                       start=True, stop=False)
                    if n > 0:
                        last = mm(G[:, n, 0:P], ident[:, :], mask_ge, start=False, stop=(n == NB - 1))
                    if n < NB - 1:
                        last = mm(G[:, n, w - P:w], ident[:, :], mask_le, start=False, stop=True)
                last.then_inc(st["e_s"], 1)

            scores(0)
            for h in range(Q_HEADS):
                if h + 1 < Q_HEADS:
                    scores(h + 1)
                pe.wait_ge(st["e_p"], h + 1)
                if h:
                    pe.wait_ge(st["e_ptc"], h)
                last = None
                for t, (n, b) in enumerate(E_BLOCKS):
                    last = nc.tensor.transpose(GF[:, 2048 + P * t:2048 + P * t + P],
                                               EPM[:, n, P * (b - band(n)[0]):P * (b - band(n)[0]) + P], ident[:, :])
                last.then_inc(st["e_pt"], 1)
                pe.wait_ge(st["e_ptc"], h + 1)
                if h % 2 == 0 and h:
                    pe.wait_ge(h_low, SPLIT_AT["e_attn"][0] + h // 2)
                rows = slice(HD * (h % 2), HD * (h % 2) + HD)
                for t, (n, b) in enumerate(E_BLOCKS):
                    last = mm(G[rows, 7, P * n:P * n + P], EVT[:, b, HD * (h // GROUP):HD * (h // GROUP) + HD],
                              EPT[:, t, :], start=(b == band(n)[0]), stop=(b == band(n)[1]))
                last.then_inc(st["e_pv"], 1)
            product(pe, CHUNKS["e_out"], 8, YH, YL, parts=SPLIT_AT["e_pool"][0])
            post_pe(pe, "evenp")

        def even_act(act):
            first_act(act, "even", CHUNKS["eu"])
            act.dma_start(INV, pool_inv).then_inc(st["inv_loaded"], 16)
            act.dma_start(ROPE[:, :, 0:T2], rope2).then_inc(st["inv_loaded"], 16)
            for s, m in (("eu", 2), ("eq", 6), ("ek", 2), ("ev", 2)):
                act_idle(act, CHUNKS[s], m, start=1 if s == "eu" else 0)
            for f in range(2):
                act.wait_ge(st["e_vt"], f + 1)
                nc.scalar.activation(EVT[:, :, P * f:P * f + P],
                                     G[:, 4 + f, :].rearrange("p (j m) -> p j m", m=P), ACT.Copy).then_inc(st["e_vc"], 1)
            split_act(act, "e_pool", [YH[:, f, 0:T2] for f in range(2)], T2)

            def pair_high(p):
                act.wait_ge(st["e_pv"], 2 * p + 2)
                nc.scalar.activation(YH[:, 2 + p, 0:T2], G[:, 7, :], ACT.Copy).then_inc(h_high, 1)
            for h in range(Q_HEADS):
                act.wait_ge(st["e_mx"], h + 1)
                if h:
                    act.wait_ge(st["e_pt"], h)
                for n in range(NB):
                    w = P * (band(n)[1] - band(n)[0] + 1)
                    nc.scalar.activation(EPM[:, n, 0:w], G[:, n, 0:w], ACT.Exp, bias=ENM[:, n:n + 1],
                                         scale=HD ** -0.5, accum_out=ESUM[:, n:n + 1])
                nc.scalar.activation(ESK, ENM, ACT.Exp, bias=vec("sink", h)).then_inc(st["e_e"], 1)
                if h and h % 2 == 0:
                    pair_high(h // 2 - 1)
                act.wait_ge(st["e_pt"], h + 1)
                if h:
                    act.wait_ge(st["e_pv"], h)
                nc.scalar.activation(EPT[:, :, :], GF[:, 2048:2048 + 10 * P].rearrange("p (j m) -> p j m", m=P),
                                     ACT.Copy).then_inc(st["e_ptc"], 1)
            pair_high(Q_HEADS // 2 - 1)
            tail_act(act, CHUNKS["e_out"], "evenp", [YF[:, f, 0:T2] for f in range(DT)], T2, False)
            post_act(act, "evenp")

        def even_pool(pool):
            gt = nc.gpsimd.tensor_tensor
            pool.wait_ge(psum_free, CHUNKS["eq"] + 4)
            pool.wait_ge(st["inv_loaded"], 32)
            for f in range(2):
                u, a, b = EU[:, f, :], EW[0], EW[1]
                gt(a[:, 1:T1], u[:, 0:T1 - 1], u[:, 1:T1], ALU.add)
                pool.drain()
                gt(b[:, 2:T1 - 1], a[:, 1:T1 - 2], a[:, 3:T1], ALU.add)
                pool.drain()
                if f:
                    a2, b2 = EW2
                    gt(a2[:, 4:T1 - 3], b[:, 2:T1 - 5], b[:, 6:T1 - 1], ALU.add)
                    pool.drain()
                    gt(b2[:, 8:T1 - 7], a2[:, 4:T1 - 11], a2[:, 12:T1 - 3], ALU.add)
                    pool.drain()
                    a, b = a2, b2
                for rows, s in ((slice(0, 64), a), (slice(64, P), b)):
                    gt(PP[rows, f, 0:T2], s[rows, 8:8 + T2], INV[rows, f, :], ALU.mult)
                pool.drain()
                last = gt(PP[:, f, 0:T2], PP[:, f, 0:T2], u[:, 8:8 + T2], ALU.subtract)
            last.then_inc(st["e_pool"], 1)

        def even_dve(dve):
            first_dve(dve, "even", CHUNKS["eu"])
            nc.vector.memset(EU[:, :, 0:8], 0.0)
            nc.vector.memset(EU[:, :, 8 + T2:16 + T2], 0.0)
            take_scaled(dve, CHUNKS["eu"], 2, EU, offset=8)
            take_scaled(dve, CHUNKS["eq"], 6, EQ)
            take_scaled(dve, CHUNKS["ek"], 2, EK)
            take_scaled(dve, CHUNKS["ev"], 2, EV)
            dve.wait_ge(st["inv_loaded"], 32)
            dve.drain()
            for f in range(10):
                bank = 2 * (f % 2)
                dve.wait_ge(st["e_rot"], f + 1)
                dve.drain()
                dst = EQ[:, f, 0:T2] if f < 6 else KD[:, f - 6, 0:T2]
                tt(SCR[:, 4, 0:T2], EQ[:, f, 0:T2] if f < 6 else G[:, bank, :], ROPE[:, 0, 0:T2], ALU.mult)
                tt(SCR[:, 5, 0:T2], G[:, bank + 1, :], ROPE[:, 1, 0:T2], ALU.mult)
                dve.drain()
                tt(dst, SCR[:, 4, 0:T2], SCR[:, 5, 0:T2], ALU.add).then_inc(st["e_rope"], 1)
            dve.wait_ge(st["e_pm"], 1)
            for f in range(2):
                ts(SCR[:, 2 + f, 0:T2], G[:, 6 + f, :], vec("pool_scale", f), None, ALU.mult).then_inc(h_ready, 1)
            dve.drain()
            for f in range(2):
                dve.wait_ge(h_high, SPLIT_AT["e_pool"][0] + f + 1)
                tt(YL[:, f, 0:T2], SCR[:, 2 + f, 0:T2], YH[:, f, 0:T2], ALU.subtract).then_inc(h_low, 1)

            def pair_low(p):
                dve.wait_ge(h_high, SPLIT_AT["e_attn"][0] + p + 1)
                tt(YL[:, 2 + p, 0:T2], G[:, 7, :], YH[:, 2 + p, 0:T2], ALU.subtract).then_inc(h_low, 1)
            for h in range(Q_HEADS):
                dve.wait_ge(st["e_s"], h + 1)
                dve.drain()
                for n in range(NB):
                    w = P * (band(n)[1] - band(n)[0] + 1)
                    nc.vector.reduce_max(EMX[:, n:n + 1], G[:, n, 0:w], AX.X)
                dve.drain()
                ts(EMX, EMX, HD ** -0.5, vec("sink", h), ALU.mult, ALU.max)
                dve.drain()
                ts(ENM, EMX, -1.0, None, ALU.mult).then_inc(st["e_mx"], 1)
                dve.wait_ge(st["e_e"], h + 1)
                tt(ERS, ESUM, ESK, ALU.add)
                dve.drain()
                nc.vector.reciprocal(EMX, ERS)
                dve.drain()
                for n in range(NB):
                    w = P * (band(n)[1] - band(n)[0] + 1)
                    last = ts(EPM[:, n, 0:w], EPM[:, n, 0:w], EMX[:, n:n + 1], None, ALU.mult)
                last.then_inc(st["e_p"], 1)
                if h and h % 2 == 0:
                    pair_low(h // 2 - 1)
            pair_low(Q_HEADS // 2 - 1)
            dve.drain()
            tail_dve(dve, CHUNKS["e_out"], "evenp", T2,
                     lambda ps, f: nc.vector.tensor_copy(YF[:, f, 0:T2], ps[:, 0, :]), False)
            post_dve(dve, "evenp", gains("norm_w_2", 3), 1.0)

        XBC = area(0, 16)
        XST = AR[:, 16 * T1:16 * T1 + 4 * D].rearrange("p (j m) -> p j m", m=D)
        DTR, SR, ER, OA, OZ, OW = (area(i, 1)[0:32, 0, 0:T2] for i in (24, 25, 26, 31, 32, 33))
        COLS = AR[:, 30 * T1:30 * T1 + 512]
        STG, CV = area(31, 2), area(33, 2)
        OWT = [area(27 + i, 1)[:, 0, 0:T2] for i in range(2)]
        OM = [area(29, 1)[:, 0, 0:T2], area(31, 1)[:, 0, 0:T2]]
        OWD = AR[:, 32 * T1:32 * T1 + 512].rearrange("p (s m) -> p s m", s=2)
        SZ = area(16, 8)
        GP = AR[:, 16 * T1:16 * T1 + 4 * (T2 + CONV_K - 1)].rearrange("p (f t) -> p f t", t=T2 + CONV_K - 1)
        GA, SB_ = area(0, 4), area(4, 4)
        CO = [area(i, 1)[:, 0, 0:T2] for i in (21, 22, 23, 27)]
        MU = area(28, 1)[:, 0, 0:T2]
        YO = area(8, 8)

        TAP = [area(29, 1)[:, 0, 0:T2], area(30, 1)[:, 0, 0:T2], ROPE[:, 0, 0:T2], ROPE[:, 1, 0:T2]]

        def tap(f, j):
            return GP[:, f, bass.ds(j, T2)], V[:, bass.ds(VEC["dw_w"] + f + 4 * j, 1)]
        AEXP = SM[0:32, 0:1]
        FE = [AR[:, 33 * T1:33 * T1 + 2 * T2].rearrange("p (a t) -> p a t", a=2), ROPE[:, :, 0:T2]]

        def odd_pe(pe):
            first_tiles(pe, "odd", CHUNKS["ga"])
            product(pe, CHUNKS["ga"], 4, XH, XL, start=2)
            product(pe, CHUNKS["gb"], 4, XH, XL, follow=True)
            product(pe, CHUNKS["dt"], 1, XH, XL, follow=True)
            product(pe, CHUNKS["xbc"], 16, XH, XL, follow=True)
            pe.wait_ge(st["o_gc"], 2)
            for f in range(4):
                last = mm(G[:, 6, :], ones[:, :], CO[f], start=(f == 0), stop=(f == 3))
            last.then_inc(st["o_mu"], 1)
            norm_pe(pe, "ln", T2)
            pe.wait_ge(var_in, 1)
            pe.wait_ge(st["o_dt"], 2)
            last = None
            for i, row in enumerate((SR, ER, DTR)):
                for j in range(NB):
                    last = nc.tensor.transpose(G[:, 4, 128 * i + 32 * j:128 * i + 32 * j + 32],
                                               row[:, P * j:P * j + P], ident[0:32, 0:32])
            last.then_inc(st["o_tr"], 1)
            pe.wait_ge(st["o_si"], 16 + 1)
            for f in range(DT):
                bank = 5 + f % 2
                if f >= 2:
                    pe.wait_ge(st["o_xc"], f - 1)
                for j in range(NB):
                    last = nc.tensor.transpose(G[:, bank, P * j:P * j + P], XBC[:, f, P * j:P * j + P], ident[:, :])
                last.then_inc(st["o_xt"], 1)
            pe.wait_ge(st["o_xc"], DT)
            pe.wait_ge(st["o_col"], 1)

            def broadcast(h):
                if h:
                    pe.wait_ge(st["o_fe"], h)
                mm(G[:, 4, :], ident[0:32, h:h + 1].broadcast_to([32, P]), SR, start=True, stop=True)
                mm(G[:, 5, :], ident[0:32, 16 + h:17 + h].broadcast_to([32, P]), ER, start=True,
                   stop=True).then_inc(st["o_bc"], 1)

            for h in range(SSM_HEADS):
                g = h // (SSM_HEADS // SSM_GROUPS)
                if h % (SSM_HEADS // SSM_GROUPS) == 0:
                    if h:
                        pe.wait_ge(st["o_m"], NB * h)
                    for j in range(NB):
                        last = mm(G[:, j, :], XBC[:, 8 + g, P * j:P * j + P], XBC[:, 12 + g, 0:T2], start=True, stop=True)
                    last.then_inc(st["o_cb"], 1)
                if h == 0:
                    broadcast(0)
                if h + 1 < SSM_HEADS:
                    broadcast(h + 1)
                if h % 2 == 0 and h >= 4:
                    pe.wait_ge(st["o_yd"], h // 2 - 1)
                for j in range(NB):
                    t = NB * h + j
                    pe.wait_ge(st["o_m"], t + 1)
                    mm(G[64 * (h % 2):64 * (h % 2) + 64, 6 + (h // 2) % 2, :], XST[:, j, 64 * h:64 * h + 64], OM[t % 2],
                       start=(j == 0), stop=(j == NB - 1)).then_inc(st["o_y"], 1)
            pe.wait_ge(st["o_yd"], SSM_HEADS // 2)
            product(pe, CHUNKS["z"], 8, XH, XL)
            product(pe, CHUNKS["o_out_g"], 4, YH, YL, kt=4, follow=True)
            norm_pe(pe, "ssm", T2)
            product(pe, CHUNKS["o_out_g"] + 4, 4, YH, YL, kt=4, follow=True)
            product(pe, CHUNKS["o_out_y"], 8, XH, XL, parts=SPLIT_AT["ssm"][0])
            post_pe(pe, "oddp")

        def odd_act(act):
            first_act(act, "odd", CHUNKS["ga"])
            act_idle(act, CHUNKS["ga"], 4, start=1)

            def step(i, c):
                split_high(act, CHUNKS["gb"] + 2, i, c)
                act.wait_ge(psum_free, 4 * i + CHUNKS["gb"] + c + 1 + 4)
                nc.scalar.activation(SB_[:, 4 * i + c, 0:T2], SB_[:, 4 * i + c, 0:T2],
                                     ACT.Sigmoid).then_inc(st["o_sl"], 1)
            fours(act, 4, step)
            act_idle(act, CHUNKS["dt"], 1)
            def step(i, c):
                split_high(act, CHUNKS["xbc"] + 2, i, c)
                if not (isinstance(i, int) and 4 * i + c == CONV_K // 2):
                    for e in range(2):
                        for f in range(2):
                            x, wj = tap(2 + f, 8 * i + 2 * c + 1 + e)
                            act.wait_ge(st["o_gu"], 16 * i + 4 * c + 2 * e + f + 1)
                            nc.scalar.activation(TAP[2 * e + f], x, ACT.Copy, scale=wj).then_inc(st["o_gt"], 1)
                act.wait_ge(st["o_cv"], 4 * i + c + 1)
                nc.scalar.activation(XBC[:, 4 * i + c, 0:T2], CV[:, c % 2, 0:T2], ACT.Silu).then_inc(st["o_si"], 1)
            act.wait_ge(st["o_gp"], 1)
            fours(act, 16, step, peel=True)
            act.wait_ge(psum_free, CHUNKS["dt"] + 1 + 4)
            nc.scalar.activation(OA, DTR, ACT.Abs)
            act.drain()
            nc.scalar.activation(OA, OA, ACT.Exp, scale=-1.0)
            nc.scalar.activation(AEXP, vec("a_log", 0, 32), ACT.Exp).then_inc(st["o_ab"], 1)
            act.wait_ge(st["o_xm"], 1)
            norm_act(act, "ln", CO, T2)
            act.wait_ge(st["o_g"], 1)
            for f in range(4):
                nc.scalar.activation(CO[f], CO[f], ACT.Silu, bias=vec("ln_b", f))
            act.drain()
            for f in range(4):
                nc.scalar.activation(YH[:, f, 0:T2], CO[f], ACT.Copy).then_inc(h_high, 1)
            act.wait_ge(h_low, split_end("o_g"))
            for f in range(DT):
                act.wait_ge(st["o_xt"], f + 1)
                nc.scalar.activation(XST[:, :, P * f:P * f + P],
                                     G[:, 5 + f % 2, :].rearrange("p (j m) -> p j m", m=P), ACT.Copy).then_inc(st["o_xc"], 1)

            def sums(h):
                act.wait_ge(st["o_bc"], h + 1)
                if h >= 2:
                    act.wait_ge(st["o_dg"], NB * (h - 1))
                nc.scalar.activation(FE[h % 2], G[:, 4:6, :], ACT.Copy).then_inc(st["o_fe"], 1)

            sums(0)
            for h in range(SSM_HEADS):
                for j in range(NB):
                    t, d0, d1 = NB * h + j, P * j, P * j + P
                    if j == 2 and h + 1 < SSM_HEADS:
                        sums(h + 1)
                    w, wd = OWT[t % 2], OWD[:, t % 2, :]
                    act.wait_ge(st["o_dg"], t + 1)
                    if t >= 2:
                        act.wait_ge(st["o_m"], t - 1)
                    nc.scalar.activation(w[:, d0:d1], wd[:, 0:P], ACT.Exp)
                    nc.scalar.activation(wd[:, P:2 * P], wd[:, P:2 * P], ACT.Exp, scale=-1.0)
                    if d1 < T2:
                        nc.scalar.activation(w[:, d1:T2], FE[h % 2][:, 0, d1:T2], ACT.Exp,
                                             bias=COLS[:, 384 + 32 * j + h:384 + 32 * j + h + 1])
                    if d0:
                        nc.scalar.activation(w[:, 0:d0], FE[h % 2][:, 1, 0:d0], ACT.Exp, scale=-1.0,
                                             bias=COLS[:, 128 + 32 * j + 16 + h:128 + 32 * j + 17 + h])
                    act.drain()
                    act.sem_inc(st["o_w"], 1)

            def step(i, c):
                split_high(act, CHUNKS["z"] + 2, i, c)
                act.wait_ge(psum_free, 4 * i + CHUNKS["z"] + c + 1 + 4)
                nc.scalar.activation(SZ[:, 4 * i + c, 0:T2], SZ[:, 4 * i + c, 0:T2], ACT.Silu).then_inc(st["o_sl"], 1)
            fours(act, 8, step)
            n = CHUNKS["o_out_g"]
            act_idle(act, n, 2)
            act.wait_ge(st["o_z"], 1)
            norm_act(act, "ssm", [XBC[:, f, 0:T2] for f in range(DT)], T2, lambda: act_idle(act, n + 2, 2))
            act_idle(act, n + 4, 2)
            split_act(act, "ssm", [XH[:, f, 0:T2] for f in range(DT)], T2)
            act_idle(act, n + 6, 2)
            tail_act(act, CHUNKS["o_out_y"], "oddp", [YO[:, f, 0:T2] for f in range(DT)], T2, False)
            post_act(act, "oddp")

        def odd_dve(dve):
            first_dve(dve, "odd", CHUNKS["ga"])
            take_scaled(dve, CHUNKS["ga"], 4, GA)
            take_scaled(dve, CHUNKS["gb"], 4, SB_)
            dve.wait_ge(tile_done, CHUNKS["dt"] + 1)
            tt(DTR, acc(CHUNKS["dt"], 0)[0:32, 0, :], RS[0:32, 0:T2], ALU.mult)
            dve.drain()
            ts(DTR, DTR, vec("dt_bias", 0, 32), None, ALU.add).then_inc(psum_free, 1)
            nc.vector.memset(GP[:, :, 0:CONV_K // 2], 0.0)
            nc.vector.memset(GP[:, :, CONV_K // 2 + T2:], 0.0)
            dve.wait_ge(st["o_sl"], 4)
            for f in range(4):
                tt(GP[:, f, CONV_K // 2:CONV_K // 2 + T2], GA[:, f, 0:T2], SB_[:, f, 0:T2], ALU.mult)
            dve.drain()
            for f in range(4):
                last = ts(CO[f], GP[:, f, 0:T2], vec("dw_w", f), vec("dw_b", f), ALU.mult, ALU.add)
            last.then_inc(st["o_gp"], 1)
            nc.vector.memset(STG[:, :, 0:2], 0.0)
            nc.vector.memset(STG[:, :, 2 + T2:3 + T2], 0.0).then_inc(st["o_si"], 1)

            def step(i, c):
                dve.drain()
                dve.wait_ge(tile_done, 4 * i + CHUNKS["xbc"] + c + 1)
                x, o = STG[:, c % 2, :], CV[:, c % 2, 0:T2]
                tt(x[:, 2:2 + T2], acc(CHUNKS["xbc"], c)[:, 0, :], RS[:, 0:T2], ALU.mult).then_inc(psum_free, 1)
                dve.drain()
                dve.wait_ge(st["o_si"], 4 * i + c + 1)

                def col(name, j):
                    return V[:, bass.ds(VEC[name] + 16 * j + c + 4 * i, 1)]
                last = ts(o, x[:, 0:T2], col("sconv_w", 0), col("sconv_b", 0), ALU.mult, ALU.add)
                for j in range(1, 4):
                    dve.drain()
                    last = stt(o, x[:, j:j + T2], col("sconv_w", j), o, ALU.mult, ALU.add)
                last.then_inc(st["o_cv"], 1)
                if isinstance(i, int) and 4 * i + c == CONV_K // 2:
                    return
                for e in range(2):
                    for f in range(2):
                        x, wj = tap(f, 8 * i + 2 * c + 1 + e)
                        stt(CO[f], x, wj, CO[f], ALU.mult, ALU.add)
                    if e == 0:
                        dve.drain()
            fours(dve, 16, step, peel=True)
            dve.drain()
            dve.sem_inc(st["o_gc"], 1)
            dve.wait_ge(st["o_ab"], 1)
            dve.drain()
            log1p(dve, SR, OA, OZ, OW)
            dve.wait_ge(st["o_mu"], 1)
            ts(MU, G[:, 6, :], 1.0 / 512, None, ALU.mult)
            dve.drain()
            for f in range(4):
                last = tt(CO[f], CO[f], MU, ALU.subtract)
            last.then_inc(st["o_xm"], 1)
            stt(DTR, DTR, 0.0, SR, ALU.max, ALU.add)
            ts(AEXP, AEXP, -1.0, None, ALU.mult)
            dve.drain()
            ts(OA, DTR, AEXP, None, ALU.mult)
            dve.drain()
            nc.vector.tensor_tensor_scan(SR, ones[0:32, 0:1].broadcast_to([32, T2]), OA, 0.0, ALU.mult, ALU.add)
            dve.drain()
            tt(ER, SR, OA, ALU.subtract).then_inc(st["o_dt"], 2)
            dve.drain()
            norm_dve_stats(dve, "ln", T2, 512)
            for f in range(4):
                last = stt(CO[f], CO[f], vec("ln_g", f), SCR[:, 4, 0:T2], ALU.mult, ALU.mult)
            last.then_inc(st["o_g"], 1)
            dve.wait_ge(st["o_tr"], 1)
            dve.drain()
            nc.vector.tensor_copy(COLS[:, 0:384], G[:, 4, 0:384])
            ts(COLS[:, 384:512], G[:, 4, 0:128], -1.0, None, ALU.mult).then_inc(st["o_col"], 1)
            for f in range(4):
                dve.wait_ge(h_high, SPLIT_AT["o_g"][0] + f + 1)
                tt(YL[:, f, 0:T2], CO[f], YH[:, f, 0:T2], ALU.subtract).then_inc(h_low, 1)
            dve.wait_ge(st["o_si"], 16 + 1)
            dve.drain()

            def diagonal(t):
                h, j = t // NB, t % NB
                d0, d1 = P * j, P * j + P
                wd = OWD[:, t % 2, :]
                if j == 0:
                    dve.wait_ge(st["o_fe"], h + 1)
                stt(wd[:, 0:P], FE[h % 2][:, 0, d0:d1], COLS[:, 384 + 32 * j + h:385 + 32 * j + h], mask_ge,
                    ALU.add, ALU.add)
                stt(wd[:, P:2 * P], FE[h % 2][:, 1, d0:d1], COLS[:, 128 + 32 * j + 16 + h:128 + 32 * j + 17 + h], mask_le,
                    ALU.subtract, ALU.subtract).then_inc(st["o_dg"], 1)

            total = NB * SSM_HEADS
            diagonal(0)
            for t in range(total):
                h, j = t // NB, t % NB
                d0, d1 = P * j, P * j + P
                w, wd, m = OWT[t % 2], OWD[:, t % 2, :], OM[t % 2]
                if t + 1 < total:
                    dve.drain()
                    diagonal(t + 1)
                if j == 0:
                    dve.wait_ge(st["o_cb"], h // (SSM_HEADS // SSM_GROUPS) + 1)
                dve.wait_ge(st["o_w"], t + 1)
                if t >= 2:
                    dve.wait_ge(st["o_y"], t - 1)
                dtf = COLS[:, 256 + 32 * j + h:257 + 32 * j + h]
                dtb = COLS[:, 256 + 32 * j + 16 + h:257 + 32 * j + 16 + h]
                dve.drain()
                stt(wd[:, P:2 * P], wd[:, P:2 * P], dtb, G[:, j, d0:d1], ALU.mult, ALU.mult)
                stt(m[:, d0:T2], w[:, d0:T2], dtf, G[:, j, d0:T2], ALU.mult, ALU.mult)
                if d0:
                    stt(m[:, 0:d0], w[:, 0:d0], dtb, G[:, j, 0:d0], ALU.mult, ALU.mult)
                dve.drain()
                tt(m[:, d0:d1], m[:, d0:d1], wd[:, P:2 * P], ALU.add).then_inc(st["o_m"], 1)
                if j == NB - 1 and h % 2:
                    f = h // 2
                    dve.wait_ge(st["o_y"], t + 1)
                    stt(XBC[:, f, 0:T2], XBC[:, f, 0:T2], vec("ssm_d", f), G[:, 6 + f % 2, :], ALU.mult,
                        ALU.add).then_inc(st["o_yd"], 1)
            take_scaled(dve, CHUNKS["z"], 8, SZ)
            dve.drain()
            dve.wait_ge(st["o_sl"], 4 + 8)
            for f in range(DT):
                last = tt(XBC[:, f, 0:T2], XBC[:, f, 0:T2], SZ[:, f, 0:T2], ALU.mult)
            last.then_inc(st["o_z"], 1)
            n = CHUNKS["o_out_g"]
            take_copy(dve, n, 4, YO)
            norm_dve_stats(dve, "ssm", T2, D)
            norm_split_dve(dve, [XBC[:, f, 0:T2] for f in range(DT)], gains("ssm_norm", 0),
                           [XH[:, f, 0:T2] for f in range(DT)], [XL[:, f, 0:T2] for f in range(DT)], T2,
                           SPLIT_AT["ssm"][0])
            take_copy(dve, n + 4, 4, YO[:, 4:8, :])
            dve.drain()
            tail_dve(dve, CHUNKS["o_out_y"], "oddp", T2,
                     lambda ps, f: tt(YO[:, f, 0:T2], ps[:, 0, :], YO[:, f, 0:T2], ALU.add), False)
            post_dve(dve, "oddp", gains("norm_w_2", 9), 1.0, YO)

        CONST_LOADS = 16 * 5

        @block.sync
        def _(sp):
            sp.dma_start(V[:, :], vecs).then_inc(vecs_loaded, 16)
            for f in range(DT):
                sp.dma_start(H[:, f, :], xT[P * f:P * f + P, :]).then_inc(x_loaded[f], 16)
                if f < 4:
                    load_chunk(sp, f, f)
            for dst, src in ((ident[:, :], mats[:, 0, :]), (LRU_W, lru_w), (MATS[:, :, :], mats[:, 1:9, :]),
                             (PW[:, :, :], pool_w), (ROPE[:, :, :], rope1)):
                sp.dma_start(dst, src).then_inc(const_loaded, 16)
            stream(sp)
            for f in range(DT):
                sp.wait_ge(updated, 8 * UPDATES.index("f3p") + f + 1)
                sp.dma_start(out[P * f:P * f + P, :], H[:, f, META:T1]).then_inc(out_done, 16)
            sp.wait_ge(out_done, 16 * DT)

        @block.gpsimd
        def _(pool):
            at = 0
            for name, stage in (("f0p", "eu"), ("evenp", "ffn1_up0"), ("f1p", "ffn2_up0"),
                                ("f2p", "ga"), ("oddp", "ffn3_up0")):
                if name == "evenp":
                    pool_stream(pool, at, CHUNKS["e_out"] + 2)
                    at = CHUNKS["e_out"] + 2
                    even_pool(pool)
                if name == "oddp":
                    n = CHUNKS["xbc"] + 2
                    pool_stream(pool, at, n)
                    pool.wait_ge(st["o_gp"], 1)
                    pool.sem_inc(st["o_gu"], 4)

                    def step(i, c):
                        pool.wait_ge(high_ready, 4 * i + n + c + 1)
                        nc.gpsimd.tensor_tensor(WL[:, (n + c) % 2, :], RAW[:, (n + c) % 4, :], WH[:, (n + c) % 2, :],
                                                ALU.subtract).then_inc(low_ready, 1)
                        if isinstance(i, int) and 4 * i + c == CONV_K // 2:
                            return
                        for e in range(2):
                            for f in range(2):
                                pool.wait_ge(st["o_gt"], 16 * i + 4 * c + 2 * e + f + 1)
                                nc.gpsimd.tensor_tensor(CO[2 + f], TAP[2 * e + f], CO[2 + f],
                                                        ALU.add).then_inc(st["o_gu"], 1)
                            pool.drain()
                    fours(pool, 16, step, peel=True)
                    pool.sem_inc(st["o_gc"], 1)
                    at = n + 16
                end = CHUNKS[stage] + 2
                pool_stream(pool, at, end)
                at = end
                post_pool(pool, name)
            pool_stream(pool, at, N_CHUNKS)
            post_pool(pool, "f3p")

        @block.scalar
        def _(act):
            act.wait_ge(vecs_loaded, 16)
            for f in range(DT):
                act.wait_ge(x_loaded[f], 16)
                high_part(act, "mix0", f, T1)
                if f > 2:
                    act.wait_ge(added, f - 2)
                square(act, "mix0", f, H[:, f, :], T1)
                if f < 2:
                    split_high(act, 0, 0, f)
            first_act(act, "mix0", 0)
            lru_act(act)
            mlstm_act(act)
            mlp_act(act, 0)
            diff_act(act)
            mlp_act(act, 1)
            final_act(act)
            ffn_act(act, 0)
            even_act(act)
            ffn_act(act, 1)
            ffn_act(act, 2)
            odd_act(act)
            ffn_act(act, 3)

        @block.vector
        def _(dve):
            nc.vector.memset(ones[:, :], 1.0).then_inc(ones_ready, 1)
            nc.vector.memset(SM[:, :], 0.0).then_inc(psum_free, 4)
            dve.wait_ge(vecs_loaded, 16)
            dve.drain()
            for f in range(DT):
                dve.wait_ge(x_loaded[f], 16)
                low_part(dve, "mix0", f, T1)
                if f:
                    add_square(dve, "mix0", f, T1)
            dve.wait_ge(const_loaded, CONST_LOADS)
            first_dve(dve, "mix0", 0)
            lru_dve(dve)
            mlstm_dve(dve)
            mlp_dve(dve, 0)
            diff_dve(dve)
            mlp_dve(dve, 1)
            final_dve(dve)
            ffn_dve(dve, 0)
            even_dve(dve)
            ffn_dve(dve, 1)
            ffn_dve(dve, 2)
            odd_dve(dve)
            ffn_dve(dve, 3)

        @block.tensor
        def _(pe):
            pe.wait_ge(ones_ready, 1)
            lru_pe(pe)
            mlstm_pe(pe)
            mlp_pe(pe, 0)
            diff_pe(pe)
            mlp_pe(pe, 1)
            post_pe(pe, "final")
            ffn_pe(pe, 0)
            even_pe(pe)
            ffn_pe(pe, 1)
            ffn_pe(pe, 2)
            odd_pe(pe)
            ffn_pe(pe, 3)


def _chunks(w, k0, kt, columns):
    m = len(columns) * P if isinstance(columns, list) else columns.stop - columns.start
    if isinstance(columns, list):
        cols = np.concatenate([np.arange(c, c + P) for c in columns])
        part = w[k0:k0 + kt * P][:, cols]
    else:
        part = w[k0:k0 + kt * P, columns]
    nt = (m + P - 1) // P
    full = np.zeros((DT * P, nt * P), w.dtype)
    full[0:kt * P, 0:m] = part
    return full.reshape(DT, P, nt, P).transpose(2, 1, 0, 3).reshape(nt, P, DT * P)


def pack_weights(x):
    out = np.zeros((N_CHUNKS, P, DT * P), np.float32)

    def put(name, *args):
        c = _chunks(*args)
        out[CHUNKS[name]:CHUNKS[name] + len(c)] = c

    w = x["ab_w_in"][0]
    out[CHUNKS["qk"]:CHUNKS["gi"]:2] = _chunks(w, 0, 8, slice(0, 1024))
    out[CHUNKS["qk"] + 1:CHUNKS["gi"]:2] = _chunks(w, 0, 8, slice(1024, 2048))
    for name, a, b in (("v", 2048, 3072), ("o", 3072, 4096), ("gi", 4096, 4100),
                       ("gf", 4100, 4104), ("xb", 4104, 5128), ("gate", 5128, 6152)):
        put(name, w, 0, 8, slice(a, b))
    put("out_mlstm", x["ab_w_out"][0], 0, 8, slice(0, D))
    put("out_lru", x["ab_w_out"][0], D, 8, slice(0, D))
    for l in range(2):
        at = 0
        for p, f in enumerate(FF1_PARTS):
            put(f"mlp{l}_up{p}", x["mlp_w1"][l], 0, 8, slice(at * P, (at + f) * P))
            put(f"mlp{l}_down{p}", x["mlp_w2"][l], at * P, f, slice(0, D))
            at += f
    w = x["c_w_in"][0]
    for i, name in enumerate(("cq", "ck", "cv")):
        put(name, w, 0, 8, slice(D * i, D * i + D))
    put("c_out", x["c_w_out"][0], 0, 8, slice(0, D))
    for i in range(4):
        g, u, d = (x[f"ffn_w_{s}_2"][i // 2, i % 2] for s in ("gate", "up", "down"))
        at = 0
        for p, f in enumerate(FF2_PARTS):
            n = CHUNKS[f"ffn{i}_up{p}"]
            out[n:n + 2 * f:2] = _chunks(g, 0, 8, slice(at * P, (at + f) * P))
            out[n + 1:n + 2 * f:2] = _chunks(u, 0, 8, slice(at * P, (at + f) * P))
            put(f"ffn{i}_down{p}", d, at * P, f, slice(0, D))
            at += f
    w = x["ev_w_in_2"][0]
    for name, a, b in (("eu", 0, 256), ("eq", 256, 1024), ("ek", 1024, 1280), ("ev", 1280, 1536)):
        put(name, w, 0, 8, slice(a, b))
    put("e_out", x["ev_w_out_2"][0], 0, 8, slice(0, D))
    w = x["od_w_in_2"][0]
    for name, a, b in (("ga", 0, 512), ("gb", 512, 1024), ("z", 1024, 2048), ("xbc", 2048, 4096), ("dt", 4096, 4128)):
        put(name, w, 0, 8, slice(a, b))
    put("o_out_g", x["od_w_out_2"][0], 0, 4, slice(0, D))
    put("o_out_y", x["od_w_out_2"][0], 512, 8, slice(0, D))
    return out


def pack_vectors(x):
    v = np.zeros((P, VEC["end"]), np.float32)

    def put(name, a):
        a = np.asarray(a).reshape(-1, P).T
        v[:, VEC[name]:VEC[name] + a.shape[1]] = a

    for name, key in (("norm_mix", "norm_mix"), ("norm_mlp", "norm_mlp"), ("norm_final", "norm_final"),
                      ("mlstm_norm", "mlstm_norm"), ("conv_w", "lru_conv_w"), ("conv_b", "lru_conv_b"),
                      ("b_r", "lru_b_r"), ("b_i", "lru_b_i"), ("lam", "lru_lambda"), ("subln", "c_subln"),
                      ("norm_w_2", "norm_w_2"), ("pool_scale", "ev_pool_scale_2"), ("dw_w", "cv_dw_w_2"),
                      ("dw_b", "cv_dw_b_2"), ("ln_g", "cv_ln_g_2"), ("ln_b", "cv_ln_b_2"),
                      ("sconv_w", "ssm_conv_w_2"), ("sconv_b", "ssm_conv_b_2"), ("ssm_norm", "ssm_norm_w_2")):
        put(name, x[key])
    put("ssm_d", np.repeat(x["ssm_D_2"][0], HD))
    v[0:A_HEADS, VEC["i_bias"]] = x["ab_if_bias"][0, 0:A_HEADS]
    v[0:A_HEADS, VEC["f_bias"]] = x["ab_if_bias"][0, A_HEADS:]
    v[0:32, VEC["a_log"]] = x["ssm_A_log_2"][0].reshape(-1)
    v[0:32, VEC["dt_bias"]] = x["ssm_dt_bias_2"][0].reshape(-1)
    v[:, VEC["sink"]:VEC["sink"] + Q_HEADS] = x["ev_sink_2"][0]
    v[:, VEC["c_lambda"]:VEC["c_lambda"] + 256] = x["c_lambda"][0].reshape(-1)
    return v


def constants():
    m = np.zeros((9, P, P), np.float32)
    r, c = np.arange(P)[:, None], np.arange(P)[None, :]
    m[0] = np.eye(P)
    m[1] = np.where(c >= r, 0, -BIG)
    m[2] = np.where(c <= r, 0, -BIG)
    for base in (0, 64):
        for i in range(ROT1 // 2):
            m[3, base + ROT1 // 2 + i, base + i] = -1
            m[3, base + i, base + ROT1 // 2 + i] = 1
    for base in (0, 64):
        for i in range(HD // 2):
            m[4, base + 32 + i, base + i] = -1
            m[4, base + i, base + 32 + i] = 1
    for half in range(2):
        for base in (0, 64):
            for i in range(HD):
                m[5 + half, 64 * half + i, base + i] = 1
    for half in range(2):
        m[7 + half] = m[5 + half] @ m[4]

    def tables(t, rot, theta, inv=None):
        half = rot // 2
        f32 = np.float32
        if inv is None:
            inv = np.power(f32(theta), -np.arange(0, rot, 2, dtype=f32) / f32(rot))
        else:
            inv = (f32(1) / (f32(theta) ** (np.arange(0, rot, 2, dtype=f32) / f32(rot)))).astype(f32)
        ang = (inv.astype(f32)[:, None] * np.arange(t, dtype=f32)[None, :]).astype(f32).astype(np.float64)
        out = np.zeros((P, 2, t), np.float32)
        out[:, 0] = 1
        for base in (0, 64):
            for part in range(2):
                rows = slice(base + part * half, base + (part + 1) * half)
                out[rows, 0] = np.cos(ang)
                out[rows, 1] = np.sin(ang)
        return out

    inv = np.zeros((P, 2, T2), np.float32)
    t = np.arange(T2)
    for g, w in enumerate(POOL_W):
        count = np.clip(t + w - w // 2, 0, T2) - np.clip(t - w // 2, 0, T2)
        inv[64 * (g % 2):64 * (g % 2) + 64, g // 2] = 1.0 / count
    return m.transpose(1, 0, 2).copy(), tables(T1, ROT1, THETA1), tables(T2, HD, THETA2, True), inv


def arrays(inputs):
    x = {k: np.asarray(a) for k, a in inputs.items()}
    xT = np.ascontiguousarray(np.concatenate([x["meta_tokens"], x["x"][0]]).T)
    mats, rope1, rope2, inv = constants()
    lru_w = np.concatenate([x["lru_w_r"][0], x["lru_w_i"][0]]).transpose(1, 0, 2).copy()
    pw = np.zeros((P, 2, P), np.float32)
    for g in range(4):
        s = slice(64 * (g % 2), 64 * (g % 2) + 64)
        pw[s, g // 2, s] = x["ev_pool_w_2"][0, g]
    return {"xT": xT, "weights": pack_weights(x), "vecs": pack_vectors(x), "mats": mats, "lru_w": lru_w,
            "pool_w": pw, "rope1": rope1, "rope2": rope2, "pool_inv": inv}


def kernel(**inputs):
    import concourse.bacc as bacc
    from concourse.bass_utils import run_bass_kernel_spmd

    nc = bacc.Bacc("TRN2", target_bir_lowering=False, num_devices=1)
    data = {f"in_{k}": a for k, a in arrays(inputs).items()}
    args = [nc.dram_tensor(k, a.shape, mybir.dt.from_np(a.dtype), kind="ExternalInput").ap() for k, a in data.items()]
    out = nc.dram_tensor("out_dram", (D, T2), mybir.dt.float32, kind="ExternalOutput").ap()
    build(nc, *args, out)
    r = run_bass_kernel_spmd(nc, [data], core_ids=[0])
    return np.ascontiguousarray(r.results[0]["out_dram"].T)[None]
```
